# Optimizing a Trainium2 kernel written in Bass

```python
import math
import jax, jax.numpy as jnp
from jax import lax
import numpy as np

D_MODEL = 1024
BATCH = 1
SEQ = 256
DEPTH = 2

A_HEAD_DIM = 64
A_HEADS = D_MODEL // A_HEAD_DIM
DILATED_PAIRS = ((128, 1), (512, 4), (2048, 16))
DBLK = 128
MLA_HEADS = D_MODEL // 64
Q_RANK = 3 * D_MODEL // 8
KV_RANK = D_MODEL // 4
NOPE_DIM = 64
ROPE_DIM = 32
QK_DIM = NOPE_DIM + ROPE_DIM
V_DIM = 64
QBLK = 128
ROPE_THETA = 10000.0
N_EXPERTS = 64
N_GROUPS = 8
TOPK_GROUPS = 4
TOP_K = 6
EXPERT_DIM = D_MODEL // 4
SHARED_DIM = D_MODEL // 4
ROUTED_SCALE = 2.5
EXPERT_BLOCK = 256
NORM_EPS = 1e-6

kernel_name = 'yoco_dilated_mla_moe_adaln_block'

def _layer_split():
    n_a = (DEPTH + 1) // 2
    return n_a, DEPTH - n_a

def rms_norm(x, g):
    x32 = x.astype(jnp.float32)
    y = x32 * lax.rsqrt(jnp.mean(x32 * x32, axis=-1, keepdims=True) + NORM_EPS)
    return (y * g.astype(jnp.float32)).astype(x.dtype)

def apply_rope(t, pos):
    half = t.shape[-1] // 2
    inv = jnp.power(ROPE_THETA, -jnp.arange(half, dtype=jnp.float32) / half)
    ang = pos.astype(jnp.float32)[..., None] * inv
    cos = jnp.cos(ang)[:, :, None, :]
    sin = jnp.sin(ang)[:, :, None, :]
    t1 = t[..., :half].astype(jnp.float32)
    t2 = t[..., half:].astype(jnp.float32)
    return jnp.concatenate([t1 * cos - t2 * sin, t1 * sin + t2 * cos], axis=-1).astype(t.dtype)

def alibi_slopes(n_heads):
    return jnp.exp2(-8.0 * jnp.arange(1, n_heads + 1, dtype=jnp.float32) / n_heads)

def dilated_branch(q, k, v, pos, slopes, dil, span):
    B, S, H, Dh = q.shape
    L = S // dil
    nb = -(-L // DBLK)
    Lp = nb * DBLK

    def residues(t):
        return jnp.swapaxes(t.reshape((B, L, dil) + t.shape[2:]), 1, 2)

    def pad_len(t, front, back):
        widths = [(0, 0)] * t.ndim
        widths[2] = (front, back)
        return jnp.pad(t, widths)

    def key_windows(t):
        t = pad_len(t, DBLK, Lp - L).reshape((B, dil, nb + 1, DBLK) + t.shape[3:])
        return jnp.concatenate([t[:, :, :-1], t[:, :, 1:]], axis=3)

    qb = pad_len(residues(q), 0, Lp - L).reshape(B, dil, nb, DBLK, H, Dh)
    kw = key_windows(residues(k))
    vw = key_windows(residues(v))
    pr = residues(pos)
    pq = pad_len(pr, 0, Lp - L).reshape(B, dil, nb, DBLK)
    pk = key_windows(pr)

    s = jnp.einsum('brnqhd,brnkhd->brnhqk', qb, kw,
                   preferred_element_type=jnp.float32) * (Dh ** -0.5)
    rel = (pq[..., :, None] - pk[..., None, :]).astype(jnp.float32)
    s = s - slopes[:, None, None] * rel[:, :, :, None]
    a_idx = jnp.arange(DBLK)[:, None]
    c_idx = jnp.arange(2 * DBLK)[None, :]
    dist = a_idx - c_idx + DBLK
    key_idx = jnp.arange(nb)[:, None, None] * DBLK + c_idx[None] - DBLK
    valid = (dist >= 0) & (dist <= span) & (key_idx >= 0)
    s = jnp.where(valid[:, None], s, -jnp.inf)
    m = jnp.max(s, axis=-1, keepdims=True)
    p = jnp.exp(s - m)
    l = jnp.sum(p, axis=-1)
    o = jnp.einsum('brnhqk,brnkhd->brnqhd', p.astype(v.dtype), vw,
                   preferred_element_type=jnp.float32)
    o = o / jnp.moveaxis(l, 3, 4)[..., None]
    lse = jnp.moveaxis(m[..., 0] + jnp.log(l), 3, 4)

    def back(t):
        rest = t.shape[4:]
        t = t.reshape((B, dil, Lp) + rest)[:, :, :L]
        return jnp.swapaxes(t, 1, 2).reshape((B, S) + rest)

    return back(o), back(lse)

def dilated_attention(h, pos, w_qkv, q_norm, k_norm, w_o):
    B, S, _ = h.shape
    qkv = (h @ w_qkv).reshape(B, S, 3, A_HEADS, A_HEAD_DIM)
    q = rms_norm(qkv[:, :, 0], q_norm)
    k = rms_norm(qkv[:, :, 1], k_norm)
    v = qkv[:, :, 2]
    slopes = alibi_slopes(A_HEADS)
    outs, lses = [], []
    for win, dil in DILATED_PAIRS:
        o_b, lse_b = dilated_branch(q, k, v, pos, slopes, dil, win // dil)
        outs.append(o_b)
        lses.append(lse_b)
    wts = jax.nn.softmax(jnp.stack(lses), axis=0)
    o = jnp.einsum('gbsh,gbshd->bshd', wts, jnp.stack(outs))
    return o.reshape(B, S, A_HEADS * A_HEAD_DIM).astype(h.dtype) @ w_o

def shared_kv(x, c, pos, kv_ada_w, kv_ada_b, kv_norm_g, kv_w_down, kv_latent_norm,
              kv_w_uk, kv_w_uv, kv_k_norm):
    B, S, _ = x.shape
    mod = jax.nn.silu(c) @ kv_ada_w + kv_ada_b
    shift, scale = jnp.split(mod, 2, axis=-1)
    h = rms_norm(x, kv_norm_g) * (1.0 + scale[:, None]) + shift[:, None]
    down = h @ kv_w_down
    c_kv = rms_norm(down[..., :KV_RANK], kv_latent_norm)
    k_pe = down[..., KV_RANK:]
    k_nope = (c_kv @ kv_w_uk).reshape(B, S, MLA_HEADS, NOPE_DIM)
    v = (c_kv @ kv_w_uv).reshape(B, S, MLA_HEADS, V_DIM)
    k = jnp.concatenate(
        [k_nope, jnp.broadcast_to(k_pe[:, :, None, :], (B, S, MLA_HEADS, ROPE_DIM))], axis=-1)
    k = rms_norm(k, kv_k_norm)
    k = jnp.concatenate([k[..., :NOPE_DIM], apply_rope(k[..., NOPE_DIM:], pos)], axis=-1)
    return k, v

def mla_attention(h, k, v, pos, w_dq, q_latent_norm, w_uq, q_norm, w_o):
    B, S, _ = h.shape
    c_q = rms_norm(h @ w_dq, q_latent_norm)
    q = (c_q @ w_uq).reshape(B, S, MLA_HEADS, QK_DIM)
    q = rms_norm(q, q_norm)
    q = jnp.concatenate([q[..., :NOPE_DIM], apply_rope(q[..., NOPE_DIM:], pos)], axis=-1)
    nq = S // QBLK
    qb = jnp.moveaxis(q.reshape(B, nq, QBLK, MLA_HEADS, QK_DIM), 1, 0)
    key_pos = jnp.arange(S)

    def block(args):
        qi, start = args
        s = jnp.einsum('bqhd,bkhd->bhqk', qi, k,
                       preferred_element_type=jnp.float32) * (QK_DIM ** -0.5)
        mask = (start + jnp.arange(QBLK))[:, None] >= key_pos[None, :]
        p = jax.nn.softmax(jnp.where(mask, s, -jnp.inf), axis=-1)
        return jnp.einsum('bhqk,bkhd->bqhd', p.astype(v.dtype), v)

    o = lax.map(block, (qb, jnp.arange(nq) * QBLK))
    o = jnp.moveaxis(o, 0, 1).reshape(B, S, MLA_HEADS * V_DIM)
    return o @ w_o

def swiglu(x, w_gu, w_dn):
    g, u = jnp.split(x @ w_gu, 2, axis=-1)
    return (jax.nn.silu(g) * u) @ w_dn

def routed_experts(xf, idx, wts, w_gu, w_dn):
    N, D = xf.shape
    E = w_gu.shape[0]
    K = idx.shape[1]
    A = N * K
    e = idx.reshape(-1)
    tok = jnp.repeat(jnp.arange(N, dtype=jnp.int32), K)
    w = wts.reshape(-1)
    order = jnp.argsort(e, stable=True)
    e_s, tok_s, w_s = e[order], tok[order], w[order]
    counts = jnp.bincount(e, length=E)
    padded = ((counts + EXPERT_BLOCK - 1) // EXPERT_BLOCK) * EXPERT_BLOCK
    pad_end = jnp.cumsum(padded)
    pad_start = pad_end - padded
    raw_start = jnp.cumsum(counts) - counts
    dest = pad_start[e_s] + jnp.arange(A) - raw_start[e_s]
    nblk = (A + E * (EXPERT_BLOCK - 1) + EXPERT_BLOCK - 1) // EXPERT_BLOCK
    P = nblk * EXPERT_BLOCK
    buf_tok = jnp.full((P,), N, dtype=jnp.int32).at[dest].set(tok_s)
    buf_w = jnp.zeros((P,), jnp.float32).at[dest].set(w_s.astype(jnp.float32))
    blk_e = jnp.minimum(
        jnp.searchsorted(pad_end, jnp.arange(nblk) * EXPERT_BLOCK, side='right'), E - 1)
    x_pad = jnp.concatenate([xf, jnp.zeros((1, D), xf.dtype)], axis=0)

    def step(acc, inp):
        t, wb, ei = inp
        y = swiglu(x_pad[t], w_gu[ei], w_dn[ei])
        return acc.at[t].add(y.astype(jnp.float32) * wb[:, None]), None

    acc, _ = lax.scan(step, jnp.zeros((N + 1, D), jnp.float32),
                      (buf_tok.reshape(nblk, EXPERT_BLOCK), buf_w.reshape(nblk, EXPERT_BLOCK), blk_e))
    return acc[:N].astype(xf.dtype)

def moe_ffn(h, w_router, router_bias, w_gate_up, w_down, shared_gate_up, shared_down):
    B, S, D = h.shape
    xf = h.reshape(-1, D)
    N = xf.shape[0]
    scores = jax.nn.sigmoid(jnp.einsum('nd,de->ne', xf, w_router,
                                       preferred_element_type=jnp.float32))
    sel = scores + router_bias.astype(jnp.float32)
    grp = sel.reshape(N, N_GROUPS, N_EXPERTS // N_GROUPS)
    gscore = jnp.sum(lax.top_k(grp, 2)[0], axis=-1)
    _, gidx = lax.top_k(gscore, TOPK_GROUPS)
    gmask = jnp.sum(jax.nn.one_hot(gidx, N_GROUPS), axis=1) > 0
    emask = jnp.repeat(gmask, N_EXPERTS // N_GROUPS, axis=1)
    _, idx = lax.top_k(jnp.where(emask, sel, -jnp.inf), TOP_K)
    w = jnp.take_along_axis(scores, idx, axis=1)
    w = w / jnp.sum(w, axis=-1, keepdims=True) * ROUTED_SCALE
    routed = routed_experts(xf, idx, w, w_gate_up, w_down)
    shared = swiglu(xf, shared_gate_up, shared_down)
    return (routed + shared).reshape(B, S, D)

def setup_inputs(seed: int = 0) -> dict:
    key = jax.random.key(seed)
    ks = jax.random.split(key, 40)
    ctr = [0]

    def nxt():
        ctr[0] += 1
        return ks[ctr[0] - 1]

    f32 = jnp.float32
    D = D_MODEL
    n_a, n_b = _layer_split()

    def w(shape, fan_in, scale=1.0):
        return jax.random.normal(nxt(), shape, f32) * (scale * fan_in ** -0.5)

    def gain(shape):
        return 1.0 + 0.05 * jax.random.normal(nxt(), shape, f32)

    def small(shape, s):
        return s * jax.random.normal(nxt(), shape, f32)

    x = jax.random.normal(nxt(), (BATCH, SEQ, D), f32)
    c = jax.random.normal(nxt(), (BATCH, D), f32)
    pos = (jnp.arange(SEQ, dtype=jnp.int32)[None, :]
           + jax.random.randint(nxt(), (BATCH, 1), 0, 64, dtype=jnp.int32))
    return {
        'x': x, 'c': c, 'pos': pos,
        'ada_w': w((DEPTH, D, 6 * D), D, 0.5),
        'ada_b': small((DEPTH, 6 * D), 0.05),
        'norm1_g': gain((DEPTH, D)),
        'norm2_g': gain((DEPTH, D)),
        'a_w_qkv': w((n_a, D, 3 * A_HEADS * A_HEAD_DIM), D),
        'a_q_norm': gain((n_a, A_HEAD_DIM)),
        'a_k_norm': gain((n_a, A_HEAD_DIM)),
        'a_w_o': w((n_a, A_HEADS * A_HEAD_DIM, D), A_HEADS * A_HEAD_DIM),
        'kv_ada_w': w((D, 2 * D), D, 0.5),
        'kv_ada_b': small((2 * D,), 0.05),
        'kv_norm_g': gain((D,)),
        'kv_w_down': w((D, KV_RANK + ROPE_DIM), D),
        'kv_latent_norm': gain((KV_RANK,)),
        'kv_w_uk': w((KV_RANK, MLA_HEADS * NOPE_DIM), KV_RANK),
        'kv_w_uv': w((KV_RANK, MLA_HEADS * V_DIM), KV_RANK),
        'kv_k_norm': gain((QK_DIM,)),
        'b_w_dq': w((n_b, D, Q_RANK), D),
        'b_q_latent_norm': gain((n_b, Q_RANK)),
        'b_w_uq': w((n_b, Q_RANK, MLA_HEADS * QK_DIM), Q_RANK),
        'b_q_norm': gain((n_b, QK_DIM)),
        'b_w_o': w((n_b, MLA_HEADS * V_DIM, D), MLA_HEADS * V_DIM),
        'moe_w_router': w((DEPTH, D, N_EXPERTS), D),
        'moe_router_bias': small((DEPTH, N_EXPERTS), 0.01),
        'moe_w_gate_up': w((DEPTH, N_EXPERTS, D, 2 * EXPERT_DIM), D),
        'moe_w_down': w((DEPTH, N_EXPERTS, EXPERT_DIM, D), EXPERT_DIM),
        'moe_shared_gate_up': w((DEPTH, D, 2 * SHARED_DIM), D),
        'moe_shared_down': w((DEPTH, SHARED_DIM, D), SHARED_DIM),
    }

def reference(x, c, pos, ada_w, ada_b, norm1_g, norm2_g, a_w_qkv, a_q_norm, a_k_norm, a_w_o,
              kv_ada_w, kv_ada_b, kv_norm_g, kv_w_down, kv_latent_norm, kv_w_uk, kv_w_uv,
              kv_k_norm, b_w_dq, b_q_latent_norm, b_w_uq, b_q_norm, b_w_o, moe_w_router,
              moe_router_bias, moe_w_gate_up, moe_w_down, moe_shared_gate_up, moe_shared_down):
    n_a, _ = _layer_split()
    cond = jax.nn.silu(c)
    k_sh = None
    v_sh = None
    for l in range(DEPTH):
        mod = cond @ ada_w[l] + ada_b[l]
        sh1, sc1, g1, sh2, sc2, g2 = [m[:, None, :] for m in jnp.split(mod, 6, axis=-1)]
        if l == n_a:
            k_sh, v_sh = shared_kv(x, c, pos, kv_ada_w, kv_ada_b, kv_norm_g, kv_w_down,
                                   kv_latent_norm, kv_w_uk, kv_w_uv, kv_k_norm)
        h = rms_norm(x, norm1_g[l]) * (1.0 + sc1) + sh1
        if l < n_a:
            y = dilated_attention(h, pos, a_w_qkv[l], a_q_norm[l], a_k_norm[l], a_w_o[l])
        else:
            j = l - n_a
            y = mla_attention(h, k_sh, v_sh, pos, b_w_dq[j], b_q_latent_norm[j], b_w_uq[j],
                              b_q_norm[j], b_w_o[j])
        x = x + g1 * y
        h = rms_norm(x, norm2_g[l]) * (1.0 + sc2) + sh2
        x = x + g2 * moe_ffn(h, moe_w_router[l], moe_router_bias[l], moe_w_gate_up[l],
                             moe_w_down[l], moe_shared_gate_up[l], moe_shared_down[l])
    return x


_drawn_inputs = setup_inputs


def setup_inputs(seed=0):
    import zlib

    import numpy as np

    out = dict(_drawn_inputs(seed))
    spreads = {}
    factors = {'kv_norm_g': 4.284,
     'kv_latent_norm': 3.358,
     'kv_k_norm': 5.584,
     'b_q_latent_norm': 4.97,
     'b_q_norm': 7.57}
    for name, (base, spread) in spreads.items():
        noise = np.random.default_rng([zlib.crc32(name.encode()), seed]).standard_normal(out[name].shape)
        drawn = base * np.exp(spread * noise) if base else spread * noise
        out[name] = __import__('jax').numpy.asarray(drawn.astype(out[name].dtype))
    for name, factor in factors.items():
        out[name] = (out[name] * factor).astype(out[name].dtype)
    return out
```

```python
from contextlib import ExitStack

import numpy as np

import concourse.bass as bass
from concourse import mybir

P = 128
F32 = mybir.dt.float32
I32 = mybir.dt.int32
ALU = mybir.AluOpType
ACT = mybir.ActivationFunctionType
AX_X = mybir.AxisListType.X

N = 256
NT = N // P
D = 1024
KT = D // P
H = 16
HD = 64
QR = 384
KVR = 256
ROPE = 32
QK = HD + ROPE
E = 64
G = 8
TOPG = 4
TOPK = 6
FE = 256
ROUTED_SCALE = 2.5
THETA = 10000.0
EPS = 1e-6
C = 64
OVER = 24
ITEMS = E + OVER
MASKED = -1e30
PI = float(np.float32(3.1415925))

RING = 5
CH = 2048
SC = 3 * P

CO, _at = {}, 0
for _name, _n in (("ident", P), ("tri", P), ("ones", P), ("logcount", SC), ("causal", SC), ("slot1", C),
                  ("iota", OVER), ("inv", ROPE // 2), ("row", 1), ("eps", 1), ("halfpi", 1)):
    CO[_name] = (_at, _at + _n)
    _at += _n
NCONST = _at

VR, _at = {}, 0
for _name, _n in (("ada_b", 96), ("norm1_g", 16), ("norm2_g", 16), ("kv_ada_b", 16), ("kv_norm_g", 8),
                  ("c", 8), ("b_q_latent_norm", 3), ("kv_latent_norm", 2), ("a_q_norm", 1),
                  ("a_k_norm", 1), ("b_q_norm", 1), ("kv_k_norm", 1)):
    VR[_name] = (_at, _at + _n)
    _at += _n
NROWS = _at
NROWS_B = NROWS - P


def constants():
    c = np.zeros((P, NCONST), np.float32)
    q = np.arange(P)[:, None]
    k = np.arange(P)[None, :]

    def put(name, value):
        c[:, CO[name][0]:CO[name][1]] = value

    put("ident", q == k)
    put("tri", q < k)
    put("ones", 1.0)
    dist = np.concatenate([q - k, q + P - k, q - k], axis=1)
    seen = (dist <= 128).astype(np.int64) + (dist % 4 == 0) + (dist % 16 == 0)
    put("logcount", np.where((dist >= 0) & (seen > 0), np.log(np.maximum(seen, 1)), MASKED))
    put("causal", np.where(dist >= 0, 0.0, MASKED))
    put("slot1", np.arange(1, C + 1)[None, :])
    put("iota", np.arange(OVER)[None, :])
    put("inv", np.power(np.float32(THETA), -np.arange(ROPE // 2, dtype=np.float32) / (ROPE // 2))[None, :])
    put("row", q)
    put("eps", EPS)
    put("halfpi", np.pi / 2)
    return c


def build(nc: bass.Bass, t: dict, out: bass.AP):
    with ExitStack() as ctx:
        sems = {}

        def sem(name):
            if name not in sems:
                sems[name] = ctx.enter_context(nc.semaphore(name))
            return sems[name]

        def sb(name, shape, dt=F32, scope=ctx):
            return scope.enter_context(nc.sbuf_tensor(name, shape, dt))

        bank = [ctx.enter_context(nc.psum_tensor(f"bank{i}", [P, 512], F32)) for i in range(8)]

        x = sb("x", [P, NT, D])
        xn = sb("xn", [P, NT, D])
        hT = sb("hT", [P, KT, N])
        gate = sb("gate", [P, 2, D])
        ring = sb("ring", [P, RING, CH])
        w_gu = [sb(f"w_gu{u}", [P, KT, 2 * FE]) for u in range(2)]
        w_dn = [sb(f"w_dn{u}", [P, FE // P, D]) for u in range(2)]
        w_router = sb("w_router", [P, 2, KT, E])
        cst = sb("cst", [P, NCONST])
        vcol = sb("vcol", [P, NROWS])
        bias_row = sb("bias_row", [P, 2, E])
        ropeg = sb("ropeg", [P, 2, ROPE])
        pos_q = sb("pos_q", [P, NT], I32)
        pos_qf = sb("pos_qf", [P, NT])
        csilu = sb("csilu", [P, KT])
        mod = sb("mod", [P, 2 * 48 + 16])
        amp = sb("amp", [P, 5, KT])
        qk_gain = sb("qk_gain", [P, 2])
        small = sb("small", [P, 64])
        eps_c = cst[:, CO["eps"][0]:CO["eps"][1]]

        def const(name, rows=P):
            return cst[0:rows, CO[name][0]:CO[name][1]]

        def col(name, i=0, n=1, rows=P):
            return vcol[0:rows, VR[name][0] + i:VR[name][0] + i + n]

        with ExitStack() as early:
            rows_a = sb("rows_a", [P, P], scope=early)
            rows_b = sb("rows_b", [P, P], scope=early)
            diag = sb("diag", [P, KT, P], scope=early)
            pos_k = sb("pos_k", [P, N], I32, scope=early)
            pos_kf = sb("pos_kf", [P, N], scope=early)
        with ExitStack() as att:
            qT = sb("qT", [P, H, N], scope=att)
            kT = sb("kT", [P, H, N], scope=att)
            v_sb = sb("v_sb", [P, NT, D], scope=att)
            s_sb = sb("s_sb", [P, 2, SC], scope=att)
            p_sb = sb("p_sb", [P, 2, SC], scope=att)
            pT_sb = sb("pT_sb", [P, 2, SC], scope=att)
            negrel = sb("negrel", [P, SC], scope=att)
            smax = sb("smax", [P, H, NT], scope=att)
            nmax = sb("nmax", [P, H, NT], scope=att)
            lsum = sb("lsum", [P, H, NT], scope=att)
            rsum = sb("rsum", [P, H, NT], scope=att)
            with ExitStack() as first:
                qkn = sb("qkn", [P, 3, NT * N], scope=first)
                sq = sb("sq", [P, 2, NT * N], scope=first)
                ssq = sb("ssq", [P, 8, 8], scope=first)
                srt = sb("srt", [P, 8, 8], scope=first)
                srs = sb("srs", [P, 8, 8], scope=first)
            with ExitStack() as second:
                q_sb = sb("q_sb", [P, NT, H, QK], scope=second)
                k_sb = sb("k_sb", [P, NT, H, QK], scope=second)
                kpe = sb("kpe", [P, NT, ROPE], scope=second)
                flat_kT = kT[:, :, :].rearrange("p h n -> p (h n)")
                at = [0]

                def in_kT(*shape):
                    n = int(np.prod(shape))
                    v = flat_kT[:, at[0]:at[0] + n]
                    at[0] += n
                    names = "abcd"[:len(shape)]
                    return v.rearrange(f"p ({' '.join(names)}) -> p {' '.join(names)}", **dict(zip(names, shape)))

                lat_kv = in_kT(NT, KVR)
                lat_q = in_kT(NT, QR)
                lat_kvT = in_kT(KVR // P, N)
                lat_qT = in_kT(QR // P, N)
                rt = in_kT(4, 256)
                ang = in_kT(6, NT, ROPE // 2)
                hs_rs = in_kT(6, NT, H)
            hkvT = qT[:, 0:8, :]
        with ExitStack() as moe:
            h_tok = sb("h_tok", [P, NT, D], scope=moe)
            y_sb = sb("y_sb", [P, D], scope=moe)
            st = sb("st", [P, N], scope=moe)
            sel = sb("sel", [P, NT, 2, C], scope=moe)
            selw = sb("selw", [P, NT, 2, C], scope=moe)
            xg = sb("xg", [P, KT, 2 * C], scope=moe)
            sg = sb("sg", [P, FE], scope=moe)
            hh = sb("hh", [P, FE], scope=moe)
            hhT = sb("hhT", [P, FE // P, 2 * C], scope=moe)
            sh_g = sb("sh_g", [P, FE // P, N], scope=moe)
            sh_h = sb("sh_h", [P, FE // P, N], scope=moe)
            slot_of = sb("slot_of", [P, NT, ITEMS + 2], scope=moe)
            w_of = sb("w_of", [P, NT, ITEMS + 2], scope=moe)
            score = sb("score", [P, NT, E], scope=moe)
            choice = sb("choice", [P, NT, E + 2], scope=moe)
            left = sb("left", [P, NT, E + 2], scope=moe)
            chosen = sb("chosen", [P, NT, E], scope=moe)
            gsort = sb("gsort", [P, NT, G, 8], scope=moe)
            gsc = sb("gsc", [P, NT, G + TOPG], scope=moe)
            gleft = sb("gleft", [P, NT, G + TOPG], scope=moe)
            gtop = sb("gtop", [P, NT, 8], scope=moe)
            gmask = sb("gmask", [P, NT, G], scope=moe)
            etop = sb("etop", [P, NT, 8], scope=moe)
            rden = sb("rden", [P, NT], scope=moe)
            rtT = sb("rtT", [E, 2, N], scope=moe)
            count = sb("count", [E, 4], scope=moe)
            flag = sb("flag", [E, 4], scope=moe)
            place = sb("place", [E, 4], scope=moe)
            onehot = sb("onehot", [E, 5, OVER], scope=moe)
            tab_f = sb("tab_f", [1, OVER + 1], scope=moe)
            tab_i = sb("tab_i", [1, OVER + 2], I32, scope=moe)
        junk = sb("junk", [P, D])

        def q_flat(ti):
            return q_sb[:, ti, :, :].rearrange("p h d -> p (h d)")

        def rows_loads():
            loads = []
            for name in ("ada_b", "norm1_g", "norm2_g", "kv_ada_b", "kv_norm_g", "c", "b_q_latent_norm", "kv_latent_norm"):
                r0, r1 = VR[name]
                src = t[name]
                if len(src.shape) == 2:
                    src = src.rearrange("l (k p) -> (l k) p", p=P)
                else:
                    src = src.rearrange("(k p) -> k p", p=P)
                tile, off = (rows_a, 0) if r0 < P else (rows_b, P)
                loads.append((tile[r0 - off:r1 - off, :], src))
            for name, n, reps in (("a_q_norm", HD, 2), ("a_k_norm", HD, 2), ("b_q_norm", QK, 1), ("kv_k_norm", QK, 1)):
                src = t[name] if len(t[name].shape) == 2 else t[name].rearrange("(a n) -> a n", a=1)
                r = VR[name][0] - P
                for rep in range(reps):
                    loads.append((rows_b[r:r + 1, rep * n:rep * n + n], src))
            return loads

        ROWS_IN = 16 * len(rows_loads())

        chunks = []

        def chunk(name, src, k, n):
            chunks.append((name, src, k, n))

        def by_rows(w):
            return w.rearrange("(k p) n -> p k n", p=P)

        for l in range(2):
            for j in range(24):
                chunk(("ada", l, j), by_rows(t["ada_w"][l])[:, :, j * 256:(j + 1) * 256], KT, 256)
        for j in range(8):
            chunk(("kvada", 0, j), by_rows(t["kv_ada_w"])[:, :, j * 256:(j + 1) * 256], KT, 256)
        for j in range(12):
            chunk(("qkv", 0, j), by_rows(t["a_w_qkv"][0])[:, :, j * 256:(j + 1) * 256], KT, 256)
        for l in range(2):
            if l == 1:
                kvd = by_rows(t["kv_w_down"])
                chunk(("kvd", 1, 0), kvd[:, :, 0:KVR], KT, KVR)
                chunk(("kvd", 1, 1), kvd[:, :, KVR:KVR + ROPE], KT, ROPE)
                dq = by_rows(t["b_w_dq"][0])
                chunk(("dq", 1, 0), dq[:, :, 0:256], KT, 256)
                chunk(("dq", 1, 1), dq[:, :, 256:QR], KT, QR - 256)
                chunk(("uk", 1, 0), by_rows(t["kv_w_uk"]), 2, D)
                chunk(("uv", 1, 0), by_rows(t["kv_w_uv"]), 2, D)
                for j in range(3):
                    chunk(("uq", 1, j), by_rows(t["b_w_uq"][0])[:, :, j * 512:(j + 1) * 512], 3, 512)
            wo = by_rows(t["a_w_o"][0] if l == 0 else t["b_w_o"][0])
            for j in range(4):
                chunk(("wo", l, j), wo[:, :, j * 256:(j + 1) * 256], KT, 256)
            sgu = by_rows(t["moe_shared_gate_up"][l])
            for j in range(2):
                chunk(("sgu", l, j), sgu[:, :, j * 256:(j + 1) * 256], KT, 256)
            chunk(("sdn", l, 0), by_rows(t["moe_shared_down"][l]), 2, D)
        number = {c[0]: i for i, c in enumerate(chunks)}

        def slot(name):
            i = number[name]
            _, _, k, n = chunks[i]
            return ring[:, i % RING, 0:k * n].rearrange("p (k n) -> p k n", k=k)

        def link(eng, ins):
            s = sem("chain_" + eng[0])
            eng[1] += 1
            ins.then_inc(s, 1)
            eng[2].wait_ge(s, eng[1])

        block = ctx.enter_context(nc.Block())

        @block.sync
        def _(sp):
            def load_chunks(names):
                for name in names:
                    i = number[name]
                    _, src, k, n = chunks[i]
                    if i >= RING:
                        sp.wait_ge(sem("chunk_used"), i - RING + 1)
                    sp.dma_start(slot(name), src).then_inc(sem(f"chunk_in{i % RING}"), 16)

            def expert_pair(l, i, e0, e1, first):
                for u, e in ((0, e0), (1, e1)):
                    if not first:
                        sp.wait_ge(sem(f"gu_done{l}"), 2 * i + u - 1)
                    sp.dma_start(w_gu[u][:, :, :], gu_src[l](e)).then_inc(sem(f"gu_in{l}{u}"), 16)
                for u, e in ((0, e0), (1, e1)):
                    if not first:
                        sp.wait_ge(sem(f"down_done{l}"), 2 * i + u - 1)
                    sp.dma_start(w_dn[u][:, :, :], dn_src[l](e)).then_inc(sem(f"dn_in{l}{u}"), 16)

            gu_all = t["moe_w_gate_up"].rearrange("l e (k p) n -> l p e k n", p=P)
            dn_all = t["moe_w_down"].rearrange("l e (k p) n -> l p e k n", p=P)
            gu_src = [lambda e, l=l: gu_all[l][:, bass.ds(e, 1), :, :].rearrange("p e k n -> p (e k) n") for l in range(2)]
            dn_src = [lambda e, l=l: dn_all[l][:, bass.ds(e, 1), :, :].rearrange("p e k n -> p (e k) n") for l in range(2)]

            order = [c[0] for c in chunks]
            cut = [number[("sdn", 0, 0)] + 1, len(order)]
            done = 0
            for l in range(2):
                if l == 0:
                    load_chunks(order[0:RING])
                    done = RING
                if l == 1:
                    sp.wait_ge(sem("x_new"), 2)
                expert_pair(l, 0, 0, 1, True)
                load_chunks(order[done:cut[l]])
                done = cut[l]
                if l == 0:
                    ahead = order[done:done + RING]
                with sp.Fori(1, E // 2) as i:
                    expert_pair(l, i, 2 * i, 2 * i + 1, False)
                sp.wait_ge(sem("table"), l + 1)
                trips = sp.value_load(tab_i[0:1, OVER:OVER + 1], min_val=E // 2, max_val=ITEMS // 2)
                with sp.If(trips > E // 2):
                    with sp.Fori(E // 2, trips) as i:
                        e0 = sp.value_load(tab_i[0:1, bass.ds(2 * i - E, 1)], min_val=0, max_val=E - 1)
                        e1 = sp.value_load(tab_i[0:1, bass.ds(2 * i - E + 1, 1)], min_val=0, max_val=E - 1)
                        expert_pair(l, i, e0, e1, False)
                if l == 0:
                    load_chunks(ahead)
                    done += RING
            sp.wait_ge(sem("x_new"), 4)
            sp.dma_start(out.rearrange("b (t p) d -> p (b t) d", p=P), x[:, :, :]).then_inc(sem("stored"), 16)
            sp.wait_ge(sem("stored"), 16)

        @block.tensor
        def _(pe):
            def use(name):
                i = number[name]
                pe.wait_ge(sem(f"chunk_in{i % RING}"), 16 * (i // RING + 1))
                return slot(name)

            def used(ins):
                ins.then_inc(sem("chunk_used"), 1)

            def mm(o, a, b, first, last):
                return nc.tensor.matmul(o, a, b, start=first, stop=last)

            def tr(o, a, rows=P):
                return nc.tensor.transpose(o, a, const("ident")[0:rows, 0:rows])

            def norm_transposes(n):
                pe.wait_ge(sem("xn_ready"), 2 * n + 2)
                for j in range(4):
                    for kk in range(2):
                        for ti in range(NT):
                            k = 2 * j + kk
                            last = tr(bank[j][:, kk * N + ti * P:kk * N + (ti + 1) * P], xn[:, ti, k * P:(k + 1) * P])
                    last.then_inc(sem("xT_ps"), 1)
                pe.wait_ge(sem("hT_dve"), 2 * (n + 1))
                pe.wait_ge(sem("hT_act"), 2 * (n + 1))

            def gates(l):
                for g in range(2):
                    pe.wait_ge(sem("diag"), 2 * l + g + 1)
                    for half in range(2):
                        b = bank[4 + half]
                        mm(b[:, :], const("ones"), diag[:, 4 * half:4 * half + 4, :].rearrange("p k n -> p (k n)"), True, True)\
                            .then_inc(sem("gate_ps"), 1)
                    pe.wait_ge(sem("gate_sb"), 2 * (2 * l + g) + 2)

            def attention(l, q_of, k_of):
                base = H * l

                def scores(h):
                    if h >= 3:
                        pe.wait_ge(sem("s_ready"), base + h - 2)
                    b = bank[h % 3]
                    mm(b[:, 0:P], q_of(h)[:, 0:P], k_of(h)[:, 0:P], True, True)
                    mm(b[:, P:SC], q_of(h)[:, P:N], k_of(h), True, True).then_inc(sem("s_ps"), 1)

                def p_transposes(h):
                    pe.wait_ge(sem("p_ready"), base + h + 1)
                    if h >= 2:
                        pe.wait_ge(sem("pT_sb"), base + h - 1)
                    for c in range(3):
                        last = tr(bank[3 + h % 2][:, c * P:(c + 1) * P], p_sb[:, h % 2, c * P:(c + 1) * P])
                    last.then_inc(sem("pT_ps"), 1)

                def values(h):
                    pe.wait_ge(sem("pT_sb"), base + h + 1)
                    if h >= 2:
                        pe.wait_ge(sem("o_sb"), base + h - 1)
                    b, pT, vh = bank[5 + h % 2], pT_sb[:, h % 2, :], slice(h * HD, (h + 1) * HD)
                    mm(b[:, 0:HD], pT[:, 0:P], v_sb[:, 0, vh], True, True)
                    mm(b[:, HD:2 * HD], pT[:, P:2 * P], v_sb[:, 0, vh], True, False)
                    mm(b[:, HD:2 * HD], pT[:, 2 * P:SC], v_sb[:, 1, vh], False, True).then_inc(sem("o_ps"), 1)

                for i in range(H + 3):
                    if i < H:
                        scores(i)
                    if 2 <= i < H + 2:
                        p_transposes(i - 2)
                    if i >= 3:
                        values(i - 3)
                pe.wait_ge(sem("o_sb"), base + H)
                pe.wait_ge(sem("s_ready"), base + H)
                for j in range(4):
                    for kk in range(2):
                        for ti in range(NT):
                            k = 2 * j + kk
                            last = tr(bank[j][:, kk * N + ti * P:kk * N + (ti + 1) * P], xn[:, ti, k * P:(k + 1) * P])
                    last.then_inc(sem("oT_ps"), 1)
                pe.wait_ge(sem("oT_dve"), 2 * (l + 1))
                pe.wait_ge(sem("oT_act"), 2 * (l + 1))
                for c in range(4):
                    w = use(("wo", l, c))
                    for ti in range(NT):
                        for k in range(KT):
                            last = mm(bank[4 + c][:, ti * N:(ti + 1) * N], hT[:, k, ti * P:(ti + 1) * P], w[:, k, :],
                                      k == 0, k == KT - 1)
                    used(last)

            def experts(l):
                for ti in range(NT):
                    for k in range(KT):
                        last = mm(bank[4][:, ti * E:(ti + 1) * E], hT[:, k, ti * P:(ti + 1) * P], w_router[:, l, k, :],
                                  k == 0, k == KT - 1)
                last.then_inc(sem("logits"), 1)
                for j in range(4):
                    ti, half = j // 2, j % 2
                    if j >= 2:
                        pe.wait_ge(sem("h_act" if j % 2 == 0 else "h_dve"), 2 * l + 1)
                    b = bank[5 + j % 2]
                    for k in range(4):
                        last = tr(b[:, k * P:(k + 1) * P], hT[:, 4 * half + k, ti * P:(ti + 1) * P])
                    last.then_inc(sem("h_ps"), 1)
                pe.wait_ge(sem("h_dve"), 2 * l + 2)
                for j in range(2):
                    w = use(("sgu", l, j))
                    for f in range(2):
                        for k in range(KT):
                            last = mm(bank[6 + j][:, f * N:(f + 1) * N], w[:, k, f * P:(f + 1) * P], hT[:, k, :],
                                      k == 0, k == KT - 1)
                    used(last)
                w = use(("sdn", l, 0))
                pe.wait_ge(sem("sh_h"), l + 1)
                for ti in range(NT):
                    for half in range(2):
                        for f in range(2):
                            last = nc.tensor.matmul(bank[2 * ti + half][:, :], sh_h[:, f, ti * P:(ti + 1) * P],
                                                    w[:, f, half * 512:(half + 1) * 512], start=f == 0, stop=False,
                                                    skip_group_check=True)
                used(last)
                pe.wait_ge(sem("chosen"), l + 1)
                pe.wait_ge(sem("score"), l + 1)
                mm(bank[4][:, 0:E], const("tri"), chosen[:, 0, :], True, True)
                mm(bank[4][:, E:2 * E], const("ones"), chosen[:, 0, :], True, False)
                mm(bank[4][:, E:2 * E], const("tri"), chosen[:, 1, :], False, True).then_inc(sem("ranks"), 1)
                for ti in range(NT):
                    last = mm(bank[5][0:E, 0:1], chosen[:, ti, :], const("ones")[:, 0:1], ti == 0, ti == NT - 1)
                last.then_inc(sem("counts"), 1)
                pe.wait_ge(sem("flags"), l + 1)
                mm(bank[5][0:E, 4:7], const("tri")[0:E, 0:E], flag[:, 0:3], True, False)
                mm(bank[5][0:E, 5:7], const("ones")[0:E, 0:E], flag[:, 0:2], False, False)
                mm(bank[5][0:E, 6:7], const("ones")[0:E, 0:E], flag[:, 0:1], False, True)
                mm(bank[5][0:1, 8:9], flag[:, 3:4], const("ones")[0:E, 0:1], True, True).then_inc(sem("places"), 1)
                pe.wait_ge(sem("slots"), l + 1)
                for ti in range(NT):
                    tr(bank[6][0:E, ti * P:(ti + 1) * P], slot_of[:, ti, 0:E])
                for ti in range(NT):
                    last = tr(bank[6][0:E, N + ti * P:N + (ti + 1) * P], w_of[:, ti, 0:E])
                last.then_inc(sem("tabT_ps"), 1)
                pe.wait_ge(sem("tabT"), l + 1)
                pe.wait_ge(sem("onehot"), l + 1)
                for ti in range(NT):
                    o = bank[7][:, ti * OVER:(ti + 1) * OVER]
                    for c in range(3):
                        mm(o, rtT[:, 0, ti * P:(ti + 1) * P], onehot[:, c, :], c == 0, False)
                    mm(o, const("ones")[0:E, :], onehot[:, 3, :], False, True)
                for ti in range(NT):
                    mm(bank[7][:, 64 + ti * OVER:64 + (ti + 1) * OVER], rtT[:, 1, ti * P:(ti + 1) * P], onehot[:, 4, :],
                       True, True)
                mm(bank[7][0:1, 128:128 + OVER], const("row")[0:E, :], onehot[:, 4, :], True, True)\
                    .then_inc(sem("over_ps"), 1)
                pe.wait_ge(sem("table"), l + 1)

                def gate_up(p):
                    pe.wait_ge(sem(f"xg_ready{l}"), p + 1)
                    pe.wait_ge(sem(f"st_ready{l}"), p + 1)
                    for u in range(2):
                        pe.wait_ge(sem(f"gu_in{l}{u}"), 16 * p + 16)
                        for k in range(KT):
                            last = mm(bank[5][u * C:(u + 1) * C, :], xg[:, k, u * C:(u + 1) * C], w_gu[u][:, k, :],
                                      k == 0, k == KT - 1)
                        last.then_inc(sem(f"gu_done{l}"), 1)

                def scatter(count, stop):
                    pe.wait_ge(sem(f"y_act{l}"), count)
                    pe.wait_ge(sem(f"y_dve{l}"), count)
                    for ti in range(NT):
                        for half in range(2):
                            last = nc.tensor.matmul(bank[2 * ti + half][:, :], st[:, ti * P:(ti + 1) * P],
                                                    y_sb[:, half * 512:(half + 1) * 512], start=False, stop=stop,
                                                    skip_group_check=True)
                    return last

                def gather(count):
                    pe.wait_ge(sem(f"sel_ready{l}"), count)
                    for k in range(KT):
                        b = bank[4 if k < 4 else 7]
                        for ti in range(NT):
                            last = mm(b[:, (k % 4) * P:(k % 4 + 1) * P], h_tok[:, ti, k * P:(k + 1) * P],
                                      sel[:, ti, :, :].rearrange("p u c -> p (u c)"), ti == 0, ti == NT - 1)
                    last.then_inc(sem(f"gath_done{l}"), 1)

                def middle(p):
                    pe.wait_ge(sem(f"hh_ready{l}"), p + 1)
                    for f in range(2):
                        last = tr(bank[6][:, f * P:(f + 1) * P], hh[:, f * P:(f + 1) * P])
                    last.then_inc(sem(f"hhT_done{l}"), 1)

                def weights_transposed(p):
                    pe.wait_ge(sem(f"selw_ready{l}"), p + 1)
                    for ti in range(NT):
                        last = tr(bank[5][:, ti * P:(ti + 1) * P], selw[:, ti, :, :].rearrange("p u c -> p (u c)"))
                    last.then_inc(sem(f"stT_done{l}"), 1)

                def down(p):
                    pe.wait_ge(sem(f"hhT_sb{l}"), p + 1)
                    for u in range(2):
                        pe.wait_ge(sem(f"dn_in{l}{u}"), 16 * p + 16)
                        for half in range(2):
                            if u == 0 and half == 1:
                                pe.wait_ge(sem(f"xg_ready{l}"), p + 2)
                            for f in range(2):
                                last = mm(bank[6 + half][u * C:(u + 1) * C, :], hhT[:, f, u * C:(u + 1) * C],
                                          w_dn[u][:, f, half * 512:(half + 1) * 512], f == 0, f == 1)
                        last.then_inc(sem(f"down_done{l}"), 1)

                gather(1)
                trips = pe.value_load(tab_i[0:1, OVER:OVER + 1], min_val=E // 2, max_val=ITEMS // 2)
                with pe.Fori(0, trips) as p:
                    gate_up(p)
                    scatter(p + 1, False)
                    middle(p)
                    gather(p + 2)
                    weights_transposed(p)
                    down(p)
                scatter(trips + 1, True).then_inc(sem("routed"), 1)

            pe.wait_ge(sem("rows_in"), ROWS_IN)
            pe.wait_ge(sem("const_in"), 16)
            tr(bank[7][:, 0:P], rows_a[:, :])
            nc.tensor.transpose(bank[7][:, P:NROWS], rows_b[0:NROWS_B, :], const("ident")[0:NROWS_B, 0:NROWS_B])\
                .then_inc(sem("vcol_ps"), 1)
            pe.wait_ge(sem("csilu"), 1)
            for names, b in (([("ada", 0, j) for j in range(24)], 6), ([("ada", 1, j) for j in range(24)], 5),
                             ([("kvada", 0, j) for j in range(8)], 7)):
                for n, name in enumerate(names):
                    w = use(name)
                    for m in range(2):
                        c = 2 * n + m
                        for k in range(KT):
                            last = mm(bank[b][:, c:c + 1], w[:, k, m * P:(m + 1) * P], csilu[:, k:k + 1], k == 0, k == KT - 1)
                    used(last)
            gates(0)
            norm_transposes(0)

            def qk_transposes(c):
                pe.wait_ge(sem("qkv_sb"), c + 1)
                if c >= 2:
                    pe.wait_ge(sem("qkT_sb"), c - 1)
                for b2 in range(2):
                    for ti in range(NT):
                        last = tr(bank[4 + c % 2][:, b2 * N + ti * P:b2 * N + (ti + 1) * P],
                                  qkn[:, c % 3, ti * N + b2 * P:ti * N + (b2 + 1) * P])
                last.then_inc(sem("qkT_ps"), 1)

            for c in range(12):
                w = use(("qkv", 0, c))
                if c >= 4:
                    pe.wait_ge(sem("qkv_sb"), c - 3)
                for ti in range(NT):
                    for k in range(KT):
                        last = mm(bank[c % 4][:, ti * N:(ti + 1) * N], hT[:, k, ti * P:(ti + 1) * P], w[:, k, :],
                                  k == 0, k == KT - 1)
                used(last)
                if 2 <= c < 10:
                    qk_transposes(c - 2)
            pe.wait_ge(sem("qkv_sb"), 12)
            pe.wait_ge(sem("qkT_sb"), 8)
            pair = lambda tt: (lambda h: tt[HD * (h % 2):HD * (h % 2) + HD, h // 2, :])
            attention(0, pair(qT), pair(kT))
            norm_transposes(1)
            experts(0)
            gates(1)
            norm_transposes(2)
            for i, (name, b, n) in enumerate(((("kvd", 1, 0), 4, KVR), (("kvd", 1, 1), 5, ROPE), (("dq", 1, 0), 6, 256),
                                              (("dq", 1, 1), 7, QR - 256))):
                w = use(name)
                src = hkvT if name[0] == "kvd" else hT
                for ti in range(NT):
                    for k in range(KT):
                        last = mm(bank[b][:, ti * n:(ti + 1) * n], src[:, k, ti * P:(ti + 1) * P], w[:, k, :],
                                  k == 0, k == KT - 1)
                used(last)
            pe.wait_ge(sem("lat_n"), 1)
            for kk in range(2):
                for ti in range(NT):
                    last = tr(bank[0][:, kk * N + ti * P:kk * N + (ti + 1) * P], lat_kv[:, ti, kk * P:(kk + 1) * P])
            last.then_inc(sem("latT_ps"), 1)
            pe.wait_ge(sem("lat_n"), 2)
            for kk in range(3):
                for ti in range(NT):
                    last = tr(bank[1 + kk // 2][:, (kk % 2) * N + ti * P:(kk % 2) * N + (ti + 1) * P],
                              lat_q[:, ti, kk * P:(kk + 1) * P])
            last.then_inc(sem("latT_ps"), 1)
            up = ((("uk", 1, 0), lat_kvT, 2, 4, 0), (("uv", 1, 0), lat_kvT, 2, 0, 0), (("uq", 1, 0), lat_qT, 3, 4, 2),
                  (("uq", 1, 1), lat_qT, 3, 6, 2), (("uq", 1, 2), lat_qT, 3, 0, 4))
            pe.wait_ge(sem("latT_sb"), 1)
            for name, src, kn, b, copied in up:
                w = use(name)
                if name[0] != "uk":
                    pe.wait_ge(sem("latT_sb"), 2)
                if copied:
                    pe.wait_ge(sem("up_dve"), copied)
                    pe.wait_ge(sem("up_act"), copied)
                for ti in range(NT):
                    for half in range(2 if kn == 2 else 1):
                        o = bank[b + (2 * ti + half if kn == 2 else ti)]
                        for k in range(kn):
                            last = mm(o[:, :], src[:, k, ti * P:(ti + 1) * P], w[:, k, half * 512:(half + 1) * 512],
                                      k == 0, k == kn - 1)
                used(last)
            pe.wait_ge(sem("qk_norm"), 1)
            pe.wait_ge(sem("up_act"), 7)
            for g in range(8):
                for side, (src, b) in enumerate(((q_sb, 0), (k_sb, 2))):
                    if g >= 2:
                        pe.wait_ge(sem("mT_act" if side == 0 else "mT_dve"), g - 1)
                    for hh_ in range(2):
                        for ti in range(NT):
                            last = tr(bank[b + g % 2][0:QK, hh_ * N + ti * P:hh_ * N + (ti + 1) * P],
                                      src[:, ti, 2 * g + hh_, :])
                    last.then_inc(sem("mT_ps"), 1)
            pe.wait_ge(sem("mT_act"), 8)
            pe.wait_ge(sem("mT_dve"), 8)
            attention(1, lambda h: qT[0:QK, h, :], lambda h: kT[0:QK, h, :])
            norm_transposes(3)
            experts(1)

        @block.scalar
        def _(act):
            A = ["act", 0, act]

            def after(name):
                act.wait_ge(sem("chunk_used"), number[name] + 1)

            def copy(o, i, **kw):
                return nc.scalar.activation(o, i, ACT.Copy, **kw)

            act.dma_start(x[:, :, :], t["x"].rearrange("b (t p) d -> p (b t) d", p=P)).then_inc(sem("x_in"), 16)
            act.dma_start(cst[:, :], t["consts"]).then_inc(sem("const_in"), 16)
            act.wait_ge(sem("rows_zero"), 1)
            for dst, src in rows_loads():
                act.dma_start(dst, src).then_inc(sem("rows_in"), 16)
            act.dma_start(w_router[:, :, :, :].rearrange("p l k e -> p (l k) e"),
                          t["moe_w_router"].rearrange("l (k p) e -> p (l k) e", p=P)).then_inc(sem("small_in"), 16)
            for l in range(2):
                act.dma_start(bias_row[:, l, :], t["moe_router_bias"][l:l + 1, :].broadcast_to([P, E])).then_inc(sem("small_in"), 16)
            act.dma_start(ropeg[:, 0, :], t["b_q_norm"][0:1, HD:QK].broadcast_to([P, ROPE])).then_inc(sem("small_in"), 16)
            act.dma_start(ropeg[:, 1, :], t["kv_k_norm"].rearrange("(a n) -> a n", a=1)[:, HD:QK].broadcast_to([P, ROPE]))\
               .then_inc(sem("small_in"), 16)
            act.dma_start(pos_k[:, :], t["pos"].broadcast_to([P, N])).then_inc(sem("small_in"), 16)
            act.dma_start(pos_q[:, :], t["pos"].rearrange("b (t p) -> p (b t)", p=P), allow_slow_non_contiguous=True).then_inc(sem("small_in"), 16)

            act.wait_ge(sem("vcol"), 1)
            nc.scalar.activation(csilu[:, :], col("c", 0, 8), ACT.Silu).then_inc(sem("csilu"), 1)

            def gates(l):
                for g in range(2):
                    if l == 1 and g == 0:
                        act.wait_ge(sem("x_new"), 2)
                    for half in range(2):
                        act.wait_ge(sem("gate_ps"), 2 * (2 * l + g) + half + 1)
                        copy(gate[:, g, half * 512:(half + 1) * 512], bank[4 + half][:, :]).then_inc(sem("gate_sb"), 1)

            def norm(n, outs):
                if n == 0:
                    act.wait_ge(sem("x_in"), 16)
                else:
                    act.wait_ge(sem("x_new"), n)
                for ti in range(NT):
                    link(A, nc.scalar.activation(junk[:, :], x[:, ti, :], ACT.Square, accum_out=small[:, ti:ti + 1]))
                nc.scalar.activation(small[:, 2:4], small[:, 0:2], ACT.Sqrt, bias=eps_c, scale=1.0 / D)\
                    .then_inc(sem("x_rt"), 1)
                act.wait_ge(sem("amp"), 1)
                for j in (1, 3):
                    act.wait_ge(sem("xT_ps"), 4 * n + j + 1)
                    for a, s0, dst in outs:
                        for kk in range(2):
                            k = 2 * j + kk
                            last = nc.scalar.activation(dst[:, k, :], bank[j][:, kk * N:(kk + 1) * N], ACT.Identity,
                                                        bias=mod[:, s0 + k:s0 + k + 1], scale=amp[:, a, k:k + 1])
                    last.then_inc(sem("hT_act"), 1)

            def attention(l):
                base = H * l
                for i in range(H + 3):
                    if i < H:
                        act.wait_ge(sem("s_ready"), base + i + 1)
                        if i >= 2:
                            act.wait_ge(sem("pT_ps"), base + i - 1)
                        nc.scalar.activation(p_sb[:, i % 2, 0:P], s_sb[:, i % 2, 0:P], ACT.Exp, bias=nmax[:, i, 0:1],
                                             accum_out=lsum[:, i, 0:1])
                        nc.scalar.activation(p_sb[:, i % 2, P:SC], s_sb[:, i % 2, P:SC], ACT.Exp, bias=nmax[:, i, 1:2],
                                             accum_out=lsum[:, i, 1:2]).then_inc(sem("p_ready"), 1)
                    h = i - 2
                    if 0 <= h < H:
                        act.wait_ge(sem("pT_ps"), base + h + 1)
                        if h >= 2:
                            act.wait_ge(sem("o_ps"), base + h - 1)
                        copy(pT_sb[:, h % 2, :], bank[3 + h % 2][:, 0:SC]).then_inc(sem("pT_sb"), 1)
                for j in (1, 3):
                    act.wait_ge(sem("oT_ps"), 4 * l + j + 1)
                    copy(hT[:, 2 * j:2 * j + 2, :].rearrange("p k n -> p (k n)"), bank[j][:, :]).then_inc(sem("oT_act"), 1)

            def experts(l):
                act.wait_ge(sem("logits"), l + 1)
                nc.scalar.activation(score[:, :, :].rearrange("p t e -> p (t e)"), bank[4][:, 0:NT * E], ACT.Sigmoid)\
                    .then_inc(sem("score"), 1)
                for j in (0, 2):
                    act.wait_ge(sem("h_ps"), 4 * l + j + 1)
                    copy(h_tok[:, j // 2, 0:512], bank[5][:, :]).then_inc(sem("h_act"), 1)
                after(("sgu", l, 0))
                nc.scalar.activation(sh_g[:, :, :].rearrange("p f n -> p (f n)"), bank[6][:, :], ACT.Silu)\
                    .then_inc(sem("sh_g"), 1)

                def gathered(count):
                    act.wait_ge(sem(f"gath_done{l}"), count)
                    for b, k in ((7, 4), (4, 0)):
                        last = copy(xg[:, k:k + 4, :].rearrange("p k c -> p (k c)"), bank[b][:, :])
                    last.then_inc(sem(f"xg_ready{l}"), 1)

                act.wait_ge(sem("table"), l + 1)
                gathered(1)
                trips = act.value_load(tab_i[0:1, OVER:OVER + 1], min_val=E // 2, max_val=ITEMS // 2)
                with act.Fori(0, trips) as p:
                    act.wait_ge(sem(f"gu_done{l}"), 2 * p + 2)
                    nc.scalar.activation(sg[:, :], bank[5][:, 0:FE], ACT.Silu).then_inc(sem(f"silu_done{l}"), 1)
                    gathered(p + 2)
                    act.wait_ge(sem(f"down_done{l}"), 2 * p + 2)
                    copy(y_sb[:, 0:512], bank[6][:, :]).then_inc(sem(f"y_act{l}"), 1)

            gates(0)
            norm(0, ((0, 0, hT),))
            for c in range(10):
                if c < 8:
                    after(("qkv", 0, c))
                    if c >= 2:
                        act.wait_ge(sem("ssq"), c - 1)
                    nc.scalar.activation(sq[:, c % 2, :], bank[c % 4][:, :], ACT.Square).then_inc(sem("sq"), 1)
                    act.wait_ge(sem("ssq"), c + 1)
                    nc.scalar.activation(srt[:, c, :], ssq[:, c, :], ACT.Sqrt, bias=eps_c, scale=1.0 / HD)\
                        .then_inc(sem("srt"), 1)
                if c >= 2:
                    b = c - 2
                    act.wait_ge(sem("qkT_ps"), b + 1)
                    src = bank[4 + b % 2][:, :]
                    if b < 4:
                        copy(qT[:, 2 * b:2 * b + 2, :].rearrange("p k n -> p (k n)"), src, scale=qk_gain[:, 0:1])\
                            .then_inc(sem("qkT_sb"), 1)
                    else:
                        copy(kT[:, 2 * b - 8:2 * b - 6, :].rearrange("p k n -> p (k n)"), src).then_inc(sem("qkT_sb"), 1)
            attention(0)
            norm(1, ((1, 24, hT),))
            experts(0)

            gates(1)
            act.wait_ge(sem("angles"), 1)
            for a in range(2):
                last = nc.scalar.activation(ang[:, 4 + a, :, :], ang[:, 2 + a, :, :], ACT.Sin)
            last.then_inc(sem("sines"), 1)
            norm(2, ((2, 48, hT), (4, 96, hkvT)))
            act.wait_ge(sem("lat_raw"), 1)
            for ti in range(NT):
                nc.scalar.activation(junk[:, 512 + ti * ROPE:512 + (ti + 1) * ROPE], kpe[:, ti, :], ACT.Square, accum_out=small[:, 12 + ti:13 + ti])
                link(A, nc.scalar.activation(junk[:, 0:KVR], lat_kv[:, ti, :], ACT.Square, accum_out=small[:, 8 + ti:9 + ti]))
            nc.scalar.activation(small[:, 14:16], small[:, 8:10], ACT.Sqrt, bias=eps_c, scale=1.0 / KVR)\
                .then_inc(sem("lat_rt"), 1)
            act.wait_ge(sem("lat_raw"), 2)
            for ti in range(NT):
                link(A, nc.scalar.activation(junk[:, 0:QR], lat_q[:, ti, :], ACT.Square, accum_out=small[:, 10 + ti:11 + ti]))
            nc.scalar.activation(small[:, 16:18], small[:, 10:12], ACT.Sqrt, bias=eps_c, scale=1.0 / QR)\
                .then_inc(sem("lat_rt"), 1)
            act.wait_ge(sem("latT_ps"), 1)
            for kk in range(2):
                last = copy(lat_kvT[:, kk, :], bank[0][:, kk * N:(kk + 1) * N], scale=col("kv_latent_norm", kk))
            last.then_inc(sem("latT_sb"), 1)
            act.wait_ge(sem("latT_ps"), 2)
            for kk in range(3):
                last = copy(lat_qT[:, kk, :], bank[1 + kk // 2][:, (kk % 2) * N:(kk % 2 + 1) * N],
                            scale=col("b_q_latent_norm", kk))
            last.then_inc(sem("latT_sb"), 1)
            after(("uk", 1, 0))
            for ti in range(NT):
                copy(k_sb[:, ti, 8:16, 0:HD], bank[4 + 2 * ti + 1][:, :].rearrange("p (h d) -> p h d", d=HD))\
                    .then_inc(sem("up_act"), 1)
            after(("uv", 1, 0))
            for ti in range(NT):
                copy(v_sb[:, ti, 512:1024], bank[2 * ti + 1][:, :]).then_inc(sem("up_act"), 1)
            for j, b in enumerate((4, 6, 0)):
                after(("uq", 1, j))
                copy(q_flat(1)[:, j * 512:(j + 1) * 512], bank[b + 1][:, :]).then_inc(sem("up_act"), 1)
            act.wait_ge(sem("qk_ss"), 1)
            nc.scalar.activation(hs_rs[:, 2:4, :, :], hs_rs[:, 0:2, :, :], ACT.Sqrt, bias=eps_c, scale=1.0 / QK)\
                .then_inc(sem("qk_rt"), 1)
            for g in range(8):
                act.wait_ge(sem("mT_ps"), 2 * g + 1)
                copy(qT[0:QK, 2 * g:2 * g + 2, :].rearrange("p k n -> p (k n)"), bank[g % 2][0:QK, :], scale=qk_gain[0:QK, 1:2])\
                    .then_inc(sem("mT_act"), 1)
            attention(1)
            norm(3, ((3, 72, hT),))
            experts(1)

        @block.vector
        def _(dve):
            V = ["dve", 0, dve]
            v = nc.vector

            def after(name):
                dve.wait_ge(sem("chunk_used"), number[name] + 1)

            def flat(a):
                return a.rearrange("p a b -> p (a b)")

            dve.wait_ge(sem("vcol_ps"), 1)
            link(V, v.tensor_copy(vcol[:, :], bank[7][:, 0:NROWS]))
            v.tensor_copy(small[:, 40:41], vcol[:, 0:1]).then_inc(sem("vcol"), 1)
            link(V, v.memset(qk_gain[:, 1:2], QK ** -0.5))
            link(V, v.tensor_tensor(qk_gain[:, 0:1], col("a_q_norm"), col("a_k_norm"), ALU.mult))
            link(V, v.tensor_scalar(qk_gain[:, 0:1], qk_gain[:, 0:1], HD ** -0.5, None, ALU.mult))
            link(V, v.scalar_tensor_tensor(out=qk_gain[0:HD, 1:2], in0=col("b_q_norm", rows=HD), scalar=QK ** -0.5,
                                           in1=col("kv_k_norm", rows=HD), op0=ALU.mult, op1=ALU.mult))
            dve.wait_ge(sem("small_in"), 7 * 16)
            link(V, v.tensor_copy(pos_kf[:, :], pos_k[:, :]))
            link(V, v.tensor_copy(pos_qf[:, :], pos_q[:, :]))

            for b, base, n, bias, name in ((6, 0, 48, col("ada_b", 0, 48), ("ada", 0, 23)),
                                           (5, 48, 48, col("ada_b", 48, 48), ("ada", 1, 23)),
                                           (7, 96, 16, col("kv_ada_b", 0, 16), ("kvada", 0, 7))):
                after(name)
                link(V, v.tensor_tensor(mod[:, base:base + n], bank[b][:, 0:n], bias, ALU.add))
            for a, s0, g in ((0, 8, col("norm1_g", 0, 8)), (1, 32, col("norm2_g", 0, 8)), (2, 56, col("norm1_g", 8, 8)),
                             (3, 80, col("norm2_g", 8, 8)), (4, 104, col("kv_norm_g", 0, 8))):
                ins = v.scalar_tensor_tensor(out=amp[:, a, :], in0=mod[:, s0:s0 + 8], scalar=1.0, in1=g, op0=ALU.add,
                                             op1=ALU.mult)
                if a < 4:
                    link(V, ins)
            ins.then_inc(sem("amp"), 1)
            dve.wait_ge(sem("amp"), 1)

            def gates(l):
                for g in range(2):
                    s0 = 48 * l + (16 if g == 0 else 40)
                    if 2 * l + g:
                        dve.wait_ge(sem("gate_ps"), 2 * (2 * l + g))
                    v.tensor_tensor(diag[:, :, :], const("ident").unsqueeze(1).broadcast_to([P, KT, P]),
                                    mod[:, s0:s0 + 8].unsqueeze(2).broadcast_to([P, KT, P]), ALU.mult)\
                        .then_inc(sem("diag"), 1)

            def norm(n, outs):
                dve.wait_ge(sem("x_rt"), n + 1)
                link(V, v.reciprocal(small[:, 4:6], small[:, 2:4]))
                for ti in range(NT):
                    v.tensor_scalar(xn[:, ti, :], x[:, ti, :], small[:, 4 + ti:5 + ti], None, ALU.mult)\
                        .then_inc(sem("xn_ready"), 1)
                for j in (0, 2):
                    dve.wait_ge(sem("xT_ps"), 4 * n + j + 1)
                    for a, s0, dst in outs:
                        for kk in range(2):
                            k = 2 * j + kk
                            last = v.tensor_scalar(dst[:, k, :], bank[j][:, kk * N:(kk + 1) * N], amp[:, a, k:k + 1],
                                                   mod[:, s0 + k:s0 + k + 1], ALU.mult, ALU.add)
                    last.then_inc(sem("hT_dve"), 1)

            def attention(l):
                base = H * l
                for i in range(H + 3):
                    if i < H:
                        b = i % 2
                        dve.wait_ge(sem("s_ps"), base + i + 1)
                        if i >= 2:
                            dve.wait_ge(sem("p_ready"), base + i - 1)
                        src = bank[i % 3]
                        mask = const("causal")
                        if l == 0:
                            slope = float(np.exp2(np.float32(-8.0 * (i + 1) / H)))
                            link(V, v.scalar_tensor_tensor(out=s_sb[:, b, :], in0=negrel[:, :], scalar=slope,
                                                           in1=src[:, 0:SC], op0=ALU.mult, op1=ALU.add))
                            src, mask = s_sb[:, b, :], const("logcount")
                        for ti, (c0, c1) in enumerate(((0, P), (P, SC))):
                            last = v.tensor_tensor_reduce(out=s_sb[:, b, c0:c1], in0=src[:, c0:c1], in1=mask[:, c0:c1],
                                                          scale=1.0, scalar=-3e38, op0=ALU.add, op1=ALU.max,
                                                          accum_out=smax[:, i, ti:ti + 1])
                        link(V, last)
                        v.tensor_scalar(nmax[:, i, :], smax[:, i, :], -1.0, None, ALU.mult).then_inc(sem("s_ready"), 1)
                    h = i - 3
                    if h >= 0:
                        dve.wait_ge(sem("o_ps"), base + h + 1)
                        link(V, v.reciprocal(rsum[:, h, :], lsum[:, h, :]))
                        v.tensor_tensor(xn[:, :, h * HD:(h + 1) * HD], bank[5 + h % 2][:, 0:2 * HD].rearrange("p (t d) -> p t d", t=2),
                                        rsum[:, h, :].unsqueeze(2).broadcast_to([P, NT, HD]), ALU.mult)\
                            .then_inc(sem("o_sb"), 1)
                for j in (0, 2):
                    dve.wait_ge(sem("oT_ps"), 4 * l + j + 1)
                    v.tensor_copy(flat(hT[:, 2 * j:2 * j + 2, :]), bank[j][:, :]).then_inc(sem("oT_dve"), 1)
                for c in range(4):
                    after(("wo", l, c))
                    gj = junk[:, (c % 2) * 512:(c % 2) * 512 + 512].rearrange("p (t n) -> p t n", t=NT)
                    link(V, v.tensor_tensor(gj, bank[4 + c][:, :].rearrange("p (t n) -> p t n", t=NT),
                                            gate[:, 0:1, c * N:(c + 1) * N].broadcast_to([P, NT, N]), ALU.mult))
                    xs = x[:, :, c * N:(c + 1) * N]
                    ins = v.tensor_tensor(xs, xs, gj, ALU.add)
                ins.then_inc(sem("x_new"), 1)
                dve.wait_ge(sem("x_new"), 2 * l + 1)

            def experts(l):
                big = 1e30
                for j in (1, 3):
                    dve.wait_ge(sem("h_ps"), 4 * l + j + 1)
                    v.tensor_copy(h_tok[:, j // 2, 512:1024], bank[6][:, :]).then_inc(sem("h_dve"), 1)
                dve.wait_ge(sem("score"), l + 1)
                link(V, v.tensor_tensor(choice[:, :, 0:E], score[:, :, :],
                                        bias_row[:, l:l + 1, :].broadcast_to([P, NT, E]), ALU.add))
                for ti in range(NT):
                    for g in range(G):
                        last = v.max(gsort[:, ti, g, :], choice[:, ti, 8 * g:8 * g + 8])
                link(V, last)
                link(V, v.tensor_tensor(gsc[:, :, 0:G], gsort[:, :, :, 0], gsort[:, :, :, 1], ALU.add))
                link(V, v.memset(gsc[:, :, G:G + TOPG], big))
                for ti in range(NT):
                    link(V, v.max(gtop[:, ti, :], gsc[:, ti, 0:G]))
                link(V, v.memset(gtop[:, :, TOPG:8], big))
                for ti in range(NT):
                    link(V, v.match_replace(gleft[:, ti, :], gtop[:, ti, :], gsc[:, ti, :], -3e38))
                link(V, v.tensor_tensor(gmask[:, :, :], gleft[:, :, 0:G], gsc[:, :, 0:G], ALU.not_equal))
                for ti in range(NT):
                    ch = choice[:, ti, 0:E].rearrange("p (g e) -> p g e", g=G)
                    link(V, v.tensor_tensor(ch, ch, gmask[:, ti, :].unsqueeze(2).broadcast_to([P, G, 8]), ALU.mult))
                link(V, v.tensor_scalar(gleft[:, :, 0:G], gmask[:, :, :], -1.0, big, ALU.add, ALU.mult))
                for ti in range(NT):
                    ch = choice[:, ti, 0:E].rearrange("p (g e) -> p g e", g=G)
                    link(V, v.tensor_tensor(ch, ch, gleft[:, ti, 0:G].unsqueeze(2).broadcast_to([P, G, 8]), ALU.add))
                link(V, v.memset(choice[:, :, E:E + 2], big))
                for ti in range(NT):
                    link(V, v.max(etop[:, ti, :], choice[:, ti, 0:E]))
                link(V, v.memset(etop[:, :, TOPK:8], big))
                for ti in range(NT):
                    link(V, v.match_replace(left[:, ti, :], etop[:, ti, :], choice[:, ti, :], -3e38))
                v.tensor_tensor(chosen[:, :, :], left[:, :, 0:E], choice[:, :, 0:E], ALU.not_equal).then_inc(sem("chosen"), 1)
                after(("sgu", l, 1))
                dve.wait_ge(sem("sh_g"), l + 1)
                v.tensor_tensor(flat(sh_h[:, :, :]), flat(sh_g[:, :, :]), bank[7][:, :], ALU.mult).then_inc(sem("sh_h"), 1)
                dve.wait_ge(sem("chosen"), l + 1)
                link(V, v.tensor_tensor(w_of[:, :, 0:E], score[:, :, :], chosen[:, :, :], ALU.mult))
                link(V, v.tensor_reduce(rden[:, :], w_of[:, :, 0:E], AX_X, ALU.add))
                link(V, v.reciprocal(rden[:, :], rden[:, :]))
                for ti in range(NT):
                    v.tensor_scalar(w_of[:, ti, 0:E], w_of[:, ti, 0:E], rden[:, ti:ti + 1], ROUTED_SCALE, ALU.mult, ALU.mult)
                v.memset(slot_of[:, :, ITEMS:ITEMS + 2], 0.0)
                v.memset(w_of[:, :, ITEMS:ITEMS + 2], 0.0)
                dve.wait_ge(sem("ranks"), l + 1)
                v.scalar_tensor_tensor(out=slot_of[:, :, 0:E], in0=bank[4][:, 0:NT * E].rearrange("p (t e) -> p t e", t=NT),
                                       scalar=1.0, in1=chosen[:, :, :], op0=ALU.add, op1=ALU.mult).then_inc(sem("slots"), 1)
                dve.wait_ge(sem("counts"), l + 1)
                link(V, v.tensor_copy(count[:, 0:1], bank[5][0:E, 0:1]))
                for c in range(3):
                    link(V, v.tensor_scalar(flag[:, c:c + 1], count[:, 0:1], float(C * (c + 1)), None, ALU.is_gt))
                v.tensor_reduce(flag[:, 3:4], flag[:, 0:3], AX_X, ALU.add).then_inc(sem("flags"), 1)
                dve.wait_ge(sem("places"), l + 1)
                link(V, v.tensor_copy(place[:, 0:3], bank[5][0:E, 4:7]))
                for c in range(3):
                    link(V, v.tensor_scalar(onehot[:, c, :], const("iota", E), place[:, c:c + 1], flag[:, c:c + 1],
                                            ALU.is_equal, ALU.mult))
                link(V, v.tensor_scalar(onehot[:, 3, :], onehot[:, 0, :], -float(C), None, ALU.mult))
                for c in (1, 2):
                    link(V, v.scalar_tensor_tensor(out=onehot[:, 3, :], in0=onehot[:, c, :], scalar=-float(C * (c + 1)),
                                                   in1=onehot[:, 3, :], op0=ALU.mult, op1=ALU.add))
                link(V, v.tensor_tensor(onehot[:, 4, :], onehot[:, 0, :], onehot[:, 1, :], ALU.add))
                v.tensor_tensor(onehot[:, 4, :], onehot[:, 4, :], onehot[:, 2, :], ALU.add).then_inc(sem("onehot"), 1)
                dve.wait_ge(sem("tabT_ps"), l + 1)
                v.tensor_copy(flat(rtT[:, :, :]), bank[6][0:E, :]).then_inc(sem("tabT"), 1)
                dve.wait_ge(sem("over_ps"), l + 1)
                v.tensor_copy(slot_of[:, :, E:ITEMS], bank[7][:, 0:NT * OVER].rearrange("p (t e) -> p t e", t=NT))
                v.tensor_copy(w_of[:, :, E:ITEMS], bank[7][:, 64:64 + NT * OVER].rearrange("p (t e) -> p t e", t=NT))
                v.tensor_copy(tab_i[:, 0:OVER], bank[7][0:1, 128:128 + OVER])
                v.tensor_scalar(tab_i[:, OVER:OVER + 1], bank[5][0:1, 8:9], 0.5, E / 2 + 0.25, ALU.mult, ALU.add)
                v.memset(y_sb[:, :], 0.0)
                v.memset(st[:, :], 0.0).then_inc(sem(f"st_ready{l}"), 1)
                v.memset(count[:, 1:2], 0.0).then_inc(sem("table"), 1)
                v.memset(count[:, 2:3], 0.0).then_inc(sem(f"y_act{l}"), 1)
                v.memset(count[:, 3:4], 0.0).then_inc(sem(f"y_dve{l}"), 1)
                dve.wait_ge(sem("table"), l + 1)

                slot1 = const("slot1").unsqueeze(1).unsqueeze(1).broadcast_to([P, NT, 2, C])

                def of_pair(table, p):
                    return table[:, :, bass.ds(2 * p, 2)].unsqueeze(3).broadcast_to([P, NT, 2, C])

                def select(p):
                    v.tensor_tensor(sel[:, :, :, :], slot1, of_pair(slot_of, p), ALU.is_equal)\
                        .then_inc(sem(f"sel_ready{l}"), 1)

                select(0)
                trips = dve.value_load(tab_i[0:1, OVER:OVER + 1], min_val=E // 2, max_val=ITEMS // 2)
                with dve.Fori(0, trips) as p:
                    dve.wait_ge(sem(f"gath_done{l}"), p + 1)
                    dve.wait_ge(sem(f"sel_ready{l}"), p + 1)
                    v.tensor_tensor(selw[:, :, :, :], sel[:, :, :, :], of_pair(w_of, p), ALU.mult)\
                        .then_inc(sem(f"selw_ready{l}"), 1)
                    dve.wait_ge(sem(f"selw_ready{l}"), p + 1)
                    select(p + 1)
                    dve.wait_ge(sem(f"silu_done{l}"), p + 1)
                    v.tensor_tensor(hh[:, :], sg[:, :], bank[5][:, FE:2 * FE], ALU.mult).then_inc(sem(f"hh_ready{l}"), 1)
                    dve.wait_ge(sem(f"hhT_done{l}"), p + 1)
                    v.tensor_copy(flat(hhT[:, :, :]), bank[6][:, 0:FE]).then_inc(sem(f"hhT_sb{l}"), 1)
                    dve.wait_ge(sem(f"stT_done{l}"), p + 1)
                    v.tensor_copy(st[:, :], bank[5][:, 0:N]).then_inc(sem(f"st_ready{l}"), 1)
                    dve.wait_ge(sem(f"down_done{l}"), 2 * p + 2)
                    v.tensor_copy(y_sb[:, 512:1024], bank[7][:, :]).then_inc(sem(f"y_dve{l}"), 1)
                dve.wait_ge(sem("routed"), l + 1)
                for ti in range(NT):
                    for half in range(2):
                        c = slice(half * 512, (half + 1) * 512)
                        link(V, v.tensor_tensor(junk[:, c], bank[2 * ti + half][:, :], gate[:, 1, c], ALU.mult))
                        ins = v.tensor_tensor(x[:, ti, c], x[:, ti, c], junk[:, c], ALU.add)
                ins.then_inc(sem("x_new"), 1)
                dve.wait_ge(sem("x_new"), 2 * l + 2)

            gates(0)
            norm(0, ((0, 0, hT),))
            v.tensor_scalar(negrel[:, 0:P], pos_kf[:, 0:P], pos_qf[:, 0:1], None, ALU.subtract)
            link(V, v.tensor_scalar(negrel[:, P:SC], pos_kf[:, :], pos_qf[:, 1:2], None, ALU.subtract))
            for c in range(12):
                if c < 8:
                    dve.wait_ge(sem("sq"), c + 1)
                    v.tensor_reduce(ssq[:, c, :], sq[:, c % 2, :].rearrange("p (g d) -> p g d", d=HD), AX_X, ALU.add)\
                        .then_inc(sem("ssq"), 1)
                    dve.wait_ge(sem("srt"), c + 1)
                    link(V, v.reciprocal(srs[:, c, :], srt[:, c, :]))
                    if c >= 3:
                        dve.wait_ge(sem("qkT_ps"), c - 2)
                    v.tensor_tensor(qkn[:, c % 3, :].rearrange("p (g d) -> p g d", d=HD),
                                    bank[c % 4][:, :].rearrange("p (g d) -> p g d", d=HD),
                                    srs[:, c, :].unsqueeze(2).broadcast_to([P, 8, HD]), ALU.mult).then_inc(sem("qkv_sb"), 1)
                else:
                    after(("qkv", 0, c))
                    v.tensor_copy(v_sb[:, :, (c - 8) * N:(c - 7) * N], bank[c % 4][:, :].rearrange("p (t n) -> p t n", t=NT))\
                        .then_inc(sem("qkv_sb"), 1)
            attention(0)
            norm(1, ((1, 24, hT),))
            experts(0)

            gates(1)
            for ti in range(NT):
                link(V, v.tensor_scalar(ang[:, 0, ti, :], const("inv"), pos_qf[:, ti:ti + 1], None, ALU.mult))
            a0, a1, a2, a3 = (flat(ang[:, n, :, :]) for n in range(4))
            magic = float(3 << 22)
            link(V, v.tensor_scalar(a1, a0, float(1 / (2 * np.pi)), magic, ALU.mult, ALU.add))
            link(V, v.tensor_scalar(a1, a1, -magic, None, ALU.add))
            link(V, v.scalar_tensor_tensor(out=a2, in0=a1, scalar=-6.28125, in1=a0, op0=ALU.mult, op1=ALU.add))
            link(V, v.scalar_tensor_tensor(out=a2, in0=a1, scalar=-float(2 * np.pi - 6.28125), in1=a2, op0=ALU.mult, op1=ALU.add))
            link(V, v.tensor_scalar(a2, a2, PI, -PI, ALU.min, ALU.max))
            link(V, v.scalar_tensor_tensor(out=a3, in0=a2, scalar=-1.0, in1=a2, op0=ALU.mult, op1=ALU.max))
            v.tensor_scalar(a3, a3, -1.0, float(np.pi / 2), ALU.mult, ALU.add).then_inc(sem("angles"), 1)
            norm(2, ((2, 48, hT), (4, 96, hkvT)))
            after(("kvd", 1, 0))
            link(V, v.tensor_copy(flat(lat_kv[:, :, :]), bank[4][:, :]))
            after(("kvd", 1, 1))
            v.tensor_copy(flat(kpe[:, :, :]), bank[5][:, 0:NT * ROPE]).then_inc(sem("lat_raw"), 1)
            after(("dq", 1, 1))
            link(V, v.tensor_copy(lat_q[:, :, 0:256], bank[6][:, :].rearrange("p (t n) -> p t n", t=NT)))
            v.tensor_copy(lat_q[:, :, 256:QR], bank[7][:, 0:2 * (QR - 256)].rearrange("p (t n) -> p t n", t=NT))\
                .then_inc(sem("lat_raw"), 1)
            for n, (lat, s0) in enumerate(((lat_kv, 14), (lat_q, 16))):
                dve.wait_ge(sem("lat_rt"), n + 1)
                link(V, v.reciprocal(small[:, s0 + 4:s0 + 6], small[:, s0:s0 + 2]))
                for ti in range(NT):
                    last = v.tensor_scalar(lat[:, ti, :], lat[:, ti, :], small[:, s0 + 4 + ti:s0 + 5 + ti], None, ALU.mult)
                last.then_inc(sem("lat_n"), 1)
            dve.wait_ge(sem("sines"), 1)
            sin, cos = ang[:, 4, :, :], ang[:, 5, :, :]
            half_r = ROPE // 2

            def rotate(a, b, s, c, shape):
                r = [rt[:, n, 0:int(np.prod(shape[1:]))].rearrange("p (a b) -> p a b", b=half_r) for n in range(4)]
                for n, (m, f) in enumerate(((a, c), (b, s), (a, s), (b, c))):
                    last = v.tensor_tensor(r[n], m, f, ALU.mult)
                link(V, last)
                v.tensor_tensor(a, r[0], r[1], ALU.subtract)
                link(V, v.tensor_tensor(b, r[2], r[3], ALU.add))

            dve.wait_ge(sem("lat_rt"), 1)
            link(V, v.tensor_tensor(kpe[:, :, :], kpe[:, :, :], ropeg[:, 1:2, :].broadcast_to([P, NT, ROPE]), ALU.mult))
            rotate(kpe[:, :, 0:half_r], kpe[:, :, half_r:ROPE], sin, cos, [P, NT, half_r])
            after(("uk", 1, 0))
            for ti in range(NT):
                v.tensor_copy(k_sb[:, ti, 0:8, 0:HD], bank[4 + 2 * ti][:, :].rearrange("p (h d) -> p h d", d=HD))\
                    .then_inc(sem("up_dve"), 1)
            after(("uv", 1, 0))
            for ti in range(NT):
                v.tensor_copy(v_sb[:, ti, 0:512], bank[2 * ti][:, :]).then_inc(sem("up_dve"), 1)
            for j, b in enumerate((4, 6, 0)):
                after(("uq", 1, j))
                v.tensor_copy(q_flat(0)[:, j * 512:(j + 1) * 512], bank[b][:, :]).then_inc(sem("up_dve"), 1)
            dve.wait_ge(sem("up_act"), 7)
            dve.wait_ge(sem("up_dve"), 7)
            wide = flat(xn[:, :, :])
            for ti in range(NT):
                for row, m, n in ((0, q_sb[:, ti, :, :], QK), (1, k_sb[:, ti, :, 0:HD], HD)):
                    w3 = wide[:, 0:H * n].rearrange("p (h d) -> p h d", d=n)
                    link(V, v.tensor_tensor(w3, m, m, ALU.mult))
                    link(V, v.tensor_reduce(hs_rs[:, row, ti, :], w3, AX_X, ALU.add))
                last = v.tensor_scalar(hs_rs[:, 1, ti, :], hs_rs[:, 1, ti, :], small[:, 12 + ti:13 + ti], None, ALU.add)
            last.then_inc(sem("qk_ss"), 1)
            for ti in range(NT):
                pe_part = q_sb[:, ti, :, HD:QK]
                link(V, v.tensor_tensor(pe_part, pe_part, ropeg[:, 0:1, :].broadcast_to([P, H, ROPE]), ALU.mult))
                rotate(q_sb[:, ti, :, HD:HD + half_r], q_sb[:, ti, :, HD + half_r:QK],
                       sin[:, ti:ti + 1, :].broadcast_to([P, H, half_r]), cos[:, ti:ti + 1, :].broadcast_to([P, H, half_r]),
                       [P, H, half_r])
            dve.wait_ge(sem("qk_rt"), 1)
            link(V, v.reciprocal(hs_rs[:, 4:6, :, :].rearrange("p a b c -> p (a b c)"),
                                 hs_rs[:, 2:4, :, :].rearrange("p a b c -> p (a b c)")))
            for ti in range(NT):
                v.tensor_tensor(q_sb[:, ti, :, :], q_sb[:, ti, :, :], hs_rs[:, 4, ti, :].unsqueeze(2).broadcast_to([P, H, QK]), ALU.mult)
                kn = k_sb[:, ti, :, 0:HD]
                v.tensor_tensor(kn, kn, hs_rs[:, 5, ti, :].unsqueeze(2).broadcast_to([P, H, HD]), ALU.mult)
                last = v.tensor_tensor(k_sb[:, ti, :, HD:QK], kpe[:, ti:ti + 1, :].broadcast_to([P, H, ROPE]),
                                       hs_rs[:, 5, ti, :].unsqueeze(2).broadcast_to([P, H, ROPE]), ALU.mult)
            last.then_inc(sem("qk_norm"), 1)
            for g in range(8):
                dve.wait_ge(sem("mT_ps"), 2 * g + 2)
                v.tensor_copy(flat(kT[0:QK, 2 * g:2 * g + 2, :]), bank[2 + g % 2][0:QK, :]).then_inc(sem("mT_dve"), 1)
            attention(1)
            norm(3, ((3, 72, hT),))
            experts(1)

        @block.gpsimd
        def _(pool):
            nc.gpsimd.memset(rows_b[:, :], 0.0).then_inc(sem("rows_zero"), 1)


_INS = ["x", "c", "pos", "ada_w", "ada_b", "norm1_g", "norm2_g", "a_w_qkv", "a_q_norm", "a_k_norm", "a_w_o", "kv_ada_w",
        "kv_ada_b", "kv_norm_g", "kv_w_down", "kv_latent_norm", "kv_w_uk", "kv_w_uv", "kv_k_norm", "b_w_dq",
        "b_q_latent_norm", "b_w_uq", "b_q_norm", "b_w_o", "moe_w_router", "moe_router_bias", "moe_w_gate_up",
        "moe_w_down", "moe_shared_gate_up", "moe_shared_down"]


def kernel(**inputs):
    import concourse.bacc as _bacc
    from concourse.bass_utils import run_bass_kernel_spmd as _run

    nc = _bacc.Bacc("TRN2", target_bir_lowering=False, num_devices=1)
    arrays, tensors = {}, {}
    for name in _INS + ["consts"]:
        a = np.ascontiguousarray(constants() if name == "consts" else inputs[name])
        arrays[f"in_{name}"] = a
        tensors[name] = nc.dram_tensor(f"in_{name}", a.shape, mybir.dt.from_np(a.dtype), kind="ExternalInput").ap()
    out = nc.dram_tensor("out", (1, N, D), F32, kind="ExternalOutput").ap()
    build(nc, tensors, out)
    r = _run(nc, [arrays], core_ids=[0])
    return r.results[0]["out"]
```

```python
from contextlib import ExitStack

import numpy as np

import concourse.bass as bass
from concourse import mybir

P = 128
F32 = mybir.dt.float32
F32R = mybir.dt.float32r
I32 = mybir.dt.int32
ALU = mybir.AluOpType
ACT = mybir.ActivationFunctionType
AX_X = mybir.AxisListType.X

N = 256
NT = N // P
D = 1024
KT = D // P
H = 16
HD = 64
QR = 384
KVR = 256
ROPE = 32
QK = HD + ROPE
E = 64
G = 8
TOPG = 4
TOPK = 6
FE = 256
ROUTED_SCALE = 2.5
THETA = 10000.0
EPS = 1e-6
C = 64
FIRST_ADA = 8
OVER = 24
ITEMS = E + OVER
ADA_COL = 256
MASKED = -1e30
PI = float(np.float32(3.1415925))

RING = 5
CH = 2048
SC = 3 * P

CO, _at = {}, 0
for _name, _n in (("ident", P), ("tri", P), ("ones", P), ("logcount", SC), ("causal", SC), ("slot1", C),
                  ("iota", OVER), ("inv", ROPE // 2), ("row", 1), ("eps", 1), ("halfpi", 1)):
    CO[_name] = (_at, _at + _n)
    _at += _n
NCONST = _at

VR, _at = {}, 0
for _name, _n in (("ada_b", 96), ("norm1_g", 16), ("norm2_g", 16), ("kv_ada_b", 16), ("kv_norm_g", 8),
                  ("c", 8), ("b_q_latent_norm", 3), ("kv_latent_norm", 2), ("a_q_norm", 1),
                  ("a_k_norm", 1), ("b_q_norm", 1), ("kv_k_norm", 1)):
    VR[_name] = (_at, _at + _n)
    _at += _n
NROWS = _at
NROWS_B = NROWS - P


def constants():
    c = np.zeros((P, NCONST), np.float32)
    q = np.arange(P)[:, None]
    k = np.arange(P)[None, :]

    def put(name, value):
        c[:, CO[name][0]:CO[name][1]] = value

    put("ident", q == k)
    put("tri", q < k)
    put("ones", 1.0)
    dist = np.concatenate([q - k, q + P - k, q - k], axis=1)
    seen = (dist <= 128).astype(np.int64) + (dist % 4 == 0) + (dist % 16 == 0)
    put("logcount", np.where((dist >= 0) & (seen > 0), np.log(np.maximum(seen, 1)), MASKED))
    put("causal", np.where(dist >= 0, 0.0, MASKED))
    put("slot1", np.arange(1, C + 1)[None, :])
    put("iota", np.arange(OVER)[None, :])
    put("inv", np.power(np.float32(THETA), -np.arange(ROPE // 2, dtype=np.float32) / (ROPE // 2))[None, :])
    put("row", q)
    put("eps", EPS)
    put("halfpi", np.pi / 2)
    return c


def build(nc: bass.Bass, t: dict, out: bass.AP):
    with ExitStack() as ctx:
        sems = {}

        def sem(name):
            if name not in sems:
                sems[name] = ctx.enter_context(nc.semaphore(name))
            return sems[name]

        def sb(name, shape, dt=F32, scope=ctx):
            return scope.enter_context(nc.sbuf_tensor(name, shape, dt))

        bank = [ctx.enter_context(nc.psum_tensor(f"bank{i}", [P, 512], F32)) for i in range(8)]

        x = sb("x", [P, NT, D])
        xn = sb("xn", [P, NT, D])
        hT = sb("hT", [P, KT, N])
        gate = sb("gate", [P, 2, D])
        ring = sb("ring", [P, RING, CH])
        w_gu = [sb(f"w_gu{u}", [P, KT, 2 * FE]) for u in range(2)]
        w_dn = [sb(f"w_dn{u}", [P, FE // P, D]) for u in range(2)]
        w_router = sb("w_router", [P, 2, KT, E])
        cst = sb("cst", [P, NCONST])
        vcol = sb("vcol", [P, NROWS])
        bias_row = sb("bias_row", [P, 2, E])
        ropeg = sb("ropeg", [P, 2, ROPE])
        pos_q = sb("pos_q", [P, NT], I32)
        pos_qf = sb("pos_qf", [P, NT])
        csilu = sb("csilu", [P, KT])
        ada_row = sb("ada_row", [P, 256])
        mod = sb("mod", [P, 2 * 48 + 16])
        amp = sb("amp", [P, 5, KT])
        qk_gain = sb("qk_gain", [P, 2])
        small = sb("small", [P, 64])
        eps_c = cst[:, CO["eps"][0]:CO["eps"][1]]

        def const(name, rows=P):
            return cst[0:rows, CO[name][0]:CO[name][1]]

        def col(name, i=0, n=1, rows=P):
            return vcol[0:rows, VR[name][0] + i:VR[name][0] + i + n]

        with ExitStack() as early:
            rows_a = sb("rows_a", [P, P], scope=early)
            rows_b = sb("rows_b", [P, P], scope=early)
            diag = sb("diag", [P, KT, P], scope=early)
            pos_k = sb("pos_k", [P, N], I32, scope=early)
            pos_kf = sb("pos_kf", [P, N], scope=early)
        with ExitStack() as att:
            qT = sb("qT", [P, H, N], scope=att)
            kT = sb("kT", [P, H, N], scope=att)
            v_sb = sb("v_sb", [P, NT, D], scope=att)
            negrel = sb("negrel", [P, SC], scope=att)
            smax = sb("smax", [P, H, NT], scope=att)
            nmax = sb("nmax", [P, H, NT], scope=att)
            lsum = sb("lsum", [P, H, NT], scope=att)
            rsum = sb("rsum", [P, H, NT], scope=att)
            with ExitStack() as first:
                qkn = sb("qkn", [P, 3, NT * N], scope=first)
                sq = sb("sq", [P, 2, NT * N], scope=first)
                ssq = sb("ssq", [P, 8, 8], scope=first)
                srt = sb("srt", [P, 8, 8], scope=first)
                srs = sb("srs", [P, 8, 8], scope=first)
            with ExitStack() as heads:
                s_sb = sb("s_sb", [P, 4, SC], scope=heads)
                p_sb = sb("p_sb", [P, 4, SC], scope=heads)
                pT_sb = sb("pT_sb", [P, 4, SC], scope=heads)
            with ExitStack() as second:
                q_sb = sb("q_sb", [P, NT, H, QK], scope=second)
                k_sb = sb("k_sb", [P, NT, H, QK], scope=second)
                kpe = sb("kpe", [P, NT, ROPE], scope=second)
                flat_kT = kT[:, :, :].rearrange("p h n -> p (h n)")
                at = [0]

                def in_kT(*shape):
                    n = int(np.prod(shape))
                    v = flat_kT[:, at[0]:at[0] + n]
                    at[0] += n
                    names = "abcd"[:len(shape)]
                    return v.rearrange(f"p ({' '.join(names)}) -> p {' '.join(names)}", **dict(zip(names, shape)))

                lat_kv = in_kT(NT, KVR)
                lat_q = in_kT(NT, QR)
                lat_kvT = in_kT(KVR // P, N)
                lat_qT = in_kT(QR // P, N)
                rt = in_kT(4, 256)
                ang = in_kT(6, NT, ROPE // 2)
                hs_rs = in_kT(6, NT, H)
            hkvT = qT[:, 0:8, :]
        with ExitStack() as moe:
            h_tok = sb("h_tok", [P, NT, D], scope=moe)
            y_hi = sb("y_hi", [P, D], F32R, scope=moe)
            y_lo = sb("y_lo", [P, D], F32R, scope=moe)
            st = sb("st", [P, N], F32R, scope=moe)
            w_slot = sb("w_slot", [P, 1], scope=moe)
            sel = sb("sel", [P, NT, 2, C], scope=moe)
            selw = sb("selw", [P, NT, 2, C], scope=moe)
            xg = sb("xg", [P, KT, 2 * C], scope=moe)
            sg = sb("sg", [P, FE], scope=moe)
            hh = sb("hh", [P, FE], scope=moe)
            hhT = sb("hhT", [P, FE // P, 2 * C], scope=moe)
            sh_g = sb("sh_g", [P, FE // P, N], scope=moe)
            sh_h = sb("sh_h", [P, FE // P, N], scope=moe)
            slot_of = sb("slot_of", [P, NT, ITEMS + 2], scope=moe)
            w_of = sb("w_of", [P, NT, ITEMS + 2], scope=moe)
            score = sb("score", [P, NT, E], scope=moe)
            choice = sb("choice", [P, NT, E + 2], scope=moe)
            left = sb("left", [P, NT, E + 2], scope=moe)
            chosen = sb("chosen", [P, NT, E], scope=moe)
            gsort = sb("gsort", [P, NT, G, 8], scope=moe)
            gsc = sb("gsc", [P, NT, G + TOPG], scope=moe)
            gleft = sb("gleft", [P, NT, G + TOPG], scope=moe)
            gtop = sb("gtop", [P, NT, 8], scope=moe)
            gmask = sb("gmask", [P, NT, G], scope=moe)
            etop = sb("etop", [P, NT, 8], scope=moe)
            rden = sb("rden", [P, NT], scope=moe)
            rtT = sb("rtT", [E, 2, N], scope=moe)
            count = sb("count", [E, 4], scope=moe)
            flag = sb("flag", [E, 4], scope=moe)
            place = sb("place", [E, 4], scope=moe)
            onehot = sb("onehot", [E, 5, OVER], scope=moe)
            tab_f = sb("tab_f", [1, OVER + 1], scope=moe)
            tab_i = sb("tab_i", [1, OVER + 2], I32, scope=moe)
        junk = sb("junk", [P, D])

        def q_flat(ti):
            return q_sb[:, ti, :, :].rearrange("p h d -> p (h d)")

        def rows_loads():
            loads = []
            for name in ("ada_b", "norm1_g", "norm2_g", "kv_ada_b", "kv_norm_g", "c", "b_q_latent_norm", "kv_latent_norm"):
                r0, r1 = VR[name]
                src = t[name]
                if len(src.shape) == 2:
                    src = src.rearrange("l (k p) -> (l k) p", p=P)
                else:
                    src = src.rearrange("(k p) -> k p", p=P)
                tile, off = (rows_a, 0) if r0 < P else (rows_b, P)
                loads.append((tile[r0 - off:r1 - off, :], src))
            for name, n, reps in (("a_q_norm", HD, 2), ("a_k_norm", HD, 2), ("b_q_norm", QK, 1), ("kv_k_norm", QK, 1)):
                src = t[name] if len(t[name].shape) == 2 else t[name].rearrange("(a n) -> a n", a=1)
                r = VR[name][0] - P
                for rep in range(reps):
                    loads.append((rows_b[r:r + 1, rep * n:rep * n + n], src))
            return loads

        ROWS_IN = 16 * len(rows_loads())

        chunks = []

        def chunk(name, src, k, n):
            chunks.append((name, src, k, n))

        def by_rows(w):
            return w.rearrange("(k p) n -> p k n", p=P)

        def ada_chunk(n):
            src, j = (t["ada_w"][n // 24], n % 24) if n < 48 else (t["kv_ada_w"], n - 48)
            chunk(("ada", n), by_rows(src)[:, :, j * 256:(j + 1) * 256], KT, 256)

        ada_by_qkv = [[FIRST_ADA + 2 * c, FIRST_ADA + 2 * c + 1] for c in range(12)]
        at_head = FIRST_ADA + 24
        ada_by_pair = [[at_head + 3 * g + m for m in range(3)] for g in range(H // 2)]
        for n in range(FIRST_ADA):
            ada_chunk(n)
        for j in range(12):
            chunk(("qkv", 0, j), by_rows(t["a_w_qkv"][0])[:, :, j * 256:(j + 1) * 256], KT, 256)
            for n in ada_by_qkv[j]:
                ada_chunk(n)
        for g in range(H // 2):
            for n in ada_by_pair[g]:
                ada_chunk(n)
        for l in range(2):
            if l == 1:
                kvd = by_rows(t["kv_w_down"])
                chunk(("kvd", 1, 0), kvd[:, :, 0:KVR], KT, KVR)
                chunk(("kvd", 1, 1), kvd[:, :, KVR:KVR + ROPE], KT, ROPE)
                dq = by_rows(t["b_w_dq"][0])
                chunk(("dq", 1, 0), dq[:, :, 0:256], KT, 256)
                chunk(("dq", 1, 1), dq[:, :, 256:QR], KT, QR - 256)
                chunk(("uk", 1, 0), by_rows(t["kv_w_uk"]), 2, D)
                chunk(("uv", 1, 0), by_rows(t["kv_w_uv"]), 2, D)
                for j in range(3):
                    chunk(("uq", 1, j), by_rows(t["b_w_uq"][0])[:, :, j * 512:(j + 1) * 512], 3, 512)
            wo = by_rows(t["a_w_o"][0] if l == 0 else t["b_w_o"][0])
            for j in range(4):
                chunk(("wo", l, j), wo[:, :, j * 256:(j + 1) * 256], KT, 256)
            sgu = by_rows(t["moe_shared_gate_up"][l])
            for j in range(2):
                chunk(("sgu", l, j), sgu[:, :, j * 256:(j + 1) * 256], KT, 256)
            chunk(("sdn", l, 0), by_rows(t["moe_shared_down"][l]), 2, D)
        number = {c[0]: i for i, c in enumerate(chunks)}

        def slot(name):
            i = number[name]
            _, _, k, n = chunks[i]
            return ring[:, i % RING, 0:k * n].rearrange("p (k n) -> p k n", k=k)

        def link(eng, ins):
            s = sem("chain_" + eng[0])
            eng[1] += 1
            ins.then_inc(s, 1)
            eng[2].wait_ge(s, eng[1])

        block = ctx.enter_context(nc.Block())

        @block.sync
        def _(sp):
            def load_chunks(names):
                for name in names:
                    i = number[name]
                    _, src, k, n = chunks[i]
                    if i >= RING:
                        sp.wait_ge(sem("chunk_used"), i - RING + 1)
                    sp.dma_start(slot(name), src).then_inc(sem(f"chunk_in{i % RING}"), 16)

            def expert_pair(l, i, e0, e1, first):
                for half in range(2):
                    if not first:
                        sp.wait_ge(sem(f"gu_done{l}"), 2 * i + half - 1)
                    for u, e in ((0, e0), (1, e1)):
                        ks = slice(half * KT // 2, (half + 1) * KT // 2)
                        sp.dma_start(w_gu[u][:, ks, :], gu_src[l](e)[:, ks, :]).then_inc(sem(f"gu_in{l}{half}"), 16)
                for u, e in ((0, e0), (1, e1)):
                    if not first:
                        sp.wait_ge(sem(f"down_done{l}"), 2 * i + u - 1)
                    sp.dma_start(w_dn[u][:, :, :], dn_src[l](e)).then_inc(sem(f"dn_in{l}{u}"), 16)

            gu_all = t["moe_w_gate_up"].rearrange("l e (k p) n -> l p e k n", p=P)
            dn_all = t["moe_w_down"].rearrange("l e (k p) n -> l p e k n", p=P)
            gu_src = [lambda e, l=l: gu_all[l][:, bass.ds(e, 1), :, :].rearrange("p e k n -> p (e k) n") for l in range(2)]
            dn_src = [lambda e, l=l: dn_all[l][:, bass.ds(e, 1), :, :].rearrange("p e k n -> p (e k) n") for l in range(2)]

            order = [c[0] for c in chunks]
            cut = [number[("sdn", 0, 0)] + 1, len(order)]
            done = 0
            for l in range(2):
                before_wo = number[("wo", l, 0)]
                if l == 0:
                    load_chunks(order[0:before_wo])
                    done = before_wo
                else:
                    sp.wait_ge(sem("x_new"), 2)
                expert_pair(l, 0, 0, 1, True)
                load_chunks(order[done:cut[l]])
                done = cut[l]
                if l == 0:
                    ahead = order[done:done + RING]
                with sp.Fori(1, E // 2) as i:
                    expert_pair(l, i, 2 * i, 2 * i + 1, False)
                sp.wait_ge(sem("table"), l + 1)
                trips = sp.value_load(tab_i[0:1, OVER:OVER + 1], min_val=E // 2, max_val=ITEMS // 2)
                with sp.If(trips > E // 2):
                    with sp.Fori(E // 2, trips) as i:
                        e0 = sp.value_load(tab_i[0:1, bass.ds(2 * i - E, 1)], min_val=0, max_val=E - 1)
                        e1 = sp.value_load(tab_i[0:1, bass.ds(2 * i - E + 1, 1)], min_val=0, max_val=E - 1)
                        expert_pair(l, i, e0, e1, False)
                if l == 0:
                    load_chunks(ahead)
                    done += RING
            sp.wait_ge(sem("x_new"), 4)
            sp.dma_start(out.rearrange("b (t p) d -> p (b t) d", p=P), x[:, :, :]).then_inc(sem("stored"), 16)
            sp.wait_ge(sem("stored"), 16)

        @block.tensor
        def _(pe):
            def use(name):
                i = number[name]
                pe.wait_ge(sem(f"chunk_in{i % RING}"), 16 * (i // RING + 1))
                return slot(name)

            def used(ins):
                ins.then_inc(sem("chunk_used"), 1)

            def mm(o, a, b, first, last):
                return nc.tensor.matmul(o, a, b, start=first, stop=last)

            def tr(o, a, rows=P):
                return nc.tensor.transpose(o, a, const("ident")[0:rows, 0:rows])

            def norm_transposes(n):
                pe.wait_ge(sem("xn_ready"), 2 * n + 2)
                for j in range(4):
                    for kk in range(2):
                        for ti in range(NT):
                            k = 2 * j + kk
                            last = tr(bank[j][:, kk * N + ti * P:kk * N + (ti + 1) * P], xn[:, ti, k * P:(k + 1) * P])
                    last.then_inc(sem("xT_ps"), 1)
                pe.wait_ge(sem("hT_dve"), 2 * (n + 1))
                pe.wait_ge(sem("hT_act"), 2 * (n + 1))

            ada_next = [0]

            def ada_columns():
                n = ada_next[0]
                pe.wait_ge(sem("row_sb"), n)
                for m in range(2):
                    c = ADA_COL + 2 * (n - 1) + m
                    last = mm(bank[7][:, c:c + 1], ada_row[:, m * P:(m + 1) * P], const("ones")[:, 0:1], True, True)
                return last

            def ada_step():
                if ada_next[0]:
                    ada_columns()
                w = use(("ada", ada_next[0]))
                for k in range(KT):
                    r = 32 * (k % 4)
                    last = mm(bank[7][r:r + 1, 0:256], csilu[:, k:k + 1], w[:, k, :], k < 4, k >= 4)
                used(last)
                ada_next[0] += 1

            def gates(l):
                for g in range(2):
                    pe.wait_ge(sem("diag"), 2 * l + g + 1)
                    for half in range(2):
                        b = bank[half]
                        mm(b[:, :], const("ones"), diag[:, 4 * half:4 * half + 4, :].rearrange("p k n -> p (k n)"), True, True)\
                            .then_inc(sem("gate_ps"), 1)
                    pe.wait_ge(sem("gate_sb"), 2 * (2 * l + g) + 2)

            def attention(l, q_of, k_of):
                heads, pairs = H * l, H // 2 * l

                def scores(g):
                    if g >= 2:
                        pe.wait_ge(sem("s_ready"), heads + 2 * g - 2)
                    for c0, c1, kn in ((0, P, P), (P, SC, N)):
                        for h in (2 * g, 2 * g + 1):
                            last = mm(bank[h % 4][:, c0:c1], q_of(h)[:, c0:c0 + P], k_of(h)[:, 0:kn], True, True)
                    last.then_inc(sem("s_ps"), 1)

                def p_transposes(h):
                    pe.wait_ge(sem("p_norm"), heads + h + 1)
                    if h >= 2:
                        pe.wait_ge(sem("pT_sb"), heads + h - 1)
                    for c in range(3):
                        last = tr(bank[4 + h % 2][:, c * P:(c + 1) * P], p_sb[:, h % 4, c * P:(c + 1) * P])
                    last.then_inc(sem("pT_ps"), 1)

                def values(g):
                    pe.wait_ge(sem("pT_sb"), heads + 2 * g + 2)
                    if g >= 1:
                        pe.wait_ge(sem("o_sb"), pairs + g)
                    for q, c, ti in ((0, 0, 0), (1, 1, 0), (1, 2, 1)):
                        for u, h in enumerate((2 * g, 2 * g + 1)):
                            last = mm(bank[6][u * HD:(u + 1) * HD, q * P:(q + 1) * P], v_sb[:, ti, h * HD:(h + 1) * HD],
                                      pT_sb[:, h % 4, c * P:(c + 1) * P], c < 2, c != 1)
                    last.then_inc(sem("o_ps"), 1)

                for g in range(H // 2 + 2):
                    if g < H // 2:
                        scores(g)
                        if l == 0:
                            for _ in ada_by_pair[g]:
                                ada_step()
                            if g == H // 2 - 1:
                                ada_columns().then_inc(sem("ada_ps"), 1)
                    if 1 <= g <= H // 2:
                        p_transposes(2 * g - 2)
                        p_transposes(2 * g - 1)
                    if g >= 2:
                        values(g - 2)
                gates(l)
                pe.wait_ge(sem("o_sb"), pairs + H // 2)
                for c in range(4):
                    w = use(("wo", l, c))
                    for ti in range(NT):
                        for k in range(KT):
                            last = mm(bank[4 + c][:, ti * N:(ti + 1) * N], hT[:, k, ti * P:(ti + 1) * P], w[:, k, :],
                                      k == 0, k == KT - 1)
                    used(last)

            def experts(l):
                for ti in range(NT):
                    for k in range(KT):
                        last = mm(bank[4][:, ti * E:(ti + 1) * E], hT[:, k, ti * P:(ti + 1) * P], w_router[:, l, k, :],
                                  k == 0, k == KT - 1)
                last.then_inc(sem("logits"), 1)
                for j in range(4):
                    ti, half = j // 2, j % 2
                    for k in range(4):
                        last = tr(bank[j][:, k * P:(k + 1) * P], hT[:, 4 * half + k, ti * P:(ti + 1) * P])
                    last.then_inc(sem("h_ps"), 1)

                def shared_gate_up(j):
                    w = use(("sgu", l, j))
                    for f in range(2):
                        for k in range(KT):
                            last = mm(bank[6 + j][:, f * N:(f + 1) * N], w[:, k, f * P:(f + 1) * P], hT[:, k, :],
                                      k == 0, k == KT - 1)
                    used(last)

                shared_gate_up(0)
                pe.wait_ge(sem("chosen"), l + 1)
                pe.wait_ge(sem("score"), l + 1)
                mm(bank[4][:, 0:E], const("tri"), chosen[:, 0, :], True, True)
                mm(bank[4][:, E:2 * E], const("ones"), chosen[:, 0, :], True, False)
                mm(bank[4][:, E:2 * E], const("tri"), chosen[:, 1, :], False, True).then_inc(sem("ranks"), 1)
                for ti in range(NT):
                    last = mm(bank[5][0:E, 0:1], chosen[:, ti, :], const("ones")[:, 0:1], ti == 0, ti == NT - 1)
                last.then_inc(sem("counts"), 1)
                shared_gate_up(1)
                pe.wait_ge(sem("flags"), l + 1)
                mm(bank[5][0:E, 4:7], const("tri")[0:E, 0:E], flag[:, 0:3], True, False)
                mm(bank[5][0:E, 5:7], const("ones")[0:E, 0:E], flag[:, 0:2], False, False)
                mm(bank[5][0:E, 6:7], const("ones")[0:E, 0:E], flag[:, 0:1], False, True)
                mm(bank[5][0:1, 8:9], flag[:, 3:4], const("ones")[0:E, 0:1], True, True).then_inc(sem("places"), 1)
                pe.wait_ge(sem("slots"), l + 1)
                pe.wait_ge(sem("sh_g"), l + 1)
                for ti in range(NT):
                    tr(bank[6][0:E, ti * P:(ti + 1) * P], slot_of[:, ti, 0:E])
                for ti in range(NT):
                    last = tr(bank[6][0:E, N + ti * P:N + (ti + 1) * P], w_of[:, ti, 0:E])
                last.then_inc(sem("tabT_ps"), 1)
                pe.wait_ge(sem("sh_h"), l + 1)
                pe.wait_ge(sem("tabT"), l + 1)
                pe.wait_ge(sem("onehot"), l + 1)
                for ti in range(NT):
                    o = bank[7][:, ti * OVER:(ti + 1) * OVER]
                    for c in range(3):
                        mm(o, rtT[:, 0, ti * P:(ti + 1) * P], onehot[:, c, :], c == 0, False)
                    mm(o, const("ones")[0:E, :], onehot[:, 3, :], False, True)
                for ti in range(NT):
                    mm(bank[7][:, 64 + ti * OVER:64 + (ti + 1) * OVER], rtT[:, 1, ti * P:(ti + 1) * P], onehot[:, 4, :],
                       True, True)
                mm(bank[7][0:1, 128:128 + OVER], const("row")[0:E, :], onehot[:, 4, :], True, True)\
                    .then_inc(sem("over_ps"), 1)
                w = use(("sdn", l, 0))
                pe.wait_ge(sem("h_act"), 2 * l + 2)
                pe.wait_ge(sem("h_dve"), 2 * l + 2)
                for ti in range(NT):
                    for half in range(2):
                        for f in range(2):
                            last = nc.tensor.matmul(bank[2 * ti + half][:, :], sh_h[:, f, ti * P:(ti + 1) * P],
                                                    w[:, f, half * 512:(half + 1) * 512], start=f == 0, stop=False,
                                                    skip_group_check=True)
                used(last)
                pe.wait_ge(sem("table"), l + 1)

                def gate_up(p):
                    pe.wait_ge(sem(f"xg_ready{l}"), p + 1)
                    pe.wait_ge(sem(f"st_ready{l}"), p + 1)
                    for half in range(2):
                        pe.wait_ge(sem(f"gu_in{l}{half}"), 32 * p + 32)
                        for k in range(half * KT // 2, (half + 1) * KT // 2):
                            for u in range(2):
                                last = mm(bank[5][u * C:(u + 1) * C, :], xg[:, k, u * C:(u + 1) * C], w_gu[u][:, k, :],
                                          k == 0, k == KT - 1)
                        last.then_inc(sem(f"gu_done{l}"), 1)

                def scatter(count, stop):
                    pe.wait_ge(sem(f"y_act{l}"), 2 * count)
                    pe.wait_ge(sem(f"y_dve{l}"), count)
                    for ti in range(NT):
                        for half in range(2):
                            for y in (y_hi, y_lo):
                                last = nc.tensor.matmul(bank[2 * ti + half][:, :], st[:, ti * P:(ti + 1) * P],
                                                        y[:, half * 512:(half + 1) * 512], start=False,
                                                        stop=stop and y is y_lo, skip_group_check=True)
                    return last

                def gather(count):
                    pe.wait_ge(sem(f"sel_ready{l}"), count)
                    for k in range(KT):
                        b = bank[4 if k < 4 else 7]
                        for ti in range(NT):
                            last = mm(b[:, (k % 4) * P:(k % 4 + 1) * P], h_tok[:, ti, k * P:(k + 1) * P],
                                      sel[:, ti, :, :].rearrange("p u c -> p (u c)"), ti == 0, ti == NT - 1)
                    last.then_inc(sem(f"gath_done{l}"), 1)

                def middle(p):
                    pe.wait_ge(sem(f"hh_ready{l}"), p + 1)
                    for f in range(2):
                        last = tr(bank[6][:, f * P:(f + 1) * P], hh[:, f * P:(f + 1) * P])
                    last.then_inc(sem(f"hhT_done{l}"), 1)

                def weights_transposed(p):
                    pe.wait_ge(sem(f"selw_ready{l}"), p + 1)
                    for ti in range(NT):
                        last = tr(bank[5][:, ti * P:(ti + 1) * P], selw[:, ti, :, :].rearrange("p u c -> p (u c)"))
                    last.then_inc(sem(f"stT_done{l}"), 1)

                def down(p):
                    pe.wait_ge(sem(f"hhT_sb{l}"), p + 1)
                    for u in range(2):
                        pe.wait_ge(sem(f"dn_in{l}{u}"), 16 * p + 16)
                    for half in range(2):
                        if half == 1:
                            pe.wait_ge(sem(f"xg_ready{l}"), p + 2)
                        for f in range(2):
                            for u in range(2):
                                ins = mm(bank[6 + half][u * C:(u + 1) * C, :], hhT[:, f, u * C:(u + 1) * C],
                                         w_dn[u][:, f, half * 512:(half + 1) * 512], f == 0, f == 1)
                                if half == 1 and f == 1:
                                    ins.then_inc(sem(f"down_done{l}"), 1)

                gather(1)
                trips = pe.value_load(tab_i[0:1, OVER:OVER + 1], min_val=E // 2, max_val=ITEMS // 2)
                with pe.Fori(0, trips) as p:
                    gate_up(p)
                    scatter(p + 1, False)
                    middle(p)
                    gather(p + 2)
                    weights_transposed(p)
                    down(p)
                scatter(trips + 1, True).then_inc(sem("routed"), 1)

            pe.wait_ge(sem("rows_in"), ROWS_IN)
            pe.wait_ge(sem("const_in"), 16)
            tr(bank[7][:, 0:P], rows_a[:, :])
            nc.tensor.transpose(bank[7][:, P:NROWS], rows_b[0:NROWS_B, :], const("ident")[0:NROWS_B, 0:NROWS_B])\
                .then_inc(sem("vcol_ps"), 1)
            pe.wait_ge(sem("csilu"), 1)
            for n in range(FIRST_ADA):
                ada_step()
            ada_columns().then_inc(sem("ada_ps"), 1)
            norm_transposes(0)

            def qk_transposes(c):
                pe.wait_ge(sem("qkv_sb"), c + 1)
                if c >= 2:
                    pe.wait_ge(sem("qkT_sb"), c - 1)
                for b2 in range(2):
                    for ti in range(NT):
                        last = tr(bank[4 + c % 2][:, b2 * N + ti * P:b2 * N + (ti + 1) * P],
                                  qkn[:, c % 3, ti * N + b2 * P:ti * N + (b2 + 1) * P])
                last.then_inc(sem("qkT_ps"), 1)

            for c in range(12):
                w = use(("qkv", 0, c))
                if c >= 4:
                    pe.wait_ge(sem("qkv_sb"), c - 3)
                for ti in range(NT):
                    for k in range(KT):
                        last = mm(bank[c % 4][:, ti * N:(ti + 1) * N], hT[:, k, ti * P:(ti + 1) * P], w[:, k, :],
                                  k == 0, k == KT - 1)
                used(last)
                for _ in ada_by_qkv[c]:
                    ada_step()
                if 2 <= c < 10:
                    qk_transposes(c - 2)
            pe.wait_ge(sem("qkv_sb"), 12)
            pe.wait_ge(sem("qkT_sb"), 8)
            pair = lambda tt: (lambda h: tt[HD * (h % 2):HD * (h % 2) + HD, h // 2, :])
            attention(0, pair(qT), pair(kT))
            norm_transposes(1)
            experts(0)
            norm_transposes(2)
            for i, (name, b, n) in enumerate(((("kvd", 1, 0), 4, KVR), (("kvd", 1, 1), 5, ROPE), (("dq", 1, 0), 6, 256),
                                              (("dq", 1, 1), 7, QR - 256))):
                w = use(name)
                src = hkvT if name[0] == "kvd" else hT
                for ti in range(NT):
                    for k in range(KT):
                        last = mm(bank[b][:, ti * n:(ti + 1) * n], src[:, k, ti * P:(ti + 1) * P], w[:, k, :],
                                  k == 0, k == KT - 1)
                used(last)
            pe.wait_ge(sem("lat_n"), 1)
            for kk in range(2):
                for ti in range(NT):
                    last = tr(bank[0][:, kk * N + ti * P:kk * N + (ti + 1) * P], lat_kv[:, ti, kk * P:(kk + 1) * P])
            last.then_inc(sem("latT_ps"), 1)
            pe.wait_ge(sem("lat_n"), 2)
            for kk in range(3):
                for ti in range(NT):
                    last = tr(bank[1 + kk // 2][:, (kk % 2) * N + ti * P:(kk % 2) * N + (ti + 1) * P],
                              lat_q[:, ti, kk * P:(kk + 1) * P])
            last.then_inc(sem("latT_ps"), 1)
            up = ((("uk", 1, 0), lat_kvT, 2, 4, 0), (("uv", 1, 0), lat_kvT, 2, 0, 0), (("uq", 1, 0), lat_qT, 3, 4, 2),
                  (("uq", 1, 1), lat_qT, 3, 6, 2), (("uq", 1, 2), lat_qT, 3, 0, 4))
            pe.wait_ge(sem("latT_sb"), 1)
            for name, src, kn, b, copied in up:
                w = use(name)
                if name[0] != "uk":
                    pe.wait_ge(sem("latT_sb"), 2)
                if copied:
                    pe.wait_ge(sem("up_dve"), copied)
                    pe.wait_ge(sem("up_act"), copied)
                for ti in range(NT):
                    for half in range(2 if kn == 2 else 1):
                        o = bank[b + (2 * ti + half if kn == 2 else ti)]
                        for k in range(kn):
                            last = mm(o[:, :], src[:, k, ti * P:(ti + 1) * P], w[:, k, half * 512:(half + 1) * 512],
                                      k == 0, k == kn - 1)
                used(last)
            pe.wait_ge(sem("qk_norm"), 1)
            pe.wait_ge(sem("up_act"), 7)
            for g in range(8):
                for side, (src, b) in enumerate(((q_sb, 0), (k_sb, 2))):
                    if g >= 2:
                        pe.wait_ge(sem("mT_act" if side == 0 else "mT_dve"), g - 1)
                    for hh_ in range(2):
                        for ti in range(NT):
                            last = tr(bank[b + g % 2][0:QK, hh_ * N + ti * P:hh_ * N + (ti + 1) * P],
                                      src[:, ti, 2 * g + hh_, :])
                    last.then_inc(sem("mT_ps"), 1)
            pe.wait_ge(sem("mT_act"), 8)
            pe.wait_ge(sem("mT_dve"), 8)
            attention(1, lambda h: qT[0:QK, h, :], lambda h: kT[0:QK, h, :])
            norm_transposes(3)
            experts(1)

        @block.scalar
        def _(act):
            A = ["act", 0, act]

            def after(name):
                act.wait_ge(sem("chunk_used"), number[name] + 1)

            def copy(o, i, **kw):
                return nc.scalar.activation(o, i, ACT.Copy, **kw)

            act.dma_start(x[:, :, :], t["x"].rearrange("b (t p) d -> p (b t) d", p=P)).then_inc(sem("x_in"), 16)
            act.dma_start(cst[:, :], t["consts"]).then_inc(sem("const_in"), 16)
            act.wait_ge(sem("rows_zero"), 1)
            for dst, src in rows_loads():
                act.dma_start(dst, src).then_inc(sem("rows_in"), 16)
            act.dma_start(w_router[:, :, :, :].rearrange("p l k e -> p (l k) e"),
                          t["moe_w_router"].rearrange("l (k p) e -> p (l k) e", p=P)).then_inc(sem("small_in"), 16)
            for l in range(2):
                act.dma_start(bias_row[:, l, :], t["moe_router_bias"][l:l + 1, :].broadcast_to([P, E])).then_inc(sem("small_in"), 16)
            act.dma_start(ropeg[:, 0, :], t["b_q_norm"][0:1, HD:QK].broadcast_to([P, ROPE])).then_inc(sem("small_in"), 16)
            act.dma_start(ropeg[:, 1, :], t["kv_k_norm"].rearrange("(a n) -> a n", a=1)[:, HD:QK].broadcast_to([P, ROPE]))\
               .then_inc(sem("small_in"), 16)
            act.dma_start(pos_k[:, :], t["pos"].broadcast_to([P, N])).then_inc(sem("small_in"), 16)
            act.dma_start(pos_q[:, :], t["pos"].rearrange("b (t p) -> p (b t)", p=P), allow_slow_non_contiguous=True).then_inc(sem("small_in"), 16)

            act.wait_ge(sem("vcol"), 1)
            nc.scalar.activation(csilu[:, :], col("c", 0, 8), ACT.Silu).then_inc(sem("csilu"), 1)

            def ada_rows(n):
                after(("ada", n))
                copy(ada_row[:, :], bank[7][:, 0:256]).then_inc(sem("row_sb"), 1)

            def gates(l):
                for g in range(2):
                    if l == 1 and g == 0:
                        act.wait_ge(sem("x_new"), 2)
                    for half in range(2):
                        act.wait_ge(sem("gate_ps"), 2 * (2 * l + g) + half + 1)
                        copy(gate[:, g, half * 512:(half + 1) * 512], bank[half][:, :]).then_inc(sem("gate_sb"), 1)

            def norm(n, outs):
                if n == 0:
                    act.wait_ge(sem("x_in"), 16)
                else:
                    act.wait_ge(sem("x_new"), n)
                for ti in range(NT):
                    link(A, nc.scalar.activation(junk[:, :], x[:, ti, :], ACT.Square, accum_out=small[:, ti:ti + 1]))
                nc.scalar.activation(small[:, 2:4], small[:, 0:2], ACT.Sqrt, bias=eps_c, scale=1.0 / D)\
                    .then_inc(sem("x_rt"), 1)
                act.wait_ge(sem("amp"), 1 if n == 0 else 2)
                for j in (1, 3):
                    act.wait_ge(sem("xT_ps"), 4 * n + j + 1)
                    for a, s0, dst in outs:
                        for kk in range(2):
                            k = 2 * j + kk
                            last = nc.scalar.activation(dst[:, k, :], bank[j][:, kk * N:(kk + 1) * N], ACT.Identity,
                                                        bias=mod[:, s0 + k:s0 + k + 1], scale=amp[:, a, k:k + 1])
                    last.then_inc(sem("hT_act"), 1)

            def attention(l):
                heads, pairs = H * l, H // 2 * l
                for g in range(H // 2 + 2):
                    if g < H // 2:
                        if l == 0:
                            for n in ada_by_pair[g]:
                                ada_rows(n)
                        for h in (2 * g, 2 * g + 1):
                            act.wait_ge(sem("s_ready"), heads + h + 1)
                            if h >= 4:
                                act.wait_ge(sem("pT_ps"), heads + h - 3)
                            for ti, (c0, c1) in enumerate(((0, P), (P, SC))):
                                last = nc.scalar.activation(p_sb[:, h % 4, c0:c1], s_sb[:, h % 4, c0:c1], ACT.Exp,
                                                            bias=nmax[:, h, ti:ti + 1], accum_out=lsum[:, h, ti:ti + 1])
                            last.then_inc(sem("p_ready"), 1)
                    if 1 <= g <= H // 2:
                        if g >= 3:
                            act.wait_ge(sem("o_ps"), pairs + g - 2)
                        for h in (2 * g - 2, 2 * g - 1):
                            act.wait_ge(sem("pT_ps"), heads + h + 1)
                            copy(pT_sb[:, h % 4, :], bank[4 + h % 2][:, 0:SC]).then_inc(sem("pT_sb"), 1)
                    if g >= 2:
                        act.wait_ge(sem("o_ps"), pairs + g - 1)
                        copy(hT[:, g - 2, :], bank[6][:, 0:N]).then_inc(sem("o_sb"), 1)
                gates(l)

            def experts(l):
                act.wait_ge(sem("logits"), l + 1)
                nc.scalar.activation(score[:, :, :].rearrange("p t e -> p (t e)"), bank[4][:, 0:NT * E], ACT.Sigmoid)\
                    .then_inc(sem("score"), 1)
                for j in (0, 2):
                    act.wait_ge(sem("h_ps"), 4 * l + j + 1)
                    copy(h_tok[:, j // 2, 0:512], bank[j][:, :]).then_inc(sem("h_act"), 1)
                after(("sgu", l, 0))
                nc.scalar.activation(sh_g[:, :, :].rearrange("p f n -> p (f n)"), bank[6][:, :], ACT.Silu)\
                    .then_inc(sem("sh_g"), 1)

                def gathered(count):
                    act.wait_ge(sem(f"gath_done{l}"), count)
                    for b, k in ((7, 4), (4, 0)):
                        last = copy(xg[:, k:k + 4, :].rearrange("p k c -> p (k c)"), bank[b][:, :])
                    last.then_inc(sem(f"xg_ready{l}"), 1)

                act.wait_ge(sem("table"), l + 1)
                gathered(1)
                trips = act.value_load(tab_i[0:1, OVER:OVER + 1], min_val=E // 2, max_val=ITEMS // 2)
                with act.Fori(0, trips) as p:
                    act.wait_ge(sem(f"gu_done{l}"), 2 * p + 2)
                    nc.scalar.activation(sg[:, :], bank[5][:, 0:FE], ACT.Silu).then_inc(sem(f"silu_done{l}"), 1)
                    gathered(p + 2)
                    act.wait_ge(sem(f"st_ready{l}"), p + 2)
                    act.wait_ge(sem(f"down_done{l}"), 2 * p + 2)
                    for half in range(2):
                        copy(y_hi[:, half * 512:(half + 1) * 512], bank[6 + half][:, :], scale=w_slot[:, :])\
                            .then_inc(sem(f"y_act{l}"), 1)

            for n in range(FIRST_ADA):
                ada_rows(n)
            norm(0, ((0, 0, hT),))
            for c in range(12):
                if c < 8:
                    after(("qkv", 0, c))
                    if c >= 2:
                        act.wait_ge(sem("ssq"), c - 1)
                    nc.scalar.activation(sq[:, c % 2, :], bank[c % 4][:, :], ACT.Square).then_inc(sem("sq"), 1)
                ada_rows(ada_by_qkv[c][0])
                if c < 8:
                    act.wait_ge(sem("ssq"), c + 1)
                    nc.scalar.activation(srt[:, c, :], ssq[:, c, :], ACT.Sqrt, bias=eps_c, scale=1.0 / HD)\
                        .then_inc(sem("srt"), 1)
                ada_rows(ada_by_qkv[c][1])
                if 2 <= c < 10:
                    b = c - 2
                    act.wait_ge(sem("qkT_ps"), b + 1)
                    src = bank[4 + b % 2][:, :]
                    if b < 4:
                        copy(qT[:, 2 * b:2 * b + 2, :].rearrange("p k n -> p (k n)"), src, scale=qk_gain[:, 0:1])\
                            .then_inc(sem("qkT_sb"), 1)
                    else:
                        copy(kT[:, 2 * b - 8:2 * b - 6, :].rearrange("p k n -> p (k n)"), src).then_inc(sem("qkT_sb"), 1)
            attention(0)
            norm(1, ((1, 24, hT),))
            experts(0)

            act.wait_ge(sem("angles"), 1)
            for a in range(2):
                last = nc.scalar.activation(ang[:, 4 + a, :, :], ang[:, 2 + a, :, :], ACT.Sin)
            last.then_inc(sem("sines"), 1)
            norm(2, ((2, 48, hT), (4, 96, hkvT)))
            act.wait_ge(sem("lat_raw"), 1)
            for ti in range(NT):
                nc.scalar.activation(junk[:, 512 + ti * ROPE:512 + (ti + 1) * ROPE], kpe[:, ti, :], ACT.Square, accum_out=small[:, 12 + ti:13 + ti])
                link(A, nc.scalar.activation(junk[:, 0:KVR], lat_kv[:, ti, :], ACT.Square, accum_out=small[:, 8 + ti:9 + ti]))
            nc.scalar.activation(small[:, 14:16], small[:, 8:10], ACT.Sqrt, bias=eps_c, scale=1.0 / KVR)\
                .then_inc(sem("lat_rt"), 1)
            act.wait_ge(sem("lat_raw"), 2)
            for ti in range(NT):
                link(A, nc.scalar.activation(junk[:, 0:QR], lat_q[:, ti, :], ACT.Square, accum_out=small[:, 10 + ti:11 + ti]))
            nc.scalar.activation(small[:, 16:18], small[:, 10:12], ACT.Sqrt, bias=eps_c, scale=1.0 / QR)\
                .then_inc(sem("lat_rt"), 1)
            act.wait_ge(sem("latT_ps"), 1)
            for kk in range(2):
                last = copy(lat_kvT[:, kk, :], bank[0][:, kk * N:(kk + 1) * N], scale=col("kv_latent_norm", kk))
            last.then_inc(sem("latT_sb"), 1)
            act.wait_ge(sem("latT_ps"), 2)
            for kk in range(3):
                last = copy(lat_qT[:, kk, :], bank[1 + kk // 2][:, (kk % 2) * N:(kk % 2 + 1) * N],
                            scale=col("b_q_latent_norm", kk))
            last.then_inc(sem("latT_sb"), 1)
            after(("uk", 1, 0))
            for ti in range(NT):
                copy(k_sb[:, ti, 8:16, 0:HD], bank[4 + 2 * ti + 1][:, :].rearrange("p (h d) -> p h d", d=HD))\
                    .then_inc(sem("up_act"), 1)
            after(("uv", 1, 0))
            for ti in range(NT):
                copy(v_sb[:, ti, 512:1024], bank[2 * ti + 1][:, :]).then_inc(sem("up_act"), 1)
            for j, b in enumerate((4, 6, 0)):
                after(("uq", 1, j))
                copy(q_flat(1)[:, j * 512:(j + 1) * 512], bank[b + 1][:, :]).then_inc(sem("up_act"), 1)
            act.wait_ge(sem("qk_ss"), 1)
            nc.scalar.activation(hs_rs[:, 2:4, :, :], hs_rs[:, 0:2, :, :], ACT.Sqrt, bias=eps_c, scale=1.0 / QK)\
                .then_inc(sem("qk_rt"), 1)
            for g in range(8):
                act.wait_ge(sem("mT_ps"), 2 * g + 1)
                copy(qT[0:QK, 2 * g:2 * g + 2, :].rearrange("p k n -> p (k n)"), bank[g % 2][0:QK, :], scale=qk_gain[0:QK, 1:2])\
                    .then_inc(sem("mT_act"), 1)
            attention(1)
            norm(3, ((3, 72, hT),))
            experts(1)

        @block.vector
        def _(dve):
            V = ["dve", 0, dve]
            v = nc.vector

            def after(name):
                dve.wait_ge(sem("chunk_used"), number[name] + 1)

            def flat(a):
                return a.rearrange("p a b -> p (a b)")

            dve.wait_ge(sem("vcol_ps"), 1)
            link(V, v.tensor_copy(vcol[:, :], bank[7][:, 0:NROWS]))
            v.memset(bank[7][:, 0:256], 0.0).then_inc(sem("vcol"), 1)
            link(V, v.memset(qk_gain[:, 1:2], QK ** -0.5))
            link(V, v.tensor_tensor(qk_gain[:, 0:1], col("a_q_norm"), col("a_k_norm"), ALU.mult))
            link(V, v.tensor_scalar(qk_gain[:, 0:1], qk_gain[:, 0:1], HD ** -0.5, None, ALU.mult))
            link(V, v.scalar_tensor_tensor(out=qk_gain[0:HD, 1:2], in0=col("b_q_norm", rows=HD), scalar=QK ** -0.5,
                                           in1=col("kv_k_norm", rows=HD), op0=ALU.mult, op1=ALU.mult))
            dve.wait_ge(sem("small_in"), 7 * 16)
            link(V, v.tensor_copy(pos_kf[:, :], pos_k[:, :]))
            link(V, v.tensor_copy(pos_qf[:, :], pos_q[:, :]))

            def modulation(biases, amps):
                for (b0, bn, bias) in biases:
                    last = v.tensor_tensor(mod[:, b0:b0 + bn], bank[7][:, ADA_COL + b0:ADA_COL + b0 + bn], bias, ALU.add)
                link(V, last)
                for a, s0, g in amps:
                    last = v.scalar_tensor_tensor(out=amp[:, a, :], in0=mod[:, s0:s0 + 8], scalar=1.0, in1=g, op0=ALU.add,
                                                  op1=ALU.mult)
                last.then_inc(sem("amp"), 1)

            dve.wait_ge(sem("ada_ps"), 1)
            modulation(((0, 16, col("ada_b", 0, 16)),), ((0, 8, col("norm1_g", 0, 8)),))
            dve.wait_ge(sem("amp"), 1)

            def gate_diagonal(l, g):
                s0 = 48 * l + (16 if g == 0 else 40)
                if 2 * l + g:
                    dve.wait_ge(sem("gate_ps"), 2 * (2 * l + g))
                v.tensor_tensor(diag[:, :, :], const("ident").unsqueeze(1).broadcast_to([P, KT, P]),
                                mod[:, s0:s0 + 8].unsqueeze(2).broadcast_to([P, KT, P]), ALU.mult)\
                    .then_inc(sem("diag"), 1)

            def norm(n, outs):
                dve.wait_ge(sem("x_rt"), n + 1)
                link(V, v.reciprocal(small[:, 4:6], small[:, 2:4]))
                for ti in range(NT):
                    v.tensor_scalar(xn[:, ti, :], x[:, ti, :], small[:, 4 + ti:5 + ti], None, ALU.mult)\
                        .then_inc(sem("xn_ready"), 1)
                for j in (0, 2):
                    dve.wait_ge(sem("xT_ps"), 4 * n + j + 1)
                    for a, s0, dst in outs:
                        for kk in range(2):
                            k = 2 * j + kk
                            last = v.tensor_scalar(dst[:, k, :], bank[j][:, kk * N:(kk + 1) * N], amp[:, a, k:k + 1],
                                                   mod[:, s0 + k:s0 + k + 1], ALU.mult, ALU.add)
                    last.then_inc(sem("hT_dve"), 1)

            def attention(l):
                heads, pairs = H * l, H // 2 * l
                for g in range(H // 2 + 1):
                    if g < H // 2:
                        both = (2 * g, 2 * g + 1)
                        dve.wait_ge(sem("s_ps"), pairs + g + 1)
                        if g >= 2:
                            dve.wait_ge(sem("p_ready"), heads + 2 * g - 2)
                        if l == 0:
                            for h in both:
                                slope = float(np.exp2(np.float32(-8.0 * (h + 1) / H)))
                                last = v.scalar_tensor_tensor(out=s_sb[:, h % 4, :], in0=negrel[:, :], scalar=slope,
                                                              in1=bank[h % 4][:, 0:SC], op0=ALU.mult, op1=ALU.add)
                            link(V, last)
                        for h in both:
                            src, mask = (s_sb[:, h % 4, :], const("logcount")) if l == 0 else (bank[h % 4], const("causal"))
                            for ti, (c0, c1) in enumerate(((0, P), (P, SC))):
                                last = v.tensor_tensor_reduce(out=s_sb[:, h % 4, c0:c1], in0=src[:, c0:c1],
                                                              in1=mask[:, c0:c1], scale=1.0, scalar=-3e38, op0=ALU.add,
                                                              op1=ALU.max, accum_out=smax[:, h, ti:ti + 1])
                        link(V, last)
                        v.tensor_scalar(nmax[:, 2 * g:2 * g + 2, :], smax[:, 2 * g:2 * g + 2, :], -1.0, None, ALU.mult)\
                            .then_inc(sem("s_ready"), 2)
                    if g >= 1:
                        both = (2 * g - 2, 2 * g - 1)
                        dve.wait_ge(sem("p_ready"), heads + 2 * g)
                        link(V, v.reciprocal(rsum[:, 2 * g - 2:2 * g, :], lsum[:, 2 * g - 2:2 * g, :]))
                        for h in both:
                            for ti, (c0, c1) in enumerate(((0, P), (P, SC))):
                                last = v.tensor_scalar(p_sb[:, h % 4, c0:c1], p_sb[:, h % 4, c0:c1], rsum[:, h, ti:ti + 1],
                                                       None, ALU.mult)
                            last.then_inc(sem("p_norm"), 1)
                if l == 0:
                    dve.wait_ge(sem("ada_ps"), 2)
                    modulation(((16, 80, col("ada_b", 16, 80)), (96, 16, col("kv_ada_b", 0, 16))),
                               ((1, 32, col("norm2_g", 0, 8)), (2, 56, col("norm1_g", 8, 8)), (3, 80, col("norm2_g", 8, 8)),
                                (4, 104, col("kv_norm_g", 0, 8))))
                    dve.wait_ge(sem("amp"), 2)
                gate_diagonal(l, 0)
                gate_diagonal(l, 1)
                dve.wait_ge(sem("gate_sb"), 4 * l + 4)
                for c in range(4):
                    after(("wo", l, c))
                    gj = junk[:, (c % 2) * 512:(c % 2) * 512 + 512].rearrange("p (t n) -> p t n", t=NT)
                    link(V, v.tensor_tensor(gj, bank[4 + c][:, :].rearrange("p (t n) -> p t n", t=NT),
                                            gate[:, 0:1, c * N:(c + 1) * N].broadcast_to([P, NT, N]), ALU.mult))
                    xs = x[:, :, c * N:(c + 1) * N]
                    ins = v.tensor_tensor(xs, xs, gj, ALU.add)
                ins.then_inc(sem("x_new"), 1)
                dve.wait_ge(sem("x_new"), 2 * l + 1)

            def experts(l):
                big = 1e30
                dve.wait_ge(sem("score"), l + 1)
                link(V, v.tensor_tensor(choice[:, :, 0:E], score[:, :, :],
                                        bias_row[:, l:l + 1, :].broadcast_to([P, NT, E]), ALU.add))
                for ti in range(NT):
                    for g in range(G):
                        last = v.max(gsort[:, ti, g, :], choice[:, ti, 8 * g:8 * g + 8])
                link(V, last)
                link(V, v.tensor_tensor(gsc[:, :, 0:G], gsort[:, :, :, 0], gsort[:, :, :, 1], ALU.add))
                link(V, v.memset(gsc[:, :, G:G + TOPG], big))
                for ti in range(NT):
                    link(V, v.max(gtop[:, ti, :], gsc[:, ti, 0:G]))
                link(V, v.memset(gtop[:, :, TOPG:8], big))
                for ti in range(NT):
                    link(V, v.match_replace(gleft[:, ti, :], gtop[:, ti, :], gsc[:, ti, :], -3e38))
                link(V, v.tensor_tensor(gmask[:, :, :], gleft[:, :, 0:G], gsc[:, :, 0:G], ALU.not_equal))
                for ti in range(NT):
                    ch = choice[:, ti, 0:E].rearrange("p (g e) -> p g e", g=G)
                    link(V, v.tensor_tensor(ch, ch, gmask[:, ti, :].unsqueeze(2).broadcast_to([P, G, 8]), ALU.mult))
                link(V, v.tensor_scalar(gleft[:, :, 0:G], gmask[:, :, :], -1.0, big, ALU.add, ALU.mult))
                for ti in range(NT):
                    ch = choice[:, ti, 0:E].rearrange("p (g e) -> p g e", g=G)
                    link(V, v.tensor_tensor(ch, ch, gleft[:, ti, 0:G].unsqueeze(2).broadcast_to([P, G, 8]), ALU.add))
                link(V, v.memset(choice[:, :, E:E + 2], big))
                for ti in range(NT):
                    link(V, v.max(etop[:, ti, :], choice[:, ti, 0:E]))
                link(V, v.memset(etop[:, :, TOPK:8], big))
                for ti in range(NT):
                    link(V, v.match_replace(left[:, ti, :], etop[:, ti, :], choice[:, ti, :], -3e38))
                v.tensor_tensor(chosen[:, :, :], left[:, :, 0:E], choice[:, :, 0:E], ALU.not_equal).then_inc(sem("chosen"), 1)
                for j in (1, 3):
                    dve.wait_ge(sem("h_ps"), 4 * l + j + 1)
                    v.tensor_copy(h_tok[:, j // 2, 512:1024], bank[j][:, :]).then_inc(sem("h_dve"), 1)
                v.memset(y_hi[:, :].bitcast(F32), 0.0)
                v.memset(y_lo[:, :].bitcast(F32), 0.0)
                v.memset(st[:, :].bitcast(F32), 0.0)
                dve.wait_ge(sem("chosen"), l + 1)
                link(V, v.tensor_tensor(w_of[:, :, 0:E], score[:, :, :], chosen[:, :, :], ALU.mult))
                link(V, v.tensor_reduce(rden[:, :], w_of[:, :, 0:E], AX_X, ALU.add))
                link(V, v.reciprocal(rden[:, :], rden[:, :]))
                for ti in range(NT):
                    v.tensor_scalar(w_of[:, ti, 0:E], w_of[:, ti, 0:E], rden[:, ti:ti + 1], ROUTED_SCALE, ALU.mult, ALU.mult)
                v.memset(slot_of[:, :, ITEMS:ITEMS + 2], 0.0)
                v.memset(w_of[:, :, ITEMS:ITEMS + 2], 0.0)
                dve.wait_ge(sem("ranks"), l + 1)
                v.scalar_tensor_tensor(out=slot_of[:, :, 0:E], in0=bank[4][:, 0:NT * E].rearrange("p (t e) -> p t e", t=NT),
                                       scalar=1.0, in1=chosen[:, :, :], op0=ALU.add, op1=ALU.mult).then_inc(sem("slots"), 1)
                dve.wait_ge(sem("counts"), l + 1)
                link(V, v.tensor_copy(count[:, 0:1], bank[5][0:E, 0:1]))
                for c in range(3):
                    link(V, v.tensor_scalar(flag[:, c:c + 1], count[:, 0:1], float(C * (c + 1)), None, ALU.is_gt))
                v.tensor_reduce(flag[:, 3:4], flag[:, 0:3], AX_X, ALU.add).then_inc(sem("flags"), 1)

                slot1 = const("slot1").unsqueeze(1).unsqueeze(1).broadcast_to([P, NT, 2, C])

                def of_pair(table, p):
                    return table[:, :, bass.ds(2 * p, 2)].unsqueeze(3).broadcast_to([P, NT, 2, C])

                def select(p):
                    v.tensor_tensor(sel[:, :, :, :], slot1, of_pair(slot_of, p), ALU.is_equal)\
                        .then_inc(sem(f"sel_ready{l}"), 1)

                dve.wait_ge(sem("slots"), l + 1)
                select(0)
                after(("sgu", l, 1))
                dve.wait_ge(sem("sh_g"), l + 1)
                v.tensor_tensor(flat(sh_h[:, :, :]), flat(sh_g[:, :, :]), bank[7][:, :], ALU.mult).then_inc(sem("sh_h"), 1)
                dve.wait_ge(sem("places"), l + 1)
                link(V, v.tensor_copy(place[:, 0:3], bank[5][0:E, 4:7]))
                for c in range(3):
                    link(V, v.tensor_scalar(onehot[:, c, :], const("iota", E), place[:, c:c + 1], flag[:, c:c + 1],
                                            ALU.is_equal, ALU.mult))
                link(V, v.tensor_scalar(onehot[:, 3, :], onehot[:, 0, :], -float(C), None, ALU.mult))
                for c in (1, 2):
                    link(V, v.scalar_tensor_tensor(out=onehot[:, 3, :], in0=onehot[:, c, :], scalar=-float(C * (c + 1)),
                                                   in1=onehot[:, 3, :], op0=ALU.mult, op1=ALU.add))
                link(V, v.tensor_tensor(onehot[:, 4, :], onehot[:, 0, :], onehot[:, 1, :], ALU.add))
                v.tensor_tensor(onehot[:, 4, :], onehot[:, 4, :], onehot[:, 2, :], ALU.add).then_inc(sem("onehot"), 1)
                dve.wait_ge(sem("tabT_ps"), l + 1)
                v.tensor_copy(flat(rtT[:, :, :]), bank[6][0:E, :]).then_inc(sem("tabT"), 1)
                dve.wait_ge(sem("over_ps"), l + 1)
                v.tensor_copy(slot_of[:, :, E:ITEMS], bank[7][:, 0:NT * OVER].rearrange("p (t e) -> p t e", t=NT))
                v.tensor_copy(w_of[:, :, E:ITEMS], bank[7][:, 64:64 + NT * OVER].rearrange("p (t e) -> p t e", t=NT))
                v.tensor_copy(tab_i[:, 0:OVER], bank[7][0:1, 128:128 + OVER])
                v.tensor_scalar(tab_i[:, OVER:OVER + 1], bank[5][0:1, 8:9], 0.5, E / 2 + 0.25, ALU.mult, ALU.add)
                v.memset(count[:, 0:1], 0.0).then_inc(sem(f"st_ready{l}"), 1)
                v.memset(count[:, 1:2], 0.0).then_inc(sem("table"), 1)
                v.memset(count[:, 2:3], 0.0).then_inc(sem(f"y_act{l}"), 2)
                v.memset(count[:, 3:4], 0.0).then_inc(sem(f"y_dve{l}"), 1)
                dve.wait_ge(sem("table"), l + 1)

                trips = dve.value_load(tab_i[0:1, OVER:OVER + 1], min_val=E // 2, max_val=ITEMS // 2)
                with dve.Fori(0, trips) as p:
                    dve.wait_ge(sem(f"gath_done{l}"), p + 1)
                    dve.wait_ge(sem(f"sel_ready{l}"), p + 1)
                    v.tensor_tensor(selw[:, :, :, :], sel[:, :, :, :], of_pair(w_of, p), ALU.mult)\
                        .then_inc(sem(f"selw_ready{l}"), 1)
                    dve.wait_ge(sem(f"selw_ready{l}"), p + 1)
                    select(p + 1)
                    dve.wait_ge(sem(f"silu_done{l}"), p + 1)
                    v.tensor_tensor(hh[:, :], sg[:, :], bank[5][:, FE:2 * FE], ALU.mult).then_inc(sem(f"hh_ready{l}"), 1)
                    dve.wait_ge(sem(f"hhT_done{l}"), p + 1)
                    v.tensor_copy(flat(hhT[:, :, :]), bank[6][:, 0:FE]).then_inc(sem(f"hhT_sb{l}"), 1)
                    dve.wait_ge(sem(f"stT_done{l}"), p + 1)
                    v.tensor_reduce(w_slot[:, :], bank[5][:, 0:N], AX_X, ALU.add)
                    v.tensor_scalar(st[:, :], bank[5][:, 0:N], 0.0, None, ALU.is_gt).then_inc(sem(f"st_ready{l}"), 1)
                    dve.wait_ge(sem(f"st_ready{l}"), p + 2)
                    for half in range(2):
                        dve.wait_ge(sem(f"y_act{l}"), 2 * p + 3 + half)
                        c = slice(half * 512, (half + 1) * 512)
                        last = v.scalar_tensor_tensor(out=y_lo[:, c], in0=bank[6 + half][:, :], scalar=w_slot[:, :],
                                                      in1=y_hi[:, c].bitcast(F32), op0=ALU.mult, op1=ALU.subtract)
                    last.then_inc(sem(f"y_dve{l}"), 1)
                dve.wait_ge(sem("routed"), l + 1)
                for ti in range(NT):
                    for half in range(2):
                        c = slice(half * 512, (half + 1) * 512)
                        link(V, v.tensor_tensor(junk[:, c], bank[2 * ti + half][:, :], gate[:, 1, c], ALU.mult))
                        ins = v.tensor_tensor(x[:, ti, c], x[:, ti, c], junk[:, c], ALU.add)
                ins.then_inc(sem("x_new"), 1)
                dve.wait_ge(sem("x_new"), 2 * l + 2)

            norm(0, ((0, 0, hT),))
            v.tensor_scalar(negrel[:, 0:P], pos_kf[:, 0:P], pos_qf[:, 0:1], None, ALU.subtract)
            link(V, v.tensor_scalar(negrel[:, P:SC], pos_kf[:, :], pos_qf[:, 1:2], None, ALU.subtract))
            for c in range(12):
                if c < 8:
                    dve.wait_ge(sem("sq"), c + 1)
                    v.tensor_reduce(ssq[:, c, :], sq[:, c % 2, :].rearrange("p (g d) -> p g d", d=HD), AX_X, ALU.add)\
                        .then_inc(sem("ssq"), 1)
                    dve.wait_ge(sem("srt"), c + 1)
                    link(V, v.reciprocal(srs[:, c, :], srt[:, c, :]))
                    if c >= 3:
                        dve.wait_ge(sem("qkT_ps"), c - 2)
                    v.tensor_tensor(qkn[:, c % 3, :].rearrange("p (g d) -> p g d", d=HD),
                                    bank[c % 4][:, :].rearrange("p (g d) -> p g d", d=HD),
                                    srs[:, c, :].unsqueeze(2).broadcast_to([P, 8, HD]), ALU.mult).then_inc(sem("qkv_sb"), 1)
                else:
                    after(("qkv", 0, c))
                    v.tensor_copy(v_sb[:, :, (c - 8) * N:(c - 7) * N], bank[c % 4][:, :].rearrange("p (t n) -> p t n", t=NT))\
                        .then_inc(sem("qkv_sb"), 1)
            attention(0)
            norm(1, ((1, 24, hT),))
            experts(0)

            for ti in range(NT):
                link(V, v.tensor_scalar(ang[:, 0, ti, :], const("inv"), pos_qf[:, ti:ti + 1], None, ALU.mult))
            a0, a1, a2, a3 = (flat(ang[:, n, :, :]) for n in range(4))
            magic = float(3 << 22)
            link(V, v.tensor_scalar(a1, a0, float(1 / (2 * np.pi)), magic, ALU.mult, ALU.add))
            link(V, v.tensor_scalar(a1, a1, -magic, None, ALU.add))
            link(V, v.scalar_tensor_tensor(out=a2, in0=a1, scalar=-6.28125, in1=a0, op0=ALU.mult, op1=ALU.add))
            link(V, v.scalar_tensor_tensor(out=a2, in0=a1, scalar=-float(2 * np.pi - 6.28125), in1=a2, op0=ALU.mult, op1=ALU.add))
            link(V, v.tensor_scalar(a2, a2, PI, -PI, ALU.min, ALU.max))
            link(V, v.scalar_tensor_tensor(out=a3, in0=a2, scalar=-1.0, in1=a2, op0=ALU.mult, op1=ALU.max))
            v.tensor_scalar(a3, a3, -1.0, float(np.pi / 2), ALU.mult, ALU.add).then_inc(sem("angles"), 1)
            norm(2, ((2, 48, hT), (4, 96, hkvT)))
            after(("kvd", 1, 0))
            link(V, v.tensor_copy(flat(lat_kv[:, :, :]), bank[4][:, :]))
            after(("kvd", 1, 1))
            v.tensor_copy(flat(kpe[:, :, :]), bank[5][:, 0:NT * ROPE]).then_inc(sem("lat_raw"), 1)
            after(("dq", 1, 1))
            link(V, v.tensor_copy(lat_q[:, :, 0:256], bank[6][:, :].rearrange("p (t n) -> p t n", t=NT)))
            v.tensor_copy(lat_q[:, :, 256:QR], bank[7][:, 0:2 * (QR - 256)].rearrange("p (t n) -> p t n", t=NT))\
                .then_inc(sem("lat_raw"), 1)
            for n, (lat, s0) in enumerate(((lat_kv, 14), (lat_q, 16))):
                dve.wait_ge(sem("lat_rt"), n + 1)
                link(V, v.reciprocal(small[:, s0 + 4:s0 + 6], small[:, s0:s0 + 2]))
                for ti in range(NT):
                    last = v.tensor_scalar(lat[:, ti, :], lat[:, ti, :], small[:, s0 + 4 + ti:s0 + 5 + ti], None, ALU.mult)
                last.then_inc(sem("lat_n"), 1)
            dve.wait_ge(sem("sines"), 1)
            sin, cos = ang[:, 4, :, :], ang[:, 5, :, :]
            half_r = ROPE // 2

            def rotate(a, b, s, c, shape):
                r = [rt[:, n, 0:int(np.prod(shape[1:]))].rearrange("p (a b) -> p a b", b=half_r) for n in range(4)]
                for n, (m, f) in enumerate(((a, c), (b, s), (a, s), (b, c))):
                    last = v.tensor_tensor(r[n], m, f, ALU.mult)
                link(V, last)
                v.tensor_tensor(a, r[0], r[1], ALU.subtract)
                link(V, v.tensor_tensor(b, r[2], r[3], ALU.add))

            dve.wait_ge(sem("lat_rt"), 1)
            link(V, v.tensor_tensor(kpe[:, :, :], kpe[:, :, :], ropeg[:, 1:2, :].broadcast_to([P, NT, ROPE]), ALU.mult))
            rotate(kpe[:, :, 0:half_r], kpe[:, :, half_r:ROPE], sin, cos, [P, NT, half_r])
            after(("uk", 1, 0))
            for ti in range(NT):
                v.tensor_copy(k_sb[:, ti, 0:8, 0:HD], bank[4 + 2 * ti][:, :].rearrange("p (h d) -> p h d", d=HD))\
                    .then_inc(sem("up_dve"), 1)
            after(("uv", 1, 0))
            for ti in range(NT):
                v.tensor_copy(v_sb[:, ti, 0:512], bank[2 * ti][:, :]).then_inc(sem("up_dve"), 1)
            for j, b in enumerate((4, 6, 0)):
                after(("uq", 1, j))
                v.tensor_copy(q_flat(0)[:, j * 512:(j + 1) * 512], bank[b][:, :]).then_inc(sem("up_dve"), 1)
            dve.wait_ge(sem("up_act"), 7)
            dve.wait_ge(sem("up_dve"), 7)
            wide = flat(xn[:, :, :])
            for ti in range(NT):
                for row, m, n in ((0, q_sb[:, ti, :, :], QK), (1, k_sb[:, ti, :, 0:HD], HD)):
                    w3 = wide[:, 0:H * n].rearrange("p (h d) -> p h d", d=n)
                    link(V, v.tensor_tensor(w3, m, m, ALU.mult))
                    link(V, v.tensor_reduce(hs_rs[:, row, ti, :], w3, AX_X, ALU.add))
                last = v.tensor_scalar(hs_rs[:, 1, ti, :], hs_rs[:, 1, ti, :], small[:, 12 + ti:13 + ti], None, ALU.add)
            last.then_inc(sem("qk_ss"), 1)
            for ti in range(NT):
                pe_part = q_sb[:, ti, :, HD:QK]
                link(V, v.tensor_tensor(pe_part, pe_part, ropeg[:, 0:1, :].broadcast_to([P, H, ROPE]), ALU.mult))
                rotate(q_sb[:, ti, :, HD:HD + half_r], q_sb[:, ti, :, HD + half_r:QK],
                       sin[:, ti:ti + 1, :].broadcast_to([P, H, half_r]), cos[:, ti:ti + 1, :].broadcast_to([P, H, half_r]),
                       [P, H, half_r])
            dve.wait_ge(sem("qk_rt"), 1)
            link(V, v.reciprocal(hs_rs[:, 4:6, :, :].rearrange("p a b c -> p (a b c)"),
                                 hs_rs[:, 2:4, :, :].rearrange("p a b c -> p (a b c)")))
            for ti in range(NT):
                v.tensor_tensor(q_sb[:, ti, :, :], q_sb[:, ti, :, :], hs_rs[:, 4, ti, :].unsqueeze(2).broadcast_to([P, H, QK]), ALU.mult)
                kn = k_sb[:, ti, :, 0:HD]
                v.tensor_tensor(kn, kn, hs_rs[:, 5, ti, :].unsqueeze(2).broadcast_to([P, H, HD]), ALU.mult)
                last = v.tensor_tensor(k_sb[:, ti, :, HD:QK], kpe[:, ti:ti + 1, :].broadcast_to([P, H, ROPE]),
                                       hs_rs[:, 5, ti, :].unsqueeze(2).broadcast_to([P, H, ROPE]), ALU.mult)
            last.then_inc(sem("qk_norm"), 1)
            for g in range(8):
                dve.wait_ge(sem("mT_ps"), 2 * g + 2)
                v.tensor_copy(flat(kT[0:QK, 2 * g:2 * g + 2, :]), bank[2 + g % 2][0:QK, :]).then_inc(sem("mT_dve"), 1)
            attention(1)
            norm(3, ((3, 72, hT),))
            experts(1)

        @block.gpsimd
        def _(pool):
            nc.gpsimd.memset(rows_b[:, :], 0.0).then_inc(sem("rows_zero"), 1)


_INS = ["x", "c", "pos", "ada_w", "ada_b", "norm1_g", "norm2_g", "a_w_qkv", "a_q_norm", "a_k_norm", "a_w_o", "kv_ada_w",
        "kv_ada_b", "kv_norm_g", "kv_w_down", "kv_latent_norm", "kv_w_uk", "kv_w_uv", "kv_k_norm", "b_w_dq",
        "b_q_latent_norm", "b_w_uq", "b_q_norm", "b_w_o", "moe_w_router", "moe_router_bias", "moe_w_gate_up",
        "moe_w_down", "moe_shared_gate_up", "moe_shared_down"]


def kernel(**inputs):
    import concourse.bacc as _bacc
    from concourse.bass_utils import run_bass_kernel_spmd as _run

    nc = _bacc.Bacc("TRN2", target_bir_lowering=False, num_devices=1)
    arrays, tensors = {}, {}
    for name in _INS + ["consts"]:
        a = np.ascontiguousarray(constants() if name == "consts" else inputs[name])
        arrays[f"in_{name}"] = a
        tensors[name] = nc.dram_tensor(f"in_{name}", a.shape, mybir.dt.from_np(a.dtype), kind="ExternalInput").ap()
    out = nc.dram_tensor("out", (1, N, D), F32, kind="ExternalOutput").ap()
    build(nc, tensors, out)
    r = _run(nc, [arrays], core_ids=[0])
    return r.results[0]["out"]
```

```python
from contextlib import ExitStack

import numpy as np

import concourse.bass as bass
from concourse import mybir

P = 128
F32 = mybir.dt.float32
F32R = mybir.dt.float32r
I32 = mybir.dt.int32
ALU = mybir.AluOpType
ACT = mybir.ActivationFunctionType
AX_X = mybir.AxisListType.X

N = 256
NT = N // P
D = 1024
KT = D // P
H = 16
HD = 64
QR = 384
KVR = 256
ROPE = 32
QK = HD + ROPE
QW = 4 * QK
E = 64
G = 8
TOPG = 4
TOPK = 6
FE = 256
ROUTED_SCALE = 2.5
THETA = 10000.0
EPS = 1e-6
C = 64
FIRST_ADA = 8
OVER = 24
ITEMS = E + OVER
ADA_COL = 256
MASKED = -1e30
PI = float(np.float32(3.1415925))

RING = 5
CH = 2048
SC = 3 * P

CO, _at = {}, 0
for _name, _n in (("ident", P), ("tri", P), ("ones", P), ("logcount", SC), ("causal", SC), ("slot1", C),
                  ("iota", OVER), ("inv", ROPE // 2), ("halves", 2), ("row", 1), ("eps", 1), ("halfpi", 1)):
    CO[_name] = (_at, _at + _n)
    _at += _n
NCONST = _at

VR, _at = {}, 0
for _name, _n in (("ada_b", 96), ("norm1_g", 16), ("norm2_g", 16), ("kv_ada_b", 16), ("kv_norm_g", 8),
                  ("c", 8), ("b_q_latent_norm", 3), ("kv_latent_norm", 2), ("a_q_norm", 1),
                  ("a_k_norm", 1), ("b_q_norm", 1), ("kv_k_norm", 1)):
    VR[_name] = (_at, _at + _n)
    _at += _n
NROWS = _at
NROWS_B = NROWS - P


def constants():
    c = np.zeros((P, NCONST), np.float32)
    q = np.arange(P)[:, None]
    k = np.arange(P)[None, :]

    def put(name, value):
        c[:, CO[name][0]:CO[name][1]] = value

    put("ident", q == k)
    put("tri", q < k)
    put("ones", 1.0)
    dist = np.concatenate([q - k, q + P - k, q - k], axis=1)
    seen = (dist <= 128).astype(np.int64) + (dist % 4 == 0) + (dist % 16 == 0)
    put("logcount", np.where((dist >= 0) & (seen > 0), np.log(np.maximum(seen, 1)), MASKED))
    put("causal", np.where(dist >= 0, 0.0, MASKED))
    put("slot1", np.arange(1, C + 1)[None, :])
    put("iota", np.arange(OVER)[None, :])
    put("inv", np.power(np.float32(THETA), -np.arange(ROPE // 2, dtype=np.float32) / (ROPE // 2))[None, :])
    put("row", q)
    put("halves", (q // 64) == np.arange(2)[None, :])
    put("eps", EPS)
    put("halfpi", np.pi / 2)
    return c


def build(nc: bass.Bass, t: dict, out: bass.AP):
    with ExitStack() as ctx:
        sems = {}

        def sem(name):
            if name not in sems:
                sems[name] = ctx.enter_context(nc.semaphore(name))
            return sems[name]

        def sb(name, shape, dt=F32, scope=ctx):
            return scope.enter_context(nc.sbuf_tensor(name, shape, dt))

        bank = [ctx.enter_context(nc.psum_tensor(f"bank{i}", [P, 512], F32)) for i in range(8)]

        x = sb("x", [P, NT, D])
        xn = sb("xn", [P, NT, D])
        hT = sb("hT", [P, KT, N])
        gate = sb("gate", [P, 2, D])
        ring = sb("ring", [P, RING, CH])
        w_gu_0 = [sb(f"w_gu_0{u}", [P, KT, 2 * FE]) for u in range(2)]
        w_dn_0 = [sb(f"w_dn_0{u}", [P, FE // P, D]) for u in range(2)]
        w_dn_1 = [xn, hT[:, :, :].rearrange("p (f a) n -> p f (a n)", f=FE // P)]
        w_router = sb("w_router", [P, 2, KT, E])
        cst = sb("cst", [P, NCONST])
        vcol = sb("vcol", [P, NROWS])
        bias_row = sb("bias_row", [P, 2, E])
        ropeg = sb("ropeg", [P, 2, ROPE])
        pos_q = sb("pos_q", [P, NT], I32)
        pos_qf = sb("pos_qf", [P, NT])
        csilu = sb("csilu", [P, KT])
        ada_row = sb("ada_row", [P, 256])
        mod = sb("mod", [P, 2 * 48 + 16])
        amp = sb("amp", [P, 5, KT])
        qk_gain = sb("qk_gain", [P, 2])
        small = sb("small", [P, 64])
        eps_c = cst[:, CO["eps"][0]:CO["eps"][1]]

        def const(name, rows=P):
            return cst[0:rows, CO[name][0]:CO[name][1]]

        def col(name, i=0, n=1, rows=P):
            return vcol[0:rows, VR[name][0] + i:VR[name][0] + i + n]

        with ExitStack() as early:
            rows_a = sb("rows_a", [P, P], scope=early)
            rows_b = sb("rows_b", [P, P], scope=early)
            diag = sb("diag", [P, KT, P], scope=early)
            pos_k = sb("pos_k", [P, N], I32, scope=early)
            pos_kf = sb("pos_kf", [P, N], scope=early)
        with ExitStack() as att:
            qT = sb("qT", [P, H, N], scope=att)
            kT = sb("kT", [P, H, N], scope=att)
            v_sb = sb("v_sb", [P, NT, D], scope=att)
            negrel = sb("negrel", [P, SC], scope=att)
            smax = sb("smax", [P, H, NT], scope=att)
            nmax = sb("nmax", [P, H, NT], scope=att)
            lsum = sb("lsum", [P, H, NT], scope=att)
            rsum = sb("rsum", [P, H, NT], scope=att)
            with ExitStack() as first:
                qkn = sb("qkn", [P, 3, NT * N], scope=first)
                sq = sb("sq", [P, 2, NT * N], scope=first)
                ssq = sb("ssq", [P, 8, 8], scope=first)
                srt = sb("srt", [P, 8, 8], scope=first)
                srs = sb("srs", [P, 8, 8], scope=first)
            with ExitStack() as heads:
                s_sb = sb("s_sb", [P, 4, SC], scope=heads)
                p_sb = sb("p_sb", [P, 4, SC], scope=heads)
                pT_sb = sb("pT_sb", [P, 4, SC], scope=heads)
            with ExitStack() as second:
                q_sb = sb("q_sb", [P, NT, H, QK], scope=second)
                k_sb = sb("k_sb", [P, NT, H, QK], scope=second)
                kpe = sb("kpe", [P, NT, ROPE], scope=second)
                flat_kT = kT[:, :, :].rearrange("p h n -> p (h n)")
                at = [0]

                def in_kT(*shape):
                    n = int(np.prod(shape))
                    v = flat_kT[:, at[0]:at[0] + n]
                    at[0] += n
                    names = "abcd"[:len(shape)]
                    return v.rearrange(f"p ({' '.join(names)}) -> p {' '.join(names)}", **dict(zip(names, shape)))

                lat_kv = in_kT(NT, KVR)
                lat_q = in_kT(NT, QR)
                lat_kvT = in_kT(KVR // P, N)
                lat_qT = in_kT(QR // P, N)
                rt = in_kT(4, 256)
                ang = in_kT(6, NT, ROPE // 2)
                hs_rs = in_kT(6, NT, H)
            def hs_row(r):
                return hs_rs[:, r, :, :].rearrange("p t h -> p (t h)")

            hkvT = qT[:, 0:8, :]
        with ExitStack() as moe:
            h_tok = sb("h_tok", [P, NT, D], scope=moe)
            y_hi = sb("y_hi", [P, D], F32R, scope=moe)
            y_lo = sb("y_lo", [P, D], F32R, scope=moe)
            st = sb("st", [P, N], F32R, scope=moe)
            w_slot = sb("w_slot", [P, 1], scope=moe)
            sel = sb("sel", [P, NT, 2, C], scope=moe)
            selw = sb("selw", [P, NT, 2, C], scope=moe)
            xg = sb("xg", [P, KT, 2 * C], scope=moe)
            sg = sb("sg", [P, FE], scope=moe)
            hh = sb("hh", [P, FE], scope=moe)
            hhT = sb("hhT", [P, FE // P, 2 * C], scope=moe)
            sh_g = sb("sh_g", [P, FE // P, N], scope=moe)
            sh_h = sb("sh_h", [P, FE // P, N], scope=moe)
            slot_of = sb("slot_of", [P, NT, ITEMS + 2], scope=moe)
            w_of = sb("w_of", [P, NT, ITEMS + 2], scope=moe)
            score = sb("score", [P, NT, E], scope=moe)
            choice = sb("choice", [P, NT, E + 2], scope=moe)
            left = sb("left", [P, NT, E + 2], scope=moe)
            chosen = sb("chosen", [P, NT, E], scope=moe)
            gsort = sb("gsort", [P, NT, G, 8], scope=moe)
            gsc = sb("gsc", [P, NT, G + TOPG], scope=moe)
            gleft = sb("gleft", [P, NT, G + TOPG], scope=moe)
            gtop = sb("gtop", [P, NT, 8], scope=moe)
            gmask = sb("gmask", [P, NT, G], scope=moe)
            etop = sb("etop", [P, NT, 8], scope=moe)
            rden = sb("rden", [P, NT], scope=moe)
            rtT = sb("rtT", [E, 2, N], scope=moe)
            count = sb("count", [E, 4], scope=moe)
            flag = sb("flag", [E, 4], scope=moe)
            place = sb("place", [E, 4], scope=moe)
            onehot = sb("onehot", [E, 5, OVER], scope=moe)
            tab_f = sb("tab_f", [1, OVER + 1], scope=moe)
            tab_i = sb("tab_i", [1, OVER + 2], I32, scope=moe)
            w_gu_1 = [sb(f"w_gu_1{u}", [P, KT, 2 * FE], scope=moe) for u in range(2)]
        w_gu, w_dn = [w_gu_0, w_gu_1], [w_dn_0, w_dn_1]
        junk = sb("junk", [P, D])

        def rows_loads():
            loads = []
            for name in ("ada_b", "norm1_g", "norm2_g", "kv_ada_b", "kv_norm_g", "c", "b_q_latent_norm", "kv_latent_norm"):
                r0, r1 = VR[name]
                src = t[name]
                if len(src.shape) == 2:
                    src = src.rearrange("l (k p) -> (l k) p", p=P)
                else:
                    src = src.rearrange("(k p) -> k p", p=P)
                tile, off = (rows_a, 0) if r0 < P else (rows_b, P)
                loads.append((tile[r0 - off:r1 - off, :], src))
            for name, n, reps in (("a_q_norm", HD, 2), ("a_k_norm", HD, 2), ("b_q_norm", QK, 1), ("kv_k_norm", QK, 1)):
                src = t[name] if len(t[name].shape) == 2 else t[name].rearrange("(a n) -> a n", a=1)
                r = VR[name][0] - P
                for rep in range(reps):
                    loads.append((rows_b[r:r + 1, rep * n:rep * n + n], src))
            return loads

        ROWS_IN = 16 * len(rows_loads())

        chunks = []

        def chunk(name, src, k, n):
            chunks.append((name, src, k, n))

        def by_rows(w):
            return w.rearrange("(k p) n -> p k n", p=P)

        def ada_chunk(n):
            src, j = (t["ada_w"][n // 24], n % 24) if n < 48 else (t["kv_ada_w"], n - 48)
            chunk(("ada", n), by_rows(src)[:, :, j * 256:(j + 1) * 256], KT, 256)

        ada_by_qkv = [FIRST_ADA + 2 * c for c in range(12)]
        at_head = FIRST_ADA + 24
        ada_by_pair = [[at_head + 3 * g, at_head + 3 * g + 2] if g % 2 == 0 else [at_head + 3 * g + 1] for g in range(H // 2)]
        for n in range(FIRST_ADA):
            ada_chunk(n)
        for j in range(12):
            chunk(("qkv", 0, j), by_rows(t["a_w_qkv"][0])[:, :, j * 256:(j + 1) * 256], KT, 256)
            for n in (0, 1):
                ada_chunk(ada_by_qkv[j] + n)
        for g in range(H // 2):
            for n in ada_by_pair[g]:
                ada_chunk(n)
                ada_chunk(n + 1)
        for l in range(2):
            if l == 1:
                kvd = by_rows(t["kv_w_down"])
                chunk(("kvd", 1, 0), kvd[:, :, 0:KVR], KT, KVR)
                chunk(("kvd", 1, 1), kvd[:, :, KVR:KVR + ROPE], KT, ROPE)
                dq = by_rows(t["b_w_dq"][0])
                chunk(("dq", 1, 0), dq[:, :, 0:256], KT, 256)
                chunk(("dq", 1, 1), dq[:, :, 256:QR], KT, QR - 256)
                chunk(("uk", 1, 0), by_rows(t["kv_w_uk"]), 2, D)
                for j in range(4):
                    chunk(("uq", 1, j), by_rows(t["b_w_uq"][0])[:, :, j * QW:(j + 1) * QW], 3, QW)
                chunk(("uv", 1, 0), by_rows(t["kv_w_uv"]), 2, D)
            wo = by_rows(t["a_w_o"][0] if l == 0 else t["b_w_o"][0])
            for j in range(4):
                chunk(("wo", l, j), wo[:, :, j * 256:(j + 1) * 256], KT, 256)
            sgu = by_rows(t["moe_shared_gate_up"][l])
            for j in range(2):
                chunk(("sgu", l, j), sgu[:, :, j * 256:(j + 1) * 256], KT, 256)
            chunk(("sdn", l, 0), by_rows(t["moe_shared_down"][l]), 2, D)
        number = {c[0]: i for i, c in enumerate(chunks)}

        def slot(name):
            i = number[name]
            _, _, k, n = chunks[i]
            return ring[:, i % RING, 0:k * n].rearrange("p (k n) -> p k n", k=k)

        def link(eng, ins):
            s = sem("chain_" + eng[0])
            eng[1] += 1
            ins.then_inc(s, 1)
            eng[2].wait_ge(s, eng[1])

        block = ctx.enter_context(nc.Block())

        @block.sync
        def _(sp):
            def load_chunks(names):
                for name in names:
                    i = number[name]
                    _, src, k, n = chunks[i]
                    if i >= RING:
                        sp.wait_ge(sem("chunk_used"), i - RING + 1)
                    sp.dma_start(slot(name), src).then_inc(sem(f"chunk_in{i % RING}"), 16)

            def pair_loads(l, i, which, e0, e1, last_user):
                for half in range(2):
                    if last_user is not None:
                        sp.wait_ge(sem(f"gu_done{l}"), 2 * last_user + 1 + half)
                    for u, e in ((0, e0), (1, e1)):
                        ks = slice(half * KT // 2, (half + 1) * KT // 2)
                        sp.dma_start(w_gu[which][u][:, ks, :], gu_src[l](e)[:, ks, :]).then_inc(sem(f"gu_in{l}{which}{half}"), 16)
                if which == 1 and last_user is None:
                    sp.wait_ge(sem("chunk_used"), number[("sgu", l, 1)] + 1)
                for u, e in ((0, e0), (1, e1)):
                    if last_user is not None:
                        sp.wait_ge(sem(f"down_done{l}"), 2 * last_user + 1 + u)
                    sp.dma_start(w_dn[which][u][:, :, :], dn_src[l](e)).then_inc(sem(f"dn_in{l}{which}{u}"), 16)

            gu_all = t["moe_w_gate_up"].rearrange("l e (k p) n -> l p e k n", p=P)
            dn_all = t["moe_w_down"].rearrange("l e (k p) n -> l p e k n", p=P)
            gu_src = [lambda e, l=l: gu_all[l][:, bass.ds(e, 1), :, :].rearrange("p e k n -> p (e k) n") for l in range(2)]
            dn_src = [lambda e, l=l: dn_all[l][:, bass.ds(e, 1), :, :].rearrange("p e k n -> p (e k) n") for l in range(2)]

            order = [c[0] for c in chunks]
            cut = [number[("sdn", 0, 0)] + 1, len(order)]
            done = 0
            for l in range(2):
                before_wo = number[("wo", l, 0)]
                if l == 0:
                    load_chunks(order[0:before_wo])
                    done = before_wo
                else:
                    sp.wait_ge(sem("x_new"), 2)
                pair_loads(l, 0, 0, 0, 1, None)
                load_chunks(order[done:cut[l]])
                done = cut[l]
                if l == 0:
                    ahead = order[done:done + RING]
                sp.wait_ge(sem("x_new"), 2 * l + 1)
                pair_loads(l, 1, 1, 2, 3, None)
                with sp.Fori(1, E // 4) as d:
                    pair_loads(l, 2 * d, 0, 4 * d, 4 * d + 1, 2 * d - 2)
                    pair_loads(l, 2 * d + 1, 1, 4 * d + 2, 4 * d + 3, 2 * d - 1)
                sp.wait_ge(sem("table"), l + 1)
                trips = sp.value_load(tab_i[0:1, OVER:OVER + 1], min_val=E // 2, max_val=ITEMS // 2)

                def overflow(i, n, last_user):
                    e0 = sp.value_load(tab_i[0:1, bass.ds(n, 1)], min_val=0, max_val=E - 1)
                    e1 = sp.value_load(tab_i[0:1, bass.ds(n + 1, 1)], min_val=0, max_val=E - 1)
                    pair_loads(l, i, 0, e0, e1, last_user)

                with sp.If(trips > E // 2):
                    overflow(E // 2, 0, E // 2 - 2)
                with sp.If(trips > E // 2 + 1):
                    with sp.Fori(E // 2 + 1, trips) as i:
                        overflow(i, 2 * i - E, i - 1)
                if l == 0:
                    load_chunks(ahead)
                    done += RING
            sp.wait_ge(sem("x_new"), 4)
            sp.dma_start(out.rearrange("b (t p) d -> p (b t) d", p=P), x[:, :, :]).then_inc(sem("stored"), 16)
            sp.wait_ge(sem("stored"), 16)

        @block.tensor
        def _(pe):
            def use(name):
                i = number[name]
                pe.wait_ge(sem(f"chunk_in{i % RING}"), 16 * (i // RING + 1))
                return slot(name)

            def used(ins):
                ins.then_inc(sem("chunk_used"), 1)

            def mm(o, a, b, first, last):
                return nc.tensor.matmul(o, a, b, start=first, stop=last)

            def tr(o, a, rows=P):
                return nc.tensor.transpose(o, a, const("ident")[0:rows, 0:rows])

            def norm_transposes(n):
                pe.wait_ge(sem("xn_ready"), 2 * n + 2)
                for j in range(4):
                    for kk in range(2):
                        for ti in range(NT):
                            k = 2 * j + kk
                            last = tr(bank[j][:, kk * N + ti * P:kk * N + (ti + 1) * P], xn[:, ti, k * P:(k + 1) * P])
                    last.then_inc(sem("xT_ps"), 1)
                pe.wait_ge(sem("hT_dve"), 2 * (n + 1))
                pe.wait_ge(sem("hT_act"), 2 * (n + 1))

            ada_next = [0]

            def ada_columns():
                n = ada_next[0]
                pe.wait_ge(sem("row_sb"), n // 2)
                for m in range(2):
                    c = ADA_COL + 2 * (n - 2) + m
                    last = mm(bank[7][:, c:c + 3:2], ada_row[:, m * P:(m + 1) * P], const("halves"), True, True)
                return last

            def ada_step():
                if ada_next[0]:
                    ada_columns()
                n = ada_next[0]
                both = [use(("ada", n)), use(("ada", n + 1))]
                for k in range(0, KT, 2):
                    for piece in range(2):
                        for odd in range(2):
                            r = 64 * piece + 32 * odd
                            last = mm(bank[7][r:r + 1, 0:256], csilu[:, k + odd:k + odd + 1], both[piece][:, k + odd, :],
                                      k == 0, k == KT - 2)
                        if k == KT - 2:
                            used(last)
                ada_next[0] += 2

            def gates(l):
                for g in range(2):
                    pe.wait_ge(sem("diag"), 2 * l + g + 1)
                    for half in range(2):
                        b = bank[half]
                        mm(b[:, :], const("ones"), diag[:, 4 * half:4 * half + 4, :].rearrange("p k n -> p (k n)"), True, True)\
                            .then_inc(sem("gate_ps"), 1)
                    pe.wait_ge(sem("gate_sb"), 2 * (2 * l + g) + 2)

            def attention(l, q_of, k_of):
                heads, pairs = H * l, H // 2 * l

                def scores(g):
                    if g >= 2:
                        pe.wait_ge(sem("s_ready"), heads + 2 * g - 2)
                    for c0, c1, kn in ((0, P, P), (P, SC, N)):
                        for h in (2 * g, 2 * g + 1):
                            last = mm(bank[h % 4][:, c0:c1], q_of(h)[:, c0:c0 + P], k_of(h)[:, 0:kn], True, True)
                    last.then_inc(sem("s_ps"), 1)

                def p_transposes(h):
                    pe.wait_ge(sem("p_norm"), heads + h + 1)
                    if h >= 2:
                        pe.wait_ge(sem("pT_sb"), heads + h - 1)
                    for c in range(3):
                        last = tr(bank[4 + h % 2][:, c * P:(c + 1) * P], p_sb[:, h % 4, c * P:(c + 1) * P])
                    last.then_inc(sem("pT_ps"), 1)

                def values(g):
                    pe.wait_ge(sem("pT_sb"), heads + 2 * g + 2)
                    if g >= 1:
                        pe.wait_ge(sem("o_sb"), pairs + g)
                    for q, c, ti in ((0, 0, 0), (1, 1, 0), (1, 2, 1)):
                        for u, h in enumerate((2 * g, 2 * g + 1)):
                            last = mm(bank[6][u * HD:(u + 1) * HD, q * P:(q + 1) * P], v_sb[:, ti, h * HD:(h + 1) * HD],
                                      pT_sb[:, h % 4, c * P:(c + 1) * P], c < 2, c != 1)
                    last.then_inc(sem("o_ps"), 1)

                for g in range(H // 2 + 3):
                    if g < H // 2:
                        scores(g)
                        if l == 0:
                            for _ in ada_by_pair[g]:
                                ada_step()
                            if g == H // 2 - 1:
                                ada_columns().then_inc(sem("ada_ps"), 1)
                    if 2 <= g < H // 2 + 2:
                        p_transposes(2 * g - 4)
                        p_transposes(2 * g - 3)
                    if g >= 3:
                        values(g - 3)
                gates(l)
                pe.wait_ge(sem("o_sb"), pairs + H // 2)
                for c in range(4):
                    w = use(("wo", l, c))
                    for ti in range(NT):
                        for k in range(KT):
                            last = mm(bank[4 + c][:, ti * N:(ti + 1) * N], hT[:, k, ti * P:(ti + 1) * P], w[:, k, :],
                                      k == 0, k == KT - 1)
                    used(last)

            def experts(l):
                for ti in range(NT):
                    for k in range(KT):
                        last = mm(bank[4][:, ti * E:(ti + 1) * E], hT[:, k, ti * P:(ti + 1) * P], w_router[:, l, k, :],
                                  k == 0, k == KT - 1)
                last.then_inc(sem("logits"), 1)
                for j in range(4):
                    ti, half = j // 2, j % 2
                    for k in range(4):
                        last = tr(bank[j][:, k * P:(k + 1) * P], hT[:, 4 * half + k, ti * P:(ti + 1) * P])
                    last.then_inc(sem("h_ps"), 1)

                def shared_gate_up(j):
                    w = use(("sgu", l, j))
                    for f in range(2):
                        for k in range(KT):
                            last = mm(bank[6 + j][:, f * N:(f + 1) * N], w[:, k, f * P:(f + 1) * P], hT[:, k, :],
                                      k == 0, k == KT - 1)
                    used(last)

                shared_gate_up(0)
                pe.wait_ge(sem("chosen"), l + 1)
                pe.wait_ge(sem("score"), l + 1)
                mm(bank[4][:, 0:E], const("tri"), chosen[:, 0, :], True, True)
                mm(bank[4][:, E:2 * E], const("ones"), chosen[:, 0, :], True, False)
                mm(bank[4][:, E:2 * E], const("tri"), chosen[:, 1, :], False, True).then_inc(sem("ranks"), 1)
                for ti in range(NT):
                    last = mm(bank[5][0:E, 0:1], chosen[:, ti, :], const("ones")[:, 0:1], ti == 0, ti == NT - 1)
                last.then_inc(sem("counts"), 1)
                shared_gate_up(1)
                pe.wait_ge(sem("flags"), l + 1)
                mm(bank[5][0:E, 4:7], const("tri")[0:E, 0:E], flag[:, 0:3], True, False)
                mm(bank[5][0:E, 5:7], const("ones")[0:E, 0:E], flag[:, 0:2], False, False)
                mm(bank[5][0:E, 6:7], const("ones")[0:E, 0:E], flag[:, 0:1], False, True)
                mm(bank[5][0:1, 8:9], flag[:, 3:4], const("ones")[0:E, 0:1], True, True).then_inc(sem("places"), 1)
                pe.wait_ge(sem("slots"), l + 1)
                pe.wait_ge(sem("sh_g"), l + 1)
                for ti in range(NT):
                    tr(bank[6][0:E, ti * P:(ti + 1) * P], slot_of[:, ti, 0:E])
                for ti in range(NT):
                    last = tr(bank[6][0:E, N + ti * P:N + (ti + 1) * P], w_of[:, ti, 0:E])
                last.then_inc(sem("tabT_ps"), 1)
                pe.wait_ge(sem("sh_h"), l + 1)
                pe.wait_ge(sem("tabT"), l + 1)
                pe.wait_ge(sem("onehot"), l + 1)
                for ti in range(NT):
                    o = bank[7][:, ti * OVER:(ti + 1) * OVER]
                    for c in range(3):
                        mm(o, rtT[:, 0, ti * P:(ti + 1) * P], onehot[:, c, :], c == 0, False)
                    mm(o, const("ones")[0:E, :], onehot[:, 3, :], False, True)
                for ti in range(NT):
                    mm(bank[7][:, 64 + ti * OVER:64 + (ti + 1) * OVER], rtT[:, 1, ti * P:(ti + 1) * P], onehot[:, 4, :],
                       True, True)
                mm(bank[7][0:1, 128:128 + OVER], const("row")[0:E, :], onehot[:, 4, :], True, True)\
                    .then_inc(sem("over_ps"), 1)
                w = use(("sdn", l, 0))
                pe.wait_ge(sem("h_act"), 2 * l + 2)
                pe.wait_ge(sem("h_dve"), 2 * l + 2)
                for ti in range(NT):
                    for half in range(2):
                        for f in range(2):
                            last = nc.tensor.matmul(bank[2 * ti + half][:, :], sh_h[:, f, ti * P:(ti + 1) * P],
                                                    w[:, f, half * 512:(half + 1) * 512], start=f == 0, stop=False,
                                                    skip_group_check=True)
                used(last)
                pe.wait_ge(sem("table"), l + 1)

                def gate_up(p, which, turn):
                    pe.wait_ge(sem(f"xg_ready{l}"), p + 1)
                    pe.wait_ge(sem(f"st_ready{l}"), p + 1)
                    for half in range(2):
                        pe.wait_ge(sem(f"gu_in{l}{which}{half}"), 32 * turn)
                        for k in range(half * KT // 2, (half + 1) * KT // 2):
                            for u in range(2):
                                last = mm(bank[5][u * C:(u + 1) * C, :], xg[:, k, u * C:(u + 1) * C], w_gu[which][u][:, k, :],
                                          k == 0, k == KT - 1)
                        last.then_inc(sem(f"gu_done{l}"), 1)

                def scatter(count, stop):
                    pe.wait_ge(sem(f"y_act{l}"), 2 * count)
                    pe.wait_ge(sem(f"y_dve{l}"), count)
                    for ti in range(NT):
                        for half in range(2):
                            for y in (y_hi, y_lo):
                                last = nc.tensor.matmul(bank[2 * ti + half][:, :], st[:, ti * P:(ti + 1) * P],
                                                        y[:, half * 512:(half + 1) * 512], start=False,
                                                        stop=stop and y is y_lo, skip_group_check=True)
                    return last

                def gather(count):
                    pe.wait_ge(sem(f"sel_ready{l}"), count)
                    for k in range(KT):
                        b = bank[4 if k < 4 else 7]
                        for ti in range(NT):
                            last = mm(b[:, (k % 4) * P:(k % 4 + 1) * P], h_tok[:, ti, k * P:(k + 1) * P],
                                      sel[:, ti, :, :].rearrange("p u c -> p (u c)"), ti == 0, ti == NT - 1)
                    last.then_inc(sem(f"gath_done{l}"), 1)

                def middle(p):
                    pe.wait_ge(sem(f"hh_ready{l}"), p + 1)
                    for f in range(2):
                        last = tr(bank[6][:, f * P:(f + 1) * P], hh[:, f * P:(f + 1) * P])
                    last.then_inc(sem(f"hhT_done{l}"), 1)

                def weights_transposed(p):
                    pe.wait_ge(sem(f"selw_ready{l}"), p + 1)
                    for ti in range(NT):
                        last = tr(bank[5][:, ti * P:(ti + 1) * P], selw[:, ti, :, :].rearrange("p u c -> p (u c)"))
                    last.then_inc(sem(f"stT_done{l}"), 1)

                def down(p, which, turn):
                    pe.wait_ge(sem(f"hhT_sb{l}"), p + 1)
                    for u in range(2):
                        pe.wait_ge(sem(f"dn_in{l}{which}{u}"), 16 * turn)
                    for half in range(2):
                        if half == 1:
                            pe.wait_ge(sem(f"xg_ready{l}"), p + 2)
                        for f in range(2):
                            for u in range(2):
                                ins = mm(bank[6 + half][u * C:(u + 1) * C, :], hhT[:, f, u * C:(u + 1) * C],
                                         w_dn[which][u][:, f, half * 512:(half + 1) * 512], f == 0, f == 1)
                                if half == 1 and f == 1:
                                    ins.then_inc(sem(f"down_done{l}"), 1)

                gather(1)
                trips = pe.value_load(tab_i[0:1, OVER:OVER + 1], min_val=E // 2, max_val=ITEMS // 2)

                def pair(p, which, turn):
                    gate_up(p, which, turn)
                    scatter(p + 1, False)
                    middle(p)
                    gather(p + 2)
                    weights_transposed(p)
                    down(p, which, turn)

                with pe.Fori(0, E // 4) as d:
                    pair(2 * d, 0, d + 1)
                    pair(2 * d + 1, 1, d + 1)
                with pe.If(trips > E // 2):
                    with pe.Fori(E // 2, trips) as p:
                        pair(p, 0, p - E // 2 + E // 4 + 1)
                scatter(trips + 1, True).then_inc(sem("routed"), 1)

            pe.wait_ge(sem("rows_in"), ROWS_IN)
            pe.wait_ge(sem("const_in"), 16)
            tr(bank[7][:, 0:P], rows_a[:, :])
            nc.tensor.transpose(bank[7][:, P:NROWS], rows_b[0:NROWS_B, :], const("ident")[0:NROWS_B, 0:NROWS_B])\
                .then_inc(sem("vcol_ps"), 1)
            pe.wait_ge(sem("csilu"), 1)
            for n in range(FIRST_ADA // 2):
                ada_step()
            ada_columns().then_inc(sem("ada_ps"), 1)
            norm_transposes(0)

            def qk_transposes(c):
                pe.wait_ge(sem("qkv_sb"), c + 1)
                if c >= 2:
                    pe.wait_ge(sem("qkT_sb"), c - 1)
                for b2 in range(2):
                    for ti in range(NT):
                        last = tr(bank[4 + c % 2][:, b2 * N + ti * P:b2 * N + (ti + 1) * P],
                                  qkn[:, c % 3, ti * N + b2 * P:ti * N + (b2 + 1) * P])
                last.then_inc(sem("qkT_ps"), 1)

            for c in range(12):
                w = use(("qkv", 0, c))
                if c >= 4:
                    pe.wait_ge(sem("qkv_sb"), c - 3)
                for ti in range(NT):
                    for k in range(KT):
                        last = mm(bank[c % 4][:, ti * N:(ti + 1) * N], hT[:, k, ti * P:(ti + 1) * P], w[:, k, :],
                                  k == 0, k == KT - 1)
                used(last)
                ada_step()
                if 2 <= c < 10:
                    qk_transposes(c - 2)
            pe.wait_ge(sem("qkv_sb"), 12)
            pe.wait_ge(sem("qkT_sb"), 8)
            pair = lambda tt: (lambda h: tt[HD * (h % 2):HD * (h % 2) + HD, h // 2, :])
            attention(0, pair(qT), pair(kT))
            norm_transposes(1)
            experts(0)
            norm_transposes(2)
            for i, (name, b, n) in enumerate(((("kvd", 1, 0), 4, KVR), (("kvd", 1, 1), 5, ROPE), (("dq", 1, 0), 6, 256),
                                              (("dq", 1, 1), 7, QR - 256))):
                w = use(name)
                src = hkvT if name[0] == "kvd" else hT
                for ti in range(NT):
                    for k in range(KT):
                        last = mm(bank[b][:, ti * n:(ti + 1) * n], src[:, k, ti * P:(ti + 1) * P], w[:, k, :],
                                  k == 0, k == KT - 1)
                used(last)
            pe.wait_ge(sem("lat_n"), 1)
            for kk in range(2):
                for ti in range(NT):
                    last = tr(bank[0][:, kk * N + ti * P:kk * N + (ti + 1) * P], lat_kv[:, ti, kk * P:(kk + 1) * P])
            last.then_inc(sem("latT_ps"), 1)

            def up(name, src, kn, n, banks):
                w = use(name)
                for ti in range(NT):
                    for half, b in enumerate(banks[ti]):
                        for k in range(kn):
                            last = mm(bank[b][:, 0:n], src[:, k, ti * P:(ti + 1) * P], w[:, k, half * n:(half + 1) * n],
                                      k == 0, k == kn - 1)
                used(last)

            pe.wait_ge(sem("latT_sb"), 1)
            pe.wait_ge(sem("lat_raw"), 2)
            up(("uk", 1, 0), lat_kvT, 2, 512, ((4, 5), (6, 7)))
            pe.wait_ge(sem("lat_n"), 2)
            for kk in range(3):
                for ti in range(NT):
                    last = tr(bank[1 + kk // 2][:, (kk % 2) * N + ti * P:(kk % 2) * N + (ti + 1) * P],
                              lat_q[:, ti, kk * P:(kk + 1) * P])
            last.then_inc(sem("latT_ps"), 1)
            pe.wait_ge(sem("latT_sb"), 2)
            for j in range(4):
                if j >= 2:
                    pe.wait_ge(sem("up_dve"), j + 1)
                    pe.wait_ge(sem("up_act"), j + 1)
                b = 2 * (j % 2)
                up(("uq", 1, j), lat_qT, 3, QW, ((b,), (b + 1,)))
            pe.wait_ge(sem("up_dve"), 2)
            pe.wait_ge(sem("up_act"), 2)
            up(("uv", 1, 0), lat_kvT, 2, 512, ((4, 5), (6, 7)))
            pe.wait_ge(sem("up_dve"), 6)
            pe.wait_ge(sem("up_act"), 6)
            for g in range(8):
                pe.wait_ge(sem("qk_norm"), g // 2 + 2)
                for side, (src, b) in enumerate(((q_sb, 0), (k_sb, 2))):
                    if g >= 2:
                        pe.wait_ge(sem("mT_act" if side == 0 else "mT_dve"), g - 1)
                    for hh_ in range(2):
                        for ti in range(NT):
                            last = tr(bank[b + g % 2][0:QK, hh_ * N + ti * P:hh_ * N + (ti + 1) * P],
                                      src[:, ti, 2 * g + hh_, :])
                    last.then_inc(sem("mT_ps"), 1)
            pe.wait_ge(sem("mT_act"), 8)
            pe.wait_ge(sem("mT_dve"), 8)
            pe.wait_ge(sem("up_dve"), 8)
            pe.wait_ge(sem("up_act"), 8)
            attention(1, lambda h: qT[0:QK, h, :], lambda h: kT[0:QK, h, :])
            norm_transposes(3)
            experts(1)

        @block.scalar
        def _(act):
            A = ["act", 0, act]

            def after(name):
                act.wait_ge(sem("chunk_used"), number[name] + 1)

            def copy(o, i, **kw):
                return nc.scalar.activation(o, i, ACT.Copy, **kw)

            act.dma_start(cst[:, :], t["consts"]).then_inc(sem("const_in"), 16)
            act.wait_ge(sem("rows_zero"), 1)
            for dst, src in rows_loads():
                act.dma_start(dst, src).then_inc(sem("rows_in"), 16)
            act.dma_start(x[:, :, :], t["x"].rearrange("b (t p) d -> p (b t) d", p=P)).then_inc(sem("x_in"), 16)
            act.dma_start(w_router[:, :, :, :].rearrange("p l k e -> p (l k) e"),
                          t["moe_w_router"].rearrange("l (k p) e -> p (l k) e", p=P)).then_inc(sem("small_in"), 16)
            for l in range(2):
                act.dma_start(bias_row[:, l, :], t["moe_router_bias"][l:l + 1, :].broadcast_to([P, E])).then_inc(sem("small_in"), 16)
            act.dma_start(ropeg[:, 0, :], t["b_q_norm"][0:1, HD:QK].broadcast_to([P, ROPE])).then_inc(sem("small_in"), 16)
            act.dma_start(ropeg[:, 1, :], t["kv_k_norm"].rearrange("(a n) -> a n", a=1)[:, HD:QK].broadcast_to([P, ROPE]))\
               .then_inc(sem("small_in"), 16)
            act.dma_start(pos_k[:, :], t["pos"].broadcast_to([P, N])).then_inc(sem("small_in"), 16)
            act.dma_start(pos_q[:, :], t["pos"].rearrange("b (t p) -> p (b t)", p=P), allow_slow_non_contiguous=True).then_inc(sem("small_in"), 16)

            act.wait_ge(sem("vcol"), 1)
            nc.scalar.activation(csilu[:, :], col("c", 0, 8), ACT.Silu).then_inc(sem("csilu"), 1)

            def ada_rows(n):
                after(("ada", n + 1))
                copy(ada_row[:, :], bank[7][:, 0:256]).then_inc(sem("row_sb"), 1)

            def gates(l):
                for g in range(2):
                    if l == 1 and g == 0:
                        act.wait_ge(sem("x_new"), 2)
                    for half in range(2):
                        act.wait_ge(sem("gate_ps"), 2 * (2 * l + g) + half + 1)
                        copy(gate[:, g, half * 512:(half + 1) * 512], bank[half][:, :]).then_inc(sem("gate_sb"), 1)

            def norm_root(n):
                if n == 0:
                    act.wait_ge(sem("x_in"), 16)
                else:
                    act.wait_ge(sem("x_new"), n)
                for ti in range(NT):
                    link(A, nc.scalar.activation(junk[:, :], x[:, ti, :], ACT.Square, accum_out=small[:, ti:ti + 1]))
                nc.scalar.activation(small[:, 2:4], small[:, 0:2], ACT.Sqrt, bias=eps_c, scale=1.0 / D)\
                    .then_inc(sem("x_rt"), 1)

            def norm(n, outs):
                if n:
                    norm_root(n)
                act.wait_ge(sem("amp"), 1 if n == 0 else 2)
                for j in (1, 3):
                    act.wait_ge(sem("xT_ps"), 4 * n + j + 1)
                    for a, s0, dst in outs:
                        for kk in range(2):
                            k = 2 * j + kk
                            last = nc.scalar.activation(dst[:, k, :], bank[j][:, kk * N:(kk + 1) * N], ACT.Identity,
                                                        bias=mod[:, s0 + k:s0 + k + 1], scale=amp[:, a, k:k + 1])
                    last.then_inc(sem("hT_act"), 1)

            def attention(l):
                heads, pairs = H * l, H // 2 * l
                for g in range(H // 2 + 3):
                    if g < H // 2:
                        if l == 0:
                            for n in ada_by_pair[g]:
                                ada_rows(n)
                        for h in (2 * g, 2 * g + 1):
                            act.wait_ge(sem("s_ready"), heads + h + 1)
                            if h >= 4:
                                act.wait_ge(sem("pT_ps"), heads + h - 3)
                            for ti, (c0, c1) in enumerate(((0, P), (P, SC))):
                                last = nc.scalar.activation(p_sb[:, h % 4, c0:c1], s_sb[:, h % 4, c0:c1], ACT.Exp,
                                                            bias=nmax[:, h, ti:ti + 1], accum_out=lsum[:, h, ti:ti + 1])
                            last.then_inc(sem("p_ready"), 1)
                    if 2 <= g < H // 2 + 2:
                        if g >= 4:
                            act.wait_ge(sem("o_ps"), pairs + g - 3)
                        for h in (2 * g - 4, 2 * g - 3):
                            act.wait_ge(sem("pT_ps"), heads + h + 1)
                            copy(pT_sb[:, h % 4, :], bank[4 + h % 2][:, 0:SC]).then_inc(sem("pT_sb"), 1)
                    if g >= 3:
                        act.wait_ge(sem("o_ps"), pairs + g - 2)
                        copy(hT[:, g - 3, :], bank[6][:, 0:N]).then_inc(sem("o_sb"), 1)
                gates(l)

            def experts(l):
                act.wait_ge(sem("logits"), l + 1)
                nc.scalar.activation(score[:, :, :].rearrange("p t e -> p (t e)"), bank[4][:, 0:NT * E], ACT.Sigmoid)\
                    .then_inc(sem("score"), 1)
                for j in (0, 2):
                    act.wait_ge(sem("h_ps"), 4 * l + j + 1)
                    copy(h_tok[:, j // 2, 0:512], bank[j][:, :]).then_inc(sem("h_act"), 1)
                after(("sgu", l, 0))
                nc.scalar.activation(sh_g[:, :, :].rearrange("p f n -> p (f n)"), bank[6][:, :], ACT.Silu)\
                    .then_inc(sem("sh_g"), 1)

                def gathered(count):
                    act.wait_ge(sem(f"gath_done{l}"), count)
                    for b, k in ((7, 4), (4, 0)):
                        last = copy(xg[:, k:k + 4, :].rearrange("p k c -> p (k c)"), bank[b][:, :])
                    last.then_inc(sem(f"xg_ready{l}"), 1)

                act.wait_ge(sem("table"), l + 1)
                gathered(1)
                trips = act.value_load(tab_i[0:1, OVER:OVER + 1], min_val=E // 2, max_val=ITEMS // 2)
                with act.Fori(0, trips) as p:
                    act.wait_ge(sem(f"gu_done{l}"), 2 * p + 2)
                    nc.scalar.activation(sg[:, :], bank[5][:, 0:FE], ACT.Silu).then_inc(sem(f"silu_done{l}"), 1)
                    gathered(p + 2)
                    act.wait_ge(sem(f"st_ready{l}"), p + 2)
                    act.wait_ge(sem(f"down_done{l}"), 2 * p + 2)
                    for half in range(2):
                        copy(y_hi[:, half * 512:(half + 1) * 512], bank[6 + half][:, :], scale=w_slot[:, :])\
                            .then_inc(sem(f"y_act{l}"), 1)

            for n in range(0, FIRST_ADA, 2):
                ada_rows(n)
                if n == 2:
                    norm_root(0)
            norm(0, ((0, 0, hT),))
            for c in range(12):
                if c < 8:
                    after(("qkv", 0, c))
                    if c >= 2:
                        act.wait_ge(sem("ssq"), c - 1)
                    nc.scalar.activation(sq[:, c % 2, :], bank[c % 4][:, :], ACT.Square).then_inc(sem("sq"), 1)
                ada_rows(ada_by_qkv[c])
                if c < 8:
                    act.wait_ge(sem("ssq"), c + 1)
                    nc.scalar.activation(srt[:, c, :], ssq[:, c, :], ACT.Sqrt, bias=eps_c, scale=1.0 / HD)\
                        .then_inc(sem("srt"), 1)
                if 2 <= c < 10:
                    b = c - 2
                    act.wait_ge(sem("qkT_ps"), b + 1)
                    src = bank[4 + b % 2][:, :]
                    if b < 4:
                        copy(qT[:, 2 * b:2 * b + 2, :].rearrange("p k n -> p (k n)"), src, scale=qk_gain[:, 0:1])\
                            .then_inc(sem("qkT_sb"), 1)
                    else:
                        copy(kT[:, 2 * b - 8:2 * b - 6, :].rearrange("p k n -> p (k n)"), src).then_inc(sem("qkT_sb"), 1)
            attention(0)
            norm(1, ((1, 24, hT),))
            experts(0)

            act.wait_ge(sem("angles"), 1)
            for a in range(2):
                last = nc.scalar.activation(ang[:, 4 + a, :, :], ang[:, 2 + a, :, :], ACT.Sin)
            last.then_inc(sem("sines"), 1)
            norm(2, ((2, 48, hT), (4, 96, hkvT)))
            act.wait_ge(sem("lat_raw"), 1)
            for ti in range(NT):
                nc.scalar.activation(junk[:, 512 + ti * ROPE:512 + (ti + 1) * ROPE], kpe[:, ti, :], ACT.Square, accum_out=small[:, 12 + ti:13 + ti])
                link(A, nc.scalar.activation(junk[:, 0:KVR], lat_kv[:, ti, :], ACT.Square, accum_out=small[:, 8 + ti:9 + ti]))
            nc.scalar.activation(small[:, 14:16], small[:, 8:10], ACT.Sqrt, bias=eps_c, scale=1.0 / KVR)\
                .then_inc(sem("lat_rt"), 1)
            act.wait_ge(sem("lat_raw"), 2)
            for ti in range(NT):
                link(A, nc.scalar.activation(junk[:, 0:QR], lat_q[:, ti, :], ACT.Square, accum_out=small[:, 10 + ti:11 + ti]))
            nc.scalar.activation(small[:, 16:18], small[:, 10:12], ACT.Sqrt, bias=eps_c, scale=1.0 / QR)\
                .then_inc(sem("lat_rt"), 1)
            act.wait_ge(sem("latT_ps"), 1)
            for kk in range(2):
                last = copy(lat_kvT[:, kk, :], bank[0][:, kk * N:(kk + 1) * N], scale=col("kv_latent_norm", kk))
            last.then_inc(sem("latT_sb"), 1)
            act.wait_ge(sem("latT_ps"), 2)
            for kk in range(3):
                last = copy(lat_qT[:, kk, :], bank[1 + kk // 2][:, (kk % 2) * N:(kk % 2 + 1) * N],
                            scale=col("b_q_latent_norm", kk))
            last.then_inc(sem("latT_sb"), 1)
            after(("uk", 1, 0))
            for ti in range(NT):
                copy(k_sb[:, ti, 8:16, 0:HD], bank[4 + 2 * ti + 1][:, :].rearrange("p (h d) -> p h d", d=HD))\
                    .then_inc(sem("up_act"), 1)
            act.wait_ge(sem("up_act"), 2)
            act.wait_ge(sem("up_dve"), 2)
            for ti in range(NT):
                last = nc.scalar.activation(xn[:, ti, :].rearrange("p (h d) -> p h d", d=HD), k_sb[:, ti, :, 0:HD], ACT.Square)
            last.then_inc(sem("qk_sq"), 1)

            def qk_root(n):
                act.wait_ge(sem("qk_ss"), n + 1)
                r = slice(0, 32) if n == 0 else slice(8 * n - 8, 8 * n)
                nc.scalar.activation(hs_row(3 if n == 0 else 2)[:, r], hs_row(1 if n == 0 else 0)[:, r], ACT.Sqrt, bias=eps_c,
                                     scale=1.0 / QK).then_inc(sem("qk_rt"), 1)

            for j in range(4):
                after(("uq", 1, j))
                heads = slice(4 * j, 4 * j + 4)
                copy(q_sb[:, 1, heads, :], bank[2 * (j % 2) + 1][:, 0:QW].rearrange("p (h d) -> p h d", d=QK))\
                    .then_inc(sem("up_act"), 1)
                qk_root(j)
                act.wait_ge(sem("up_act"), 3 + j)
                act.wait_ge(sem("up_dve"), 3 + j)
                nc.scalar.activation(junk[:, 0:2 * QW].rearrange("p (t h d) -> p t h d", t=NT, d=QK), q_sb[:, :, heads, :],
                                     ACT.Square).then_inc(sem("qk_sq"), 1)
            qk_root(4)
            after(("uv", 1, 0))
            for ti in range(NT):
                copy(v_sb[:, ti, 512:1024], bank[4 + 2 * ti + 1][:, :]).then_inc(sem("up_act"), 1)
            for g in range(8):
                act.wait_ge(sem("mT_ps"), 2 * g + 1)
                copy(qT[0:QK, 2 * g:2 * g + 2, :].rearrange("p k n -> p (k n)"), bank[g % 2][0:QK, :], scale=qk_gain[0:QK, 1:2])\
                    .then_inc(sem("mT_act"), 1)
            attention(1)
            norm(3, ((3, 72, hT),))
            experts(1)

        @block.vector
        def _(dve):
            V = ["dve", 0, dve]
            v = nc.vector

            def after(name):
                dve.wait_ge(sem("chunk_used"), number[name] + 1)

            def flat(a):
                return a.rearrange("p a b -> p (a b)")

            dve.wait_ge(sem("vcol_ps"), 1)
            link(V, v.tensor_copy(vcol[:, :], bank[7][:, 0:NROWS]))
            v.memset(bank[7][:, 0:256], 0.0).then_inc(sem("vcol"), 1)
            link(V, v.memset(qk_gain[:, 1:2], QK ** -0.5))
            link(V, v.tensor_tensor(qk_gain[:, 0:1], col("a_q_norm"), col("a_k_norm"), ALU.mult))
            link(V, v.tensor_scalar(qk_gain[:, 0:1], qk_gain[:, 0:1], HD ** -0.5, None, ALU.mult))
            link(V, v.scalar_tensor_tensor(out=qk_gain[0:HD, 1:2], in0=col("b_q_norm", rows=HD), scalar=QK ** -0.5,
                                           in1=col("kv_k_norm", rows=HD), op0=ALU.mult, op1=ALU.mult))
            dve.wait_ge(sem("small_in"), 7 * 16)
            link(V, v.tensor_copy(pos_kf[:, :], pos_k[:, :]))
            link(V, v.tensor_copy(pos_qf[:, :], pos_q[:, :]))

            def modulation(biases, amps):
                for (b0, bn, bias) in biases:
                    last = v.tensor_tensor(mod[:, b0:b0 + bn], bank[7][:, ADA_COL + b0:ADA_COL + b0 + bn], bias, ALU.add)
                link(V, last)
                for a, s0, g in amps:
                    last = v.scalar_tensor_tensor(out=amp[:, a, :], in0=mod[:, s0:s0 + 8], scalar=1.0, in1=g, op0=ALU.add,
                                                  op1=ALU.mult)
                last.then_inc(sem("amp"), 1)

            def gate_diagonal(l, g):
                s0 = 48 * l + (16 if g == 0 else 40)
                if 2 * l + g:
                    dve.wait_ge(sem("gate_ps"), 2 * (2 * l + g))
                v.tensor_tensor(diag[:, :, :], const("ident").unsqueeze(1).broadcast_to([P, KT, P]),
                                mod[:, s0:s0 + 8].unsqueeze(2).broadcast_to([P, KT, P]), ALU.mult)\
                    .then_inc(sem("diag"), 1)

            def norm_scale(n):
                dve.wait_ge(sem("x_rt"), n + 1)
                link(V, v.reciprocal(small[:, 4:6], small[:, 2:4]))
                for ti in range(NT):
                    v.tensor_scalar(xn[:, ti, :], x[:, ti, :], small[:, 4 + ti:5 + ti], None, ALU.mult)\
                        .then_inc(sem("xn_ready"), 1)

            def norm(n, outs):
                if n:
                    norm_scale(n)
                for j in (0, 2):
                    dve.wait_ge(sem("xT_ps"), 4 * n + j + 1)
                    for a, s0, dst in outs:
                        for kk in range(2):
                            k = 2 * j + kk
                            last = v.tensor_scalar(dst[:, k, :], bank[j][:, kk * N:(kk + 1) * N], amp[:, a, k:k + 1],
                                                   mod[:, s0 + k:s0 + k + 1], ALU.mult, ALU.add)
                    last.then_inc(sem("hT_dve"), 1)

            def attention(l):
                heads, pairs = H * l, H // 2 * l
                for g in range(H // 2 + 1):
                    if g < H // 2:
                        both = (2 * g, 2 * g + 1)
                        dve.wait_ge(sem("s_ps"), pairs + g + 1)
                        if g >= 2:
                            dve.wait_ge(sem("p_ready"), heads + 2 * g - 2)
                        if l == 0:
                            for h in both:
                                slope = float(np.exp2(np.float32(-8.0 * (h + 1) / H)))
                                last = v.scalar_tensor_tensor(out=s_sb[:, h % 4, :], in0=negrel[:, :], scalar=slope,
                                                              in1=bank[h % 4][:, 0:SC], op0=ALU.mult, op1=ALU.add)
                            link(V, last)
                        for h in both:
                            src, mask = (s_sb[:, h % 4, :], const("logcount")) if l == 0 else (bank[h % 4], const("causal"))
                            for ti, (c0, c1) in enumerate(((0, P), (P, SC))):
                                last = v.tensor_tensor_reduce(out=s_sb[:, h % 4, c0:c1], in0=src[:, c0:c1],
                                                              in1=mask[:, c0:c1], scale=1.0, scalar=-3e38, op0=ALU.add,
                                                              op1=ALU.max, accum_out=smax[:, h, ti:ti + 1])
                        link(V, last)
                        v.tensor_scalar(nmax[:, 2 * g:2 * g + 2, :], smax[:, 2 * g:2 * g + 2, :], -1.0, None, ALU.mult)\
                            .then_inc(sem("s_ready"), 2)
                    if g >= 1:
                        both = (2 * g - 2, 2 * g - 1)
                        dve.wait_ge(sem("p_ready"), heads + 2 * g)
                        link(V, v.reciprocal(rsum[:, 2 * g - 2:2 * g, :], lsum[:, 2 * g - 2:2 * g, :]))
                        for h in both:
                            for ti, (c0, c1) in enumerate(((0, P), (P, SC))):
                                last = v.tensor_scalar(p_sb[:, h % 4, c0:c1], p_sb[:, h % 4, c0:c1], rsum[:, h, ti:ti + 1],
                                                       None, ALU.mult)
                            last.then_inc(sem("p_norm"), 1)
                if l == 0:
                    dve.wait_ge(sem("ada_ps"), 2)
                    modulation(((16, 80, col("ada_b", 16, 80)), (96, 16, col("kv_ada_b", 0, 16))),
                               ((1, 32, col("norm2_g", 0, 8)), (2, 56, col("norm1_g", 8, 8)), (3, 80, col("norm2_g", 8, 8)),
                                (4, 104, col("kv_norm_g", 0, 8))))
                    dve.wait_ge(sem("amp"), 2)
                gate_diagonal(l, 0)
                gate_diagonal(l, 1)
                dve.wait_ge(sem("gate_sb"), 4 * l + 4)
                for c in range(4):
                    after(("wo", l, c))
                    gj = junk[:, (c % 2) * 512:(c % 2) * 512 + 512].rearrange("p (t n) -> p t n", t=NT)
                    link(V, v.tensor_tensor(gj, bank[4 + c][:, :].rearrange("p (t n) -> p t n", t=NT),
                                            gate[:, 0:1, c * N:(c + 1) * N].broadcast_to([P, NT, N]), ALU.mult))
                    xs = x[:, :, c * N:(c + 1) * N]
                    ins = v.tensor_tensor(xs, xs, gj, ALU.add)
                ins.then_inc(sem("x_new"), 1)
                dve.wait_ge(sem("x_new"), 2 * l + 1)

            def experts(l):
                big = 1e30
                dve.wait_ge(sem("score"), l + 1)
                link(V, v.tensor_tensor(choice[:, :, 0:E], score[:, :, :],
                                        bias_row[:, l:l + 1, :].broadcast_to([P, NT, E]), ALU.add))
                for ti in range(NT):
                    for g in range(G):
                        last = v.max(gsort[:, ti, g, :], choice[:, ti, 8 * g:8 * g + 8])
                link(V, last)
                link(V, v.tensor_tensor(gsc[:, :, 0:G], gsort[:, :, :, 0], gsort[:, :, :, 1], ALU.add))
                link(V, v.memset(gsc[:, :, G:G + TOPG], big))
                for ti in range(NT):
                    link(V, v.max(gtop[:, ti, :], gsc[:, ti, 0:G]))
                link(V, v.memset(gtop[:, :, TOPG:8], big))
                for ti in range(NT):
                    link(V, v.match_replace(gleft[:, ti, :], gtop[:, ti, :], gsc[:, ti, :], -3e38))
                link(V, v.tensor_tensor(gmask[:, :, :], gleft[:, :, 0:G], gsc[:, :, 0:G], ALU.not_equal))
                for ti in range(NT):
                    ch = choice[:, ti, 0:E].rearrange("p (g e) -> p g e", g=G)
                    link(V, v.tensor_tensor(ch, ch, gmask[:, ti, :].unsqueeze(2).broadcast_to([P, G, 8]), ALU.mult))
                link(V, v.tensor_scalar(gleft[:, :, 0:G], gmask[:, :, :], -1.0, big, ALU.add, ALU.mult))
                for ti in range(NT):
                    ch = choice[:, ti, 0:E].rearrange("p (g e) -> p g e", g=G)
                    link(V, v.tensor_tensor(ch, ch, gleft[:, ti, 0:G].unsqueeze(2).broadcast_to([P, G, 8]), ALU.add))
                link(V, v.memset(choice[:, :, E:E + 2], big))
                for ti in range(NT):
                    link(V, v.max(etop[:, ti, :], choice[:, ti, 0:E]))
                link(V, v.memset(etop[:, :, TOPK:8], big))
                for ti in range(NT):
                    link(V, v.match_replace(left[:, ti, :], etop[:, ti, :], choice[:, ti, :], -3e38))
                v.tensor_tensor(chosen[:, :, :], left[:, :, 0:E], choice[:, :, 0:E], ALU.not_equal).then_inc(sem("chosen"), 1)
                for j in (1, 3):
                    dve.wait_ge(sem("h_ps"), 4 * l + j + 1)
                    v.tensor_copy(h_tok[:, j // 2, 512:1024], bank[j][:, :]).then_inc(sem("h_dve"), 1)
                v.memset(y_hi[:, :].bitcast(F32), 0.0)
                v.memset(y_lo[:, :].bitcast(F32), 0.0)
                v.memset(st[:, :].bitcast(F32), 0.0)
                dve.wait_ge(sem("chosen"), l + 1)
                link(V, v.tensor_tensor(w_of[:, :, 0:E], score[:, :, :], chosen[:, :, :], ALU.mult))
                link(V, v.tensor_reduce(rden[:, :], w_of[:, :, 0:E], AX_X, ALU.add))
                link(V, v.reciprocal(rden[:, :], rden[:, :]))
                for ti in range(NT):
                    v.tensor_scalar(w_of[:, ti, 0:E], w_of[:, ti, 0:E], rden[:, ti:ti + 1], ROUTED_SCALE, ALU.mult, ALU.mult)
                v.memset(slot_of[:, :, ITEMS:ITEMS + 2], 0.0)
                v.memset(w_of[:, :, ITEMS:ITEMS + 2], 0.0)
                dve.wait_ge(sem("ranks"), l + 1)
                v.scalar_tensor_tensor(out=slot_of[:, :, 0:E], in0=bank[4][:, 0:NT * E].rearrange("p (t e) -> p t e", t=NT),
                                       scalar=1.0, in1=chosen[:, :, :], op0=ALU.add, op1=ALU.mult).then_inc(sem("slots"), 1)
                dve.wait_ge(sem("counts"), l + 1)
                link(V, v.tensor_copy(count[:, 0:1], bank[5][0:E, 0:1]))
                for c in range(3):
                    link(V, v.tensor_scalar(flag[:, c:c + 1], count[:, 0:1], float(C * (c + 1)), None, ALU.is_gt))
                v.tensor_reduce(flag[:, 3:4], flag[:, 0:3], AX_X, ALU.add).then_inc(sem("flags"), 1)

                slot1 = const("slot1").unsqueeze(1).unsqueeze(1).broadcast_to([P, NT, 2, C])

                def of_pair(table, p):
                    return table[:, :, bass.ds(2 * p, 2)].unsqueeze(3).broadcast_to([P, NT, 2, C])

                def select(p):
                    v.tensor_tensor(sel[:, :, :, :], slot1, of_pair(slot_of, p), ALU.is_equal)\
                        .then_inc(sem(f"sel_ready{l}"), 1)

                dve.wait_ge(sem("slots"), l + 1)
                select(0)
                after(("sgu", l, 1))
                dve.wait_ge(sem("sh_g"), l + 1)
                v.tensor_tensor(flat(sh_h[:, :, :]), flat(sh_g[:, :, :]), bank[7][:, :], ALU.mult).then_inc(sem("sh_h"), 1)
                dve.wait_ge(sem("places"), l + 1)
                link(V, v.tensor_copy(place[:, 0:3], bank[5][0:E, 4:7]))
                for c in range(3):
                    link(V, v.tensor_scalar(onehot[:, c, :], const("iota", E), place[:, c:c + 1], flag[:, c:c + 1],
                                            ALU.is_equal, ALU.mult))
                link(V, v.tensor_scalar(onehot[:, 3, :], onehot[:, 0, :], -float(C), None, ALU.mult))
                for c in (1, 2):
                    link(V, v.scalar_tensor_tensor(out=onehot[:, 3, :], in0=onehot[:, c, :], scalar=-float(C * (c + 1)),
                                                   in1=onehot[:, 3, :], op0=ALU.mult, op1=ALU.add))
                link(V, v.tensor_tensor(onehot[:, 4, :], onehot[:, 0, :], onehot[:, 1, :], ALU.add))
                v.tensor_tensor(onehot[:, 4, :], onehot[:, 4, :], onehot[:, 2, :], ALU.add).then_inc(sem("onehot"), 1)
                dve.wait_ge(sem("tabT_ps"), l + 1)
                v.tensor_copy(flat(rtT[:, :, :]), bank[6][0:E, :]).then_inc(sem("tabT"), 1)
                dve.wait_ge(sem("over_ps"), l + 1)
                v.tensor_copy(slot_of[:, :, E:ITEMS], bank[7][:, 0:NT * OVER].rearrange("p (t e) -> p t e", t=NT))
                v.tensor_copy(w_of[:, :, E:ITEMS], bank[7][:, 64:64 + NT * OVER].rearrange("p (t e) -> p t e", t=NT))
                v.tensor_copy(tab_i[:, 0:OVER], bank[7][0:1, 128:128 + OVER])
                v.tensor_scalar(tab_i[:, OVER:OVER + 1], bank[5][0:1, 8:9], 0.5, E / 2 + 0.25, ALU.mult, ALU.add)
                v.memset(count[:, 0:1], 0.0).then_inc(sem(f"st_ready{l}"), 1)
                v.memset(count[:, 1:2], 0.0).then_inc(sem("table"), 1)
                v.memset(count[:, 2:3], 0.0).then_inc(sem(f"y_act{l}"), 2)
                v.memset(count[:, 3:4], 0.0).then_inc(sem(f"y_dve{l}"), 1)
                dve.wait_ge(sem("table"), l + 1)

                trips = dve.value_load(tab_i[0:1, OVER:OVER + 1], min_val=E // 2, max_val=ITEMS // 2)
                with dve.Fori(0, trips) as p:
                    dve.wait_ge(sem(f"gath_done{l}"), p + 1)
                    dve.wait_ge(sem(f"sel_ready{l}"), p + 1)
                    v.tensor_tensor(selw[:, :, :, :], sel[:, :, :, :], of_pair(w_of, p), ALU.mult)\
                        .then_inc(sem(f"selw_ready{l}"), 1)
                    dve.wait_ge(sem(f"selw_ready{l}"), p + 1)
                    select(p + 1)
                    dve.wait_ge(sem(f"silu_done{l}"), p + 1)
                    v.tensor_tensor(hh[:, :], sg[:, :], bank[5][:, FE:2 * FE], ALU.mult).then_inc(sem(f"hh_ready{l}"), 1)
                    dve.wait_ge(sem(f"hhT_done{l}"), p + 1)
                    v.tensor_copy(flat(hhT[:, :, :]), bank[6][:, 0:FE]).then_inc(sem(f"hhT_sb{l}"), 1)
                    dve.wait_ge(sem(f"stT_done{l}"), p + 1)
                    v.tensor_reduce(w_slot[:, :], bank[5][:, 0:N], AX_X, ALU.add)
                    v.tensor_scalar(st[:, :], bank[5][:, 0:N], 0.0, None, ALU.is_gt).then_inc(sem(f"st_ready{l}"), 1)
                    dve.wait_ge(sem(f"st_ready{l}"), p + 2)
                    for half in range(2):
                        dve.wait_ge(sem(f"y_act{l}"), 2 * p + 3 + half)
                        c = slice(half * 512, (half + 1) * 512)
                        last = v.scalar_tensor_tensor(out=y_lo[:, c], in0=bank[6 + half][:, :], scalar=w_slot[:, :],
                                                      in1=y_hi[:, c].bitcast(F32), op0=ALU.mult, op1=ALU.subtract)
                    last.then_inc(sem(f"y_dve{l}"), 1)
                dve.wait_ge(sem("routed"), l + 1)
                for ti in range(NT):
                    for half in range(2):
                        c = slice(half * 512, (half + 1) * 512)
                        link(V, v.tensor_tensor(junk[:, c], bank[2 * ti + half][:, :], gate[:, 1, c], ALU.mult))
                        ins = v.tensor_tensor(x[:, ti, c], x[:, ti, c], junk[:, c], ALU.add)
                ins.then_inc(sem("x_new"), 1)
                dve.wait_ge(sem("x_new"), 2 * l + 2)

            norm_scale(0)
            dve.wait_ge(sem("ada_ps"), 1)
            modulation(((0, 16, col("ada_b", 0, 16)),), ((0, 8, col("norm1_g", 0, 8)),))
            dve.wait_ge(sem("amp"), 1)
            norm(0, ((0, 0, hT),))
            v.tensor_scalar(negrel[:, 0:P], pos_kf[:, 0:P], pos_qf[:, 0:1], None, ALU.subtract)
            link(V, v.tensor_scalar(negrel[:, P:SC], pos_kf[:, :], pos_qf[:, 1:2], None, ALU.subtract))
            for c in range(12):
                if c < 8:
                    dve.wait_ge(sem("sq"), c + 1)
                    v.tensor_reduce(ssq[:, c, :], sq[:, c % 2, :].rearrange("p (g d) -> p g d", d=HD), AX_X, ALU.add)\
                        .then_inc(sem("ssq"), 1)
                    dve.wait_ge(sem("srt"), c + 1)
                    link(V, v.reciprocal(srs[:, c, :], srt[:, c, :]))
                    if c >= 3:
                        dve.wait_ge(sem("qkT_ps"), c - 2)
                    v.tensor_tensor(qkn[:, c % 3, :].rearrange("p (g d) -> p g d", d=HD),
                                    bank[c % 4][:, :].rearrange("p (g d) -> p g d", d=HD),
                                    srs[:, c, :].unsqueeze(2).broadcast_to([P, 8, HD]), ALU.mult).then_inc(sem("qkv_sb"), 1)
                else:
                    after(("qkv", 0, c))
                    v.tensor_copy(v_sb[:, :, (c - 8) * N:(c - 7) * N], bank[c % 4][:, :].rearrange("p (t n) -> p t n", t=NT))\
                        .then_inc(sem("qkv_sb"), 1)
            attention(0)
            norm(1, ((1, 24, hT),))
            experts(0)

            for ti in range(NT):
                link(V, v.tensor_scalar(ang[:, 0, ti, :], const("inv"), pos_qf[:, ti:ti + 1], None, ALU.mult))
            a0, a1, a2, a3 = (flat(ang[:, n, :, :]) for n in range(4))
            magic = float(3 << 22)
            link(V, v.tensor_scalar(a1, a0, float(1 / (2 * np.pi)), magic, ALU.mult, ALU.add))
            link(V, v.tensor_scalar(a1, a1, -magic, None, ALU.add))
            link(V, v.scalar_tensor_tensor(out=a2, in0=a1, scalar=-6.28125, in1=a0, op0=ALU.mult, op1=ALU.add))
            link(V, v.scalar_tensor_tensor(out=a2, in0=a1, scalar=-float(2 * np.pi - 6.28125), in1=a2, op0=ALU.mult, op1=ALU.add))
            link(V, v.tensor_scalar(a2, a2, PI, -PI, ALU.min, ALU.max))
            link(V, v.scalar_tensor_tensor(out=a3, in0=a2, scalar=-1.0, in1=a2, op0=ALU.mult, op1=ALU.max))
            v.tensor_scalar(a3, a3, -1.0, float(np.pi / 2), ALU.mult, ALU.add).then_inc(sem("angles"), 1)
            norm(2, ((2, 48, hT), (4, 96, hkvT)))
            after(("kvd", 1, 0))
            link(V, v.tensor_copy(flat(lat_kv[:, :, :]), bank[4][:, :]))
            after(("kvd", 1, 1))
            v.tensor_copy(flat(kpe[:, :, :]), bank[5][:, 0:NT * ROPE]).then_inc(sem("lat_raw"), 1)
            after(("dq", 1, 1))
            link(V, v.tensor_copy(lat_q[:, :, 0:256], bank[6][:, :].rearrange("p (t n) -> p t n", t=NT)))
            v.tensor_copy(lat_q[:, :, 256:QR], bank[7][:, 0:2 * (QR - 256)].rearrange("p (t n) -> p t n", t=NT))\
                .then_inc(sem("lat_raw"), 1)
            for n, (lat, s0) in enumerate(((lat_kv, 14), (lat_q, 16))):
                dve.wait_ge(sem("lat_rt"), n + 1)
                link(V, v.reciprocal(small[:, s0 + 4:s0 + 6], small[:, s0:s0 + 2]))
                for ti in range(NT):
                    last = v.tensor_scalar(lat[:, ti, :], lat[:, ti, :], small[:, s0 + 4 + ti:s0 + 5 + ti], None, ALU.mult)
                last.then_inc(sem("lat_n"), 1)
            dve.wait_ge(sem("sines"), 1)
            sin, cos = ang[:, 4, :, :], ang[:, 5, :, :]
            half_r = ROPE // 2

            def rotate(a, b, s, c, shape):
                names = "abc"[:len(shape) - 1]
                sizes = dict(zip(names, shape[1:]))
                r = [rt[:, n, 0:int(np.prod(shape[1:]))].rearrange(f"p ({' '.join(names)}) -> p {' '.join(names)}", **sizes)
                     for n in range(4)]
                for n, (m, f) in enumerate(((a, c), (b, s), (a, s), (b, c))):
                    last = v.tensor_tensor(r[n], m, f, ALU.mult)
                link(V, last)
                v.tensor_tensor(a, r[0], r[1], ALU.subtract)
                link(V, v.tensor_tensor(b, r[2], r[3], ALU.add))

            dve.wait_ge(sem("lat_rt"), 1)
            link(V, v.tensor_tensor(kpe[:, :, :], kpe[:, :, :], ropeg[:, 1:2, :].broadcast_to([P, NT, ROPE]), ALU.mult))
            rotate(kpe[:, :, 0:half_r], kpe[:, :, half_r:ROPE], sin, cos, [P, NT, half_r])
            after(("uk", 1, 0))
            for ti in range(NT):
                v.tensor_copy(k_sb[:, ti, 0:8, 0:HD], bank[4 + 2 * ti][:, :].rearrange("p (h d) -> p h d", d=HD))\
                    .then_inc(sem("up_dve"), 1)
            dve.wait_ge(sem("qk_sq"), 1)
            link(V, v.tensor_reduce(hs_row(1), xn[:, :, :].rearrange("p t (h d) -> p (t h) d", d=HD), AX_X, ALU.add))
            v.tensor_tensor(hs_rs[:, 1, :, :], hs_rs[:, 1, :, :], small[:, 12:14].unsqueeze(2).broadcast_to([P, NT, H]), ALU.add)\
                .then_inc(sem("qk_ss"), 1)

            def q_norm(j):
                dve.wait_ge(sem("qk_rt"), j + 2)
                r = slice(8 * j, 8 * j + 8)
                link(V, v.reciprocal(hs_row(4)[:, r], hs_row(2)[:, r]))
                qj = q_sb[:, :, 4 * j:4 * j + 4, :]
                v.tensor_tensor(qj, qj, hs_row(4)[:, r].rearrange("p (t h) -> p t h", t=NT).unsqueeze(3)
                                .broadcast_to([P, NT, 4, QK]), ALU.mult).then_inc(sem("qk_norm"), 1)

            def k_norm():
                dve.wait_ge(sem("qk_rt"), 1)
                link(V, v.reciprocal(hs_row(5), hs_row(3)))
                for ti in range(NT):
                    kn = k_sb[:, ti, :, 0:HD]
                    v.tensor_tensor(kn, kn, hs_rs[:, 5, ti, :].unsqueeze(2).broadcast_to([P, H, HD]), ALU.mult)
                    last = v.tensor_tensor(k_sb[:, ti, :, HD:QK], kpe[:, ti:ti + 1, :].broadcast_to([P, H, ROPE]),
                                           hs_rs[:, 5, ti, :].unsqueeze(2).broadcast_to([P, H, ROPE]), ALU.mult)
                last.then_inc(sem("qk_norm"), 1)

            for j in range(4):
                after(("uq", 1, j))
                v.tensor_copy(q_sb[:, 0, 4 * j:4 * j + 4, :], bank[2 * (j % 2)][:, 0:QW].rearrange("p (h d) -> p h d", d=QK))\
                    .then_inc(sem("up_dve"), 1)
                if j == 0:
                    k_norm()
                else:
                    q_norm(j - 1)
                dve.wait_ge(sem("qk_sq"), j + 2)
                v.tensor_reduce(hs_row(0)[:, 8 * j:8 * j + 8], junk[:, 0:2 * QW].rearrange("p (g d) -> p g d", d=QK), AX_X,
                                ALU.add).then_inc(sem("qk_ss"), 1)
                pe_part = q_sb[:, :, 4 * j:4 * j + 4, HD:QK]
                link(V, v.tensor_tensor(pe_part, pe_part, ropeg[:, 0:1, :].unsqueeze(2).broadcast_to([P, NT, 4, ROPE]), ALU.mult))
                rotate(q_sb[:, :, 4 * j:4 * j + 4, HD:HD + half_r], q_sb[:, :, 4 * j:4 * j + 4, HD + half_r:QK],
                       sin.unsqueeze(2).broadcast_to([P, NT, 4, half_r]), cos.unsqueeze(2).broadcast_to([P, NT, 4, half_r]),
                       [P, NT, 4, half_r])
            q_norm(3)
            after(("uv", 1, 0))
            for ti in range(NT):
                v.tensor_copy(v_sb[:, ti, 0:512], bank[4 + 2 * ti][:, :]).then_inc(sem("up_dve"), 1)
            for g in range(8):
                dve.wait_ge(sem("mT_ps"), 2 * g + 2)
                v.tensor_copy(flat(kT[0:QK, 2 * g:2 * g + 2, :]), bank[2 + g % 2][0:QK, :]).then_inc(sem("mT_dve"), 1)
            attention(1)
            norm(3, ((3, 72, hT),))
            experts(1)

        @block.gpsimd
        def _(pool):
            nc.gpsimd.memset(rows_b[:, :], 0.0).then_inc(sem("rows_zero"), 1)


_INS = ["x", "c", "pos", "ada_w", "ada_b", "norm1_g", "norm2_g", "a_w_qkv", "a_q_norm", "a_k_norm", "a_w_o", "kv_ada_w",
        "kv_ada_b", "kv_norm_g", "kv_w_down", "kv_latent_norm", "kv_w_uk", "kv_w_uv", "kv_k_norm", "b_w_dq",
        "b_q_latent_norm", "b_w_uq", "b_q_norm", "b_w_o", "moe_w_router", "moe_router_bias", "moe_w_gate_up",
        "moe_w_down", "moe_shared_gate_up", "moe_shared_down"]


def kernel(**inputs):
    import concourse.bacc as _bacc
    from concourse.bass_utils import run_bass_kernel_spmd as _run

    nc = _bacc.Bacc("TRN2", target_bir_lowering=False, num_devices=1)
    arrays, tensors = {}, {}
    for name in _INS + ["consts"]:
        a = np.ascontiguousarray(constants() if name == "consts" else inputs[name])
        arrays[f"in_{name}"] = a
        tensors[name] = nc.dram_tensor(f"in_{name}", a.shape, mybir.dt.from_np(a.dtype), kind="ExternalInput").ap()
    out = nc.dram_tensor("out", (1, N, D), F32, kind="ExternalOutput").ap()
    build(nc, tensors, out)
    r = _run(nc, [arrays], core_ids=[0])
    return r.results[0]["out"]
```
